# Optimizing a Trainium2 kernel written in Bass

```python
import jax, jax.numpy as jnp
from jax import lax
import numpy as np

D_MODEL = 1024
BATCH = 1
SEQ = 2048
DEPTH = 1

CHUNK = 64
MIX_WIDTH = D_MODEL
HEAD_DIM = 64
SB_WIDTH = MIX_WIDTH // 2
SB_HEADS = SB_WIDTH // HEAD_DIM
RW_WIDTH = MIX_WIDTH - SB_WIDTH
RW_HEADS = RW_WIDTH // HEAD_DIM
DECAY_LORA = 32
AAA_LORA = 32
GATE_LORA = 96
Q_BLOCK = 128
SB_COLS = 3 * SB_WIDTH
RW_COLS = 3 * RW_WIDTH + DECAY_LORA + AAA_LORA + GATE_LORA
IN_COLS = SB_COLS + RW_COLS
N_GROUPS = 4
EXPERTS_PER_GROUP = 8
N_EXPERTS = N_GROUPS * EXPERTS_PER_GROUP
TOP_K = 2
D_EXPERT = 512
EXPERT_BLOCK = 128
NORM_EPS = 1e-6
LN_X_EPS = 64e-5

kernel_name = 'hybrid_stickbreak_rwkv7_hmoe_block'

def rms_norm(x, gain):
    xf = x.astype(jnp.float32)
    y = xf * lax.rsqrt(jnp.mean(xf * xf, axis=-1, keepdims=True) + NORM_EPS)
    return (y * gain.astype(jnp.float32)).astype(x.dtype)

def stick_breaking_attention(q, k, v):
    S, d = q.shape[2], q.shape[3]
    scale = d ** -0.5
    outs = []
    for blk in range(S // Q_BLOCK):
        t0 = blk * Q_BLOCK
        end = t0 + Q_BLOCK
        z = jnp.einsum('bhtd,bhsd->bhts', q[:, :, t0:end], k[:, :, :end]).astype(jnp.float32) * scale
        t_idx = t0 + jnp.arange(Q_BLOCK)[:, None]
        s_idx = jnp.arange(end)[None, :]
        causal = s_idx < t_idx
        log_keep = jnp.where(causal, jax.nn.log_sigmoid(-z), 0.0)
        suffix = lax.cumsum(log_keep, axis=3, reverse=True)
        after = jnp.concatenate([suffix[..., 1:], jnp.zeros_like(suffix[..., :1])], axis=-1)
        weights = jnp.where(causal, jnp.exp(jax.nn.log_sigmoid(z) + after), 0.0)
        outs.append(jnp.einsum('bhts,bhsd->bhtd', weights.astype(v.dtype), v[:, :, :end]))
    return jnp.concatenate(outs, axis=2)

def token_shift(p, mu):
    prev = jnp.pad(p, ((0, 0), (1, 0), (0, 0)))[:, :-1]
    return p + (prev - p) * mu

def rwkv7_time_mix(p, mu, w0, w_up, a0, a_up, g_up, k_k, k_a, r_k, ln_w, ln_b):
    B, S, _ = p.shape
    f32 = jnp.float32
    pf = token_shift(p.astype(f32), mu.astype(f32))
    c = RW_WIDTH
    r = pf[..., :c]
    k = pf[..., c:2 * c]
    v = pf[..., 2 * c:3 * c]
    wd = pf[..., 3 * c:3 * c + DECAY_LORA]
    ad = pf[..., 3 * c + DECAY_LORA:3 * c + DECAY_LORA + AAA_LORA]
    gd = pf[..., 3 * c + DECAY_LORA + AAA_LORA:]
    w = -jax.nn.softplus(-(w0.astype(f32) + jnp.tanh(wd) @ w_up.astype(f32))) - 0.5
    decay = jnp.exp(-jnp.exp(w))
    a = jax.nn.sigmoid(a0.astype(f32) + ad @ a_up.astype(f32))
    g = jax.nn.sigmoid(gd) @ g_up.astype(f32)
    heads = lambda t: t.reshape(B, S, RW_HEADS, HEAD_DIM)
    r, k, v, decay, a = heads(r), heads(k), heads(v), heads(decay), heads(a)
    kk = k * k_k.astype(f32).reshape(RW_HEADS, HEAD_DIM)
    kk = kk / jnp.maximum(jnp.sqrt(jnp.sum(kk * kk, axis=-1, keepdims=True)), 1e-12)
    k = k * (1.0 + (a - 1.0) * k_a.astype(f32).reshape(RW_HEADS, HEAD_DIM))
    xs = tuple(jnp.moveaxis(t, 1, 0) for t in (r, decay, k, v, -kk, kk * a))

    def step(state, inp):
        r_t, w_t, k_t, v_t, a_t, b_t = inp
        sa = jnp.einsum('bhvk,bhk->bhv', state, a_t)
        state = (state * w_t[:, :, None, :] + sa[..., None] * b_t[:, :, None, :]
                 + v_t[..., None] * k_t[:, :, None, :])
        return state, jnp.einsum('bhvk,bhk->bhv', state, r_t)

    state0 = jnp.zeros((B, RW_HEADS, HEAD_DIM, HEAD_DIM), f32)
    _, y = lax.scan(step, state0, xs)
    y = jnp.moveaxis(y, 0, 1)
    mean = jnp.mean(y, axis=-1, keepdims=True)
    var = jnp.mean(jnp.square(y - mean), axis=-1, keepdims=True)
    yn = ((y - mean) * lax.rsqrt(var + LN_X_EPS) * ln_w.astype(f32).reshape(RW_HEADS, HEAD_DIM)
          + ln_b.astype(f32).reshape(RW_HEADS, HEAD_DIM))
    bonus = jnp.sum(r * k * r_k.astype(f32), axis=-1, keepdims=True) * v
    out = (yn + bonus).reshape(B, S, c) * g
    return out.astype(p.dtype)

def hierarchical_moe(h, w_rg, w_re, w_g, w_u, w_d):
    B, S, D = h.shape
    hf = h.reshape(-1, D)
    n_tok = B * S
    group_logits = (hf @ w_rg).astype(jnp.float32)
    group_prob = jax.nn.softmax(group_logits, axis=-1)
    group_idx = jnp.argmax(group_logits, axis=-1).astype(jnp.int32)
    group_gate = jnp.take_along_axis(group_prob, group_idx[:, None], axis=-1)
    exp_logits = (hf @ w_re).astype(jnp.float32).reshape(n_tok, N_GROUPS, EXPERTS_PER_GROUP)
    in_group = jnp.take_along_axis(exp_logits, group_idx[:, None, None], axis=1)[:, 0]
    top_p, top_i = lax.top_k(jax.nn.softmax(in_group, axis=-1), TOP_K)
    gates = group_gate * top_p / jnp.sum(top_p, axis=-1, keepdims=True)
    eid = (group_idx[:, None] * EXPERTS_PER_GROUP + top_i.astype(jnp.int32)).reshape(-1)
    n_slot = n_tok * TOP_K
    order = jnp.argsort(eid).astype(jnp.int32)
    sorted_eid = eid[order]
    counts = jnp.zeros((N_EXPERTS,), jnp.int32).at[eid].add(1)
    padded = (counts + EXPERT_BLOCK - 1) // EXPERT_BLOCK * EXPERT_BLOCK
    pad_end = jnp.cumsum(padded).astype(jnp.int32)
    pad_start = pad_end - padded
    start = jnp.cumsum(counts).astype(jnp.int32) - counts
    dest_sorted = pad_start[sorted_eid] + jnp.arange(n_slot, dtype=jnp.int32) - start[sorted_eid]
    slot_dest = jnp.zeros((n_slot,), jnp.int32).at[order].set(dest_sorted)
    n_rows = (n_slot + EXPERT_BLOCK - 1) // EXPERT_BLOCK * EXPERT_BLOCK + N_EXPERTS * EXPERT_BLOCK
    n_blocks = n_rows // EXPERT_BLOCK
    token_of_slot = jnp.arange(n_slot, dtype=jnp.int32) // TOP_K
    buf = jnp.zeros((n_rows, D), h.dtype).at[slot_dest].set(hf[token_of_slot])
    block_start = jnp.arange(n_blocks, dtype=jnp.int32) * EXPERT_BLOCK
    block_eid = jnp.minimum(jnp.sum((pad_end[None, :] <= block_start[:, None]).astype(jnp.int32), axis=1),
                            N_EXPERTS - 1)

    def expert_block(args):
        xb, e = args
        return (jax.nn.silu(xb @ w_g[e]) * (xb @ w_u[e])) @ w_d[e]

    out = lax.map(expert_block, (buf.reshape(n_blocks, EXPERT_BLOCK, D), block_eid)).reshape(n_rows, D)
    y = jnp.sum(out[slot_dest].reshape(n_tok, TOP_K, D) * gates[..., None].astype(h.dtype), axis=1)
    return y.reshape(B, S, D)

def setup_inputs(seed: int = 0) -> dict:
    key = jax.random.key(seed)
    ks = jax.random.split(key, 24)
    L = DEPTH
    f32 = jnp.float32
    nrm = lambda k, shape: jax.random.normal(k, shape, f32)
    lin = lambda k, shape, fan_in: nrm(k, shape) * fan_in ** -0.5
    return {
        'x': nrm(ks[0], (BATCH, SEQ, D_MODEL)),
        'norm1_gain': 1.0 + 0.1 * nrm(ks[1], (L, D_MODEL)),
        'w_in': lin(ks[2], (L, D_MODEL, IN_COLS), D_MODEL),
        'sb_q_gain': 1.0 + 0.1 * nrm(ks[3], (L, HEAD_DIM)),
        'sb_k_gain': 1.0 + 0.1 * nrm(ks[4], (L, HEAD_DIM)),
        'rw_shift_mu': jax.random.uniform(ks[5], (L, RW_COLS), f32),
        'rw_w0': jax.random.uniform(ks[6], (L, RW_WIDTH), f32, minval=-6.5, maxval=-1.5),
        'rw_w_up': 0.1 * lin(ks[7], (L, DECAY_LORA, RW_WIDTH), DECAY_LORA),
        'rw_a0': 0.1 * nrm(ks[8], (L, RW_WIDTH)),
        'rw_a_up': lin(ks[9], (L, AAA_LORA, RW_WIDTH), AAA_LORA),
        'rw_g_up': lin(ks[10], (L, GATE_LORA, RW_WIDTH), GATE_LORA),
        'rw_k_k': 0.85 + 0.05 * nrm(ks[11], (L, RW_WIDTH)),
        'rw_k_a': 1.0 + 0.05 * nrm(ks[12], (L, RW_WIDTH)),
        'rw_r_k': 0.1 * nrm(ks[13], (L, RW_HEADS, HEAD_DIM)),
        'rw_ln_w': 1.0 + 0.1 * nrm(ks[14], (L, RW_WIDTH)),
        'rw_ln_b': 0.02 * nrm(ks[15], (L, RW_WIDTH)),
        'w_out': lin(ks[16], (L, MIX_WIDTH, D_MODEL), MIX_WIDTH),
        'norm2_gain': 1.0 + 0.1 * nrm(ks[17], (L, D_MODEL)),
        'w_router_group': lin(ks[18], (L, D_MODEL, N_GROUPS), D_MODEL),
        'w_router_expert': lin(ks[19], (L, D_MODEL, N_EXPERTS), D_MODEL),
        'w_exp_gate': lin(ks[20], (L, N_EXPERTS, D_MODEL, D_EXPERT), D_MODEL),
        'w_exp_up': lin(ks[21], (L, N_EXPERTS, D_MODEL, D_EXPERT), D_MODEL),
        'w_exp_down': lin(ks[22], (L, N_EXPERTS, D_EXPERT, D_MODEL), D_EXPERT),
    }

def reference(x, norm1_gain, w_in, sb_q_gain, sb_k_gain, rw_shift_mu, rw_w0, rw_w_up, rw_a0,
              rw_a_up, rw_g_up, rw_k_k, rw_k_a, rw_r_k, rw_ln_w, rw_ln_b, w_out, norm2_gain,
              w_router_group, w_router_expert, w_exp_gate, w_exp_up, w_exp_down):
    B, S, _ = x.shape
    for l in range(DEPTH):
        h = rms_norm(x, norm1_gain[l])
        proj = h @ w_in[l]
        sb = proj[..., :SB_COLS]
        q = rms_norm(sb[..., :SB_WIDTH].reshape(B, S, SB_HEADS, HEAD_DIM), sb_q_gain[l]).transpose(0, 2, 1, 3)
        k = rms_norm(sb[..., SB_WIDTH:2 * SB_WIDTH].reshape(B, S, SB_HEADS, HEAD_DIM), sb_k_gain[l]).transpose(0, 2, 1, 3)
        v = sb[..., 2 * SB_WIDTH:].reshape(B, S, SB_HEADS, HEAD_DIM).transpose(0, 2, 1, 3)
        sb_out = stick_breaking_attention(q, k, v).transpose(0, 2, 1, 3).reshape(B, S, SB_WIDTH)
        rw_out = rwkv7_time_mix(proj[..., SB_COLS:], rw_shift_mu[l], rw_w0[l], rw_w_up[l], rw_a0[l],
                                rw_a_up[l], rw_g_up[l], rw_k_k[l], rw_k_a[l], rw_r_k[l],
                                rw_ln_w[l], rw_ln_b[l])
        mix = jnp.concatenate([sb_out, rw_out], axis=-1)
        x = x + mix @ w_out[l]
        h2 = rms_norm(x, norm2_gain[l])
        x = x + hierarchical_moe(h2, w_router_group[l], w_router_expert[l],
                                 w_exp_gate[l], w_exp_up[l], w_exp_down[l])
    return x


_drawn_inputs = setup_inputs


def setup_inputs(seed=0):
    import zlib

    import numpy as np

    out = dict(_drawn_inputs(seed))
    spreads = {}
    factors = {'rw_w_up': 7.651, 'rw_ln_b': 3.108}
    for name, (base, spread) in spreads.items():
        noise = np.random.default_rng([zlib.crc32(name.encode()), seed]).standard_normal(out[name].shape)
        drawn = base * np.exp(spread * noise) if base else spread * noise
        out[name] = __import__('jax').numpy.asarray(drawn.astype(out[name].dtype))
    for name, factor in factors.items():
        out[name] = (out[name] * factor).astype(out[name].dtype)
    return out
```

```python
from contextlib import ExitStack

import concourse.bass as bass
from concourse import mybir

F32 = mybir.dt.float32
I32 = mybir.dt.int32
U32 = mybir.dt.uint32
ALU = mybir.AluOpType
ACT = mybir.ActivationFunctionType
AX_X = mybir.AxisListType.X

P = 128
SEQ, D = 2048, 1024
NT = SEQ // P
KT = D // P
HD = 64
SBW = D // 2
SB_COLS = 3 * SBW
LW, LA, LG = 32, 32, 96
RW_COLS = 3 * SBW + LW + LA + LG
IN_COLS = SB_COLS + RW_COLS
PAIRS = SBW // P
N_GROUPS, PER_GROUP = 4, 8
NE = N_GROUPS * PER_GROUP
FF = 512
MAX_BLOCKS = 2 * SEQ // P + NE
TABLE = MAX_BLOCKS + SEQ // P + 1
NORM_EPS, LN_X_EPS = 1e-6, 64e-5
EXP_HALF = 0.6065306597126334


class Program:

    def __init__(self, nc, stack):
        self.stack = stack
        self.gates_passed = [stack.enter_context(nc.semaphore(f"gates_passed_{e}")) for e in "sp act pe dve pool".split()]


CREDIT = 16


def give_credit(nc, *semaphores):
    with nc.Block() as block:
        @block.sync
        def _(sp):
            for s in semaphores:
                sp.sem_inc(s, CREDIT)


def makers(nc, ctx, program):
    def sb(name, shape, dt=F32):
        return ctx.enter_context(nc.sbuf_tensor(name, shape, dt))

    def pb(name, shape):
        return ctx.enter_context(nc.psum_tensor(name, shape, F32))

    def sem(name):
        return program.stack.enter_context(nc.semaphore(name))

    return sb, pb, sem


def identity(pool, tile):
    pool.memset(tile, 0.0)
    pool.drain()
    return pool.affine_select(out=tile, in_=tile, compare_op=ALU.not_equal, fill=1.0, base=0,
                              pattern=[[-1, P]], channel_multiplier=1)


def project_tokens(nc, program, h_all, x, norm1_gain, w_in, sb_q_gain, sb_k_gain, qT_dram, kT_dram, v_dram):
    with ExitStack() as ctx:
        sb, pb, sem = makers(nc, ctx, program)
        w_sb = sb("w_sb", [P, KT, SB_COLS])
        x_t = sb("x_t", [P, 2, D])
        squares = sb("squares", [P, D])
        hT = sb("hT", [P, 2, KT, P])
        gain = sb("gain", [P, KT])
        qkv = sb("qkv", [P, 2, 3, SBW])
        qk_sq = sb("qk_sq", [P, 2 * SBW])
        qkT = sb("qkT", [P, 8, P])
        qk_gain = sb("qk_gain", [P, 2, HD])
        ssum = sb("ssum", [P, 1])
        root = sb("root", [P, 1])
        rstd = sb("rstd", [P, 1])
        qk_sum = sb("qk_sum", [P, 16])
        qk_root = sb("qk_root", [P, 16])
        qk_rstd = sb("qk_rstd", [P, 16])
        eps = sb("eps", [P, 1])
        ident = sb("ident", [P, P])
        xT_ps = pb("xT_ps", [P, KT, P])
        qkv_ps = pb("qkv_ps", [P, 3, SBW])
        qkT_ps = pb("qkT_ps", [P, 8, P])

        consts = sem("p1_consts")
        weights = sem("p1_weights")
        x_loaded = [sem(f"p1_x_loaded{s}") for s in range(2)]
        rooted = sem("p1_rooted")
        scaled = sem("p1_scaled")
        x_turned = sem("p1_x_turned")
        h_ready = sem("p1_h_ready")
        h_kept = sem("p1_h_kept")
        projected = sem("p1_projected")
        qkv_copied = sem("p1_qkv_copied")
        qk_summed = sem("p1_qk_summed")
        qk_rooted = sem("p1_qk_rooted")
        qk_ready = sem("p1_qk_ready")
        qk_turned = sem("p1_qk_turned")
        qkT_ready = sem("p1_qkT_ready")
        stored = sem("p1_stored")
        on_sp, on_act, on_pe, on_dve, on_pool = program.gates_passed
        qT_v = qT_dram.rearrange("(c p) t -> p c t", p=P)
        kT_v = kT_dram.rearrange("(c p) t -> p c t", p=P)
        give_credit(nc, h_ready, qkT_ready, qk_turned, qkv_copied, scaled, stored)
        with nc.Block() as block:
            @block.sync
            def _(sp):
                def load(t, s):
                    sp.dma_start(x_t[:, s, :], x[0, bass.ds(t * P, P), :]).then_inc(x_loaded[s], 16)

                def store(t, s):
                    sp.wait_ge(qkT_ready, CREDIT + t * 2 + 2)
                    sp.dma_start(qT_v[:, :, bass.ds(t * P, P)], qkT[:, 0:4, :]).then_inc(stored, 16)
                    sp.dma_start(kT_v[:, :, bass.ds(t * P, P)], qkT[:, 4:8, :]).then_inc(stored, 16)
                    sp.dma_start(v_dram[bass.ds(t * P, P), :], qkv[:, s, 2, :]).then_inc(stored, 16)

                with nc.allow_non_contiguous_dma("a small vector, once"):
                    sp.dma_start(gain[:, :], norm1_gain[0, :].rearrange("(k p) -> p k", p=P)).then_inc(weights, 16)
                sp.dma_start(qk_gain[:, 0, :], sb_q_gain[0, :].partition_broadcast(P)).then_inc(weights, 16)
                sp.dma_start(qk_gain[:, 1, :], sb_k_gain[0, :].partition_broadcast(P)).then_inc(weights, 16)
                load(0, 0)
                load(1, 1)
                for k in range(KT):
                    sp.dma_start(w_sb[:, k, :], w_in[0, k * P:(k + 1) * P, 0:SB_COLS]).then_inc(weights, 16)
                with sp.Fori(0, NT // 2 - 1) as i:
                    for s in range(2):
                        t = i * 2 + s
                        sp.wait_ge(x_turned, t + 1)
                        load(t + 2, s)
                        store(t, s)
                for t in (NT - 2, NT - 1):
                    store(t, t % 2)
                sp.wait_ge(stored, CREDIT + NT * 48)

            @block.gpsimd
            def _(pool):
                pool.memset(eps[:, :], NORM_EPS)
                identity(pool, ident[:, :]).then_inc(consts, 1)
                pool.drain()
                pool.sem_inc(consts, 1)
                with pool.Fori(0, NT // 2) as i:
                    for s in range(2):
                        t = i * 2 + s
                        pool.wait_ge(h_ready, CREDIT + t * 2 + 2)
                        pool.sem_inc(on_pool, 1)
                        pool.tensor_copy(h_all[:, :, bass.ds(t * P, P)], hT[:, s, :, :]).then_inc(h_kept, 1)

            def tile_pairs(eng, one_tile):
                for s in range(2):
                    one_tile(s, s, first=(s == 0), last=False)
                with eng.Fori(1, NT // 2 - 1) as i:
                    for s in range(2):
                        one_tile(i * 2 + s, s, first=False, last=False)
                for s in range(2):
                    one_tile(NT - 2 + s, s, first=False, last=(s == 1))

            @block.scalar
            def _(act):
                def norm(t, s, n):
                    act.wait_ge(scaled, CREDIT + t)
                    act.wait_ge(x_loaded[s], n * 16 + 16)
                    act.activation(squares[:, :], x_t[:, s, :], ACT.Square, accum_out=ssum[:, :])
                    act.drain()
                    act.activation(root[:, :], ssum[:, :], ACT.Sqrt, bias=eps[:, :], scale=1.0 / D).then_inc(rooted, 1)

                def copy_turned(t):
                    act.wait_ge(qk_turned, CREDIT + t + 1)
                    act.wait_ge(stored, CREDIT + t * 48)
                    for half in range(2):
                        act.copy(qkT[:, 4 * half:4 * half + 4, :], qkT_ps[:, 4 * half:4 * half + 4, :]).then_inc(qkT_ready, 1)

                def one_tile(t, s, first, last):
                    for part in range(3):
                        if part == 0:
                            act.wait_ge(qk_turned, CREDIT + t - 1)
                        if part == 2 and not first:
                            copy_turned(t - 1)
                        if part == 2 and not first:
                            act.wait_ge(stored, CREDIT + (t - 1) * 48)
                        act.wait_ge(projected, t * 3 + part + 1)
                        act.copy(qkv[:, s, part, :], qkv_ps[:, part, :]).then_inc(qkv_copied, 1)
                    act.wait_ge(qk_summed, t + 1)
                    act.activation(qk_root[:, :], qk_sum[:, :], ACT.Sqrt, bias=eps[:, :], scale=1.0 / HD).then_inc(qk_rooted, 1)

                act.wait_ge(consts, 2)
                norm(0, 0, 0)
                norm(1, 1, 0)
                for s in range(2):
                    one_tile(s, s, first=(s == 0), last=False)
                    norm(s + 2, s, 1)
                with act.Fori(1, NT // 2 - 1) as i:
                    for s in range(2):
                        one_tile(i * 2 + s, s, first=False, last=False)
                        norm(i * 2 + s + 2, s, i + 1)
                for s in range(2):
                    one_tile(NT - 2 + s, s, first=False, last=False)
                copy_turned(NT - 1)

            @block.vector
            def _(dve):
                def scale_x(t, s):
                    dve.wait_ge(rooted, t + 1)
                    dve.reciprocal(rstd[:, :], root[:, :])
                    dve.drain()
                    dve.tensor_scalar(x_t[:, s, :], x_t[:, s, :], rstd[:, :], None, ALU.mult).then_inc(scaled, 1)

                def keep_h(t, s):
                    dve.wait_ge(x_turned, t + 1)
                    dve.wait_ge(h_kept, t + 1)
                    for half in range(2):
                        ks = slice(4 * half, 4 * half + 4)
                        dve.tensor_tensor(hT[:, s, ks, :], xT_ps[:, ks, :],
                                          gain[:, ks].unsqueeze(2).to_broadcast([P, 4, P]), ALU.mult).then_inc(h_ready, 1)

                def one_tile(t, s, first, last):
                    if not last:
                        keep_h(t + 1, 1 - s)
                    heads = qkv[:, s, 0:2, :].rearrange("p a (h d) -> p (a h) d", d=HD)
                    dve.wait_ge(qkv_copied, CREDIT + t * 3 + 2)
                    dve.tensor_tensor(qk_sq[:, :], qkv[:, s, 0:2, :], qkv[:, s, 0:2, :], ALU.mult)
                    dve.drain()
                    dve.reduce_sum(qk_sum[:, :], qk_sq[:, :].rearrange("p (h d) -> p h d", d=HD), axis=AX_X).then_inc(qk_summed, 1)
                    dve.wait_ge(qk_rooted, t + 1)
                    dve.reciprocal(qk_rstd[:, :], qk_root[:, :])
                    dve.drain()
                    dve.tensor_tensor(heads, heads, qk_rstd[:, :].unsqueeze(2).to_broadcast([P, 16, HD]), ALU.mult)
                    dve.drain()
                    for a in range(2):
                        part = qkv[:, s, a, :].rearrange("p (h d) -> p h d", d=HD)
                        done = dve.tensor_tensor(part, part, qk_gain[:, a, :].unsqueeze(1).to_broadcast([P, 8, HD]), ALU.mult)
                    done.then_inc(qk_ready, 1)
                    if not (isinstance(t, int) and t + 2 >= NT):
                        scale_x(t + 2, s)

                dve.sem_inc(h_kept, 2)
                dve.wait_ge(weights, 16 * (3 + KT))
                scale_x(0, 0)
                dve.wait_ge(x_turned, 1)
                for half in range(2):
                    ks = slice(4 * half, 4 * half + 4)
                    dve.tensor_tensor(hT[:, 0, ks, :], xT_ps[:, ks, :],
                                      gain[:, ks].unsqueeze(2).to_broadcast([P, 4, P]), ALU.mult).then_inc(h_ready, 1)
                scale_x(1, 1)
                tile_pairs(dve, one_tile)

            @block.tensor
            def _(pe):
                def turn_x(t, s):
                    pe.wait_ge(scaled, CREDIT + t + 1)
                    pe.wait_ge(h_ready, CREDIT + t * 2)
                    for k in range(KT):
                        done = pe.transpose(xT_ps[:, k, :], x_t[:, s, k * P:(k + 1) * P], ident[:, :])
                    done.then_inc(x_turned, 1)

                def turn_qk(t, s):
                    pe.wait_ge(qk_ready, t + 1)
                    pe.wait_ge(qkT_ready, CREDIT + t * 2)
                    for c in range(8):
                        done = pe.transpose(qkT_ps[:, c, :], qkv[:, s, c // 4, (c % 4) * P:(c % 4 + 1) * P], ident[:, :])
                    done.then_inc(qk_turned, 1)

                def one_tile(t, s, first, last):
                    pe.wait_ge(h_ready, CREDIT + t * 2 + 2)
                    for part in range(3):
                        pe.wait_ge(qkv_copied, CREDIT + t * 3 - 2 + part)
                        for k in range(KT):
                            done = pe.matmul(qkv_ps[:, part, :], hT[:, s, k, :], w_sb[:, k, part * SBW:(part + 1) * SBW],
                                             start=(k == 0), stop=(k == KT - 1))
                        done.then_inc(projected, 1)
                        if part == 0 and not first:
                            turn_qk(t - 1, 1 - s)
                        if part == 1 and not last:
                            turn_x(t + 1, 1 - s)

                pe.wait_ge(consts, 2)
                turn_x(0, 0)
                tile_pairs(pe, one_tile)
                turn_qk(NT - 1, 1)


def project_channels(nc, program, h_all, w_in, rw_shift_mu, pT_dram):
    with ExitStack() as ctx:
        sb, pb, sem = makers(nc, ctx, program)
        NFULL = RW_COLS // P
        REST = RW_COLS - NFULL * P
        LOOPED = NFULL // 2 * 2
        GT = 512
        NG = SEQ // GT
        w = sb("w_ch", [P, 2, KT, P])
        mu = sb("mu", [P, NFULL + 1])
        p_raw = sb("p_raw", [P, 1 + SEQ])
        diff = sb("diff", [P, SEQ])
        shifted = sb("shifted", [P, 2, SEQ])
        mu_c = sb("mu_c", [P, 1])
        p_ps = pb("p_ps", [P, 2, NG, GT])
        mu_loaded = sem("p2_mu_loaded")
        w_loaded = [sem(f"p2_w_loaded{s}") for s in range(2)]
        projected = sem("p2_projected")
        copied = sem("p2_copied")
        mixed = sem("p2_mixed")
        stored = [sem(f"p2_stored{s}") for s in range(2)]
        zeroed = sem("p2_zeroed")
        on_sp, on_act, on_pe, on_dve, on_pool = program.gates_passed
        NCH = NFULL + 1
        give_credit(nc, mixed)
        with nc.Block() as block:
            @block.sync
            def _(sp):
                def load(c, s, width=P):
                    src = w_in[0, :, bass.ds(c * P + SB_COLS, width)].rearrange("(k p) c -> p k c", p=P)
                    sp.dma_start(w[:, s, :, 0:width], src).then_inc(w_loaded[s], 16)

                def store(c, s, width=P):
                    sp.wait_ge(mixed, CREDIT + c + 1)
                    sp.dma_start(pT_dram[bass.ds(c * P, width), :], shifted[0:width, s, :]).then_inc(stored[s], 16)

                load(0, 0)
                load(1, 1)
                with nc.allow_non_contiguous_dma("a small vector, once"):
                    sp.dma_start(mu[:, 0:NFULL], rw_shift_mu[0, 0:NFULL * P].rearrange("(k p) -> p k", p=P)).then_inc(mu_loaded, 16)
                    sp.dma_start(mu[0:REST, NFULL:NFULL + 1], rw_shift_mu[0, NFULL * P:RW_COLS].rearrange("(k p) -> p k", k=1)).then_inc(mu_loaded, 16)
                with sp.Fori(0, LOOPED // 2 - 1) as i:
                    for s in range(2):
                        c = i * 2 + s
                        sp.wait_ge(projected, (c + 1) * NG)
                        load(c + 2, s)
                        store(c, s)
                for c in range(LOOPED - 2, NCH):
                    if c + 2 < NCH:
                        sp.wait_ge(projected, (c + 1) * NG)
                        load(c + 2, c % 2, P if c + 2 < NFULL else REST)
                    store(c, c % 2, P if c < NFULL else REST)
                for s in range(2):
                    sp.wait_ge(stored[s], 16 * (NCH // 2) + 16)

            @block.tensor
            def _(pe):
                def chunk(c, s, n, width=P):
                    pe.wait_ge(w_loaded[s], n * 16 + 16)
                    for g in range(NG):
                        pe.wait_ge(copied, c * NG + g + 1)
                        for k in range(KT):
                            last = pe.matmul(p_ps[0:width, s, g, :], w[:, s, k, 0:width], h_all[:, k, g * GT:(g + 1) * GT],
                                             start=(k == 0), stop=(k == KT - 1))
                        last.then_inc(projected, 1)

                with pe.Fori(0, LOOPED // 2) as i:
                    for s in range(2):
                        chunk(i * 2 + s, s, i)
                for c in range(LOOPED, NCH):
                    chunk(c, c % 2, c // 2, P if c < NFULL else REST)

            @block.scalar
            def _(act):
                act.sem_inc(copied, 2 * NG)
                act.wait_ge(zeroed, 1)

                def chunk(c, s, n, width=P):
                    act.wait_ge(mixed, CREDIT + c)
                    for g in range(NG):
                        act.wait_ge(projected, c * NG + g + 1)
                        act.copy(p_raw[0:width, 1 + g * GT:1 + (g + 1) * GT], p_ps[0:width, s, g, :]).then_inc(copied, 1)

                with act.Fori(0, LOOPED // 2) as i:
                    for s in range(2):
                        chunk(i * 2 + s, s, i)
                for c in range(LOOPED, NCH):
                    chunk(c, c % 2, c // 2, P if c < NFULL else REST)

            @block.vector
            def _(dve):
                dve.memset(p_raw[:, 0:1], 0.0).then_inc(zeroed, 1)
                dve.wait_ge(mu_loaded, 32)
                dve.sem_inc(stored[0], 16)
                dve.sem_inc(stored[1], 16)

                def chunk(c, s, n, width=P):
                    dve.wait_ge(copied, (c + 1) * NG + 2 * NG)
                    dve.tensor_tensor(diff[0:width, :], p_raw[0:width, 0:SEQ], p_raw[0:width, 1:1 + SEQ], ALU.subtract)
                    dve.tensor_copy(mu_c[0:width, :], mu[0:width, bass.ds(c, 1)])
                    dve.drain()
                    dve.wait_ge(stored[s], n * 16 + 16)
                    dve.scalar_tensor_tensor(shifted[0:width, s, :], diff[0:width, :], mu_c[0:width, :],
                                             p_raw[0:width, 1:1 + SEQ], ALU.mult, ALU.add).then_inc(mixed, 1)

                with dve.Fori(0, LOOPED // 2) as i:
                    for s in range(2):
                        chunk(i * 2 + s, s, i)
                for c in range(LOOPED, NCH):
                    chunk(c, c % 2, c // 2, P if c < NFULL else REST)


def stick_breaking(nc, program, qT_dram, kT_dram, v_dram, mixT_dram):
    with ExitStack() as ctx:
        sb, pb, sem = makers(nc, ctx, program)
        CH = 512
        SLOTS = 3
        ZR = 3
        SCALE = HD ** -0.5
        units = [(t, h) for t in range(NT) for h in range(2)]
        n_chunks = [((t + 1) * P + CH - 1) // CH for t, _ in units]
        first = [sum(n_chunks[:u]) for u in range(len(units) + 1)]
        NU, NCH = len(units), first[-1]

        q_sb = sb("q_sb", [P, SEQ])
        k_sb = sb("k_sb", [P, SEQ])
        v_sb = sb("v_sb", [P, NT, P])
        keep = sb("keep", [P, SLOTS, SEQ])
        take = sb("take", [P, SLOTS, SEQ])
        prod = sb("prod", [P, SLOTS, SEQ])
        wT = sb("wT", [P, 2, CH])
        o_sb = sb("o_sb", [P, P])
        oT_sb = sb("oT_sb", [P, 2, P])
        ident = sb("ident_a", [P, P])
        z_ps = [pb(f"z_ps{i}", [P, CH]) for i in range(ZR)]
        wT_ps = [pb(f"wT_ps{i}", [P, CH]) for i in range(2)]
        o_banks = pb("o_banks", [P, 3, CH])
        o_ps = [o_banks[:, 0, 0:P], o_banks[:, 1, 0:P]]
        oT_ps = o_banks[:, 2, 0:P]

        consts = sem("p3_consts")
        qkv_loaded = sem("p3_qkv_loaded")
        z_done = sem("p3_z_done")
        z_read = sem("p3_z_read")
        masked = sem("p3_masked")
        scanned = sem("p3_scanned")
        weighted = sem("p3_weighted")
        turned = sem("p3_turned")
        turned_copied = sem("p3_turned_copied")
        weighed = sem("p3_weighed")
        o_copied = sem("p3_o_copied")
        o_turned = sem("p3_o_turned")
        oT_copied = sem("p3_oT_copied")
        stored = [sem(f"p3_stored{s}") for s in range(2)]
        on_sp, on_act, on_pe, on_dve, on_pool = program.gates_passed

        give_credit(nc, oT_copied, o_copied, o_turned, *stored, turned_copied, weighed, z_read)
        with nc.Block() as block:
            @block.sync
            def _(sp):
                with sp.Fori(0, PAIRS) as j:
                    sp.wait_ge(weighed, CREDIT + j * NCH)
                    sp.dma_start(q_sb[:, :], qT_dram[bass.ds(j * P, P), :]).then_inc(qkv_loaded, 16)
                    sp.dma_start(k_sb[:, :], kT_dram[bass.ds(j * P, P), :]).then_inc(qkv_loaded, 16)
                    sp.dma_start(v_sb[:, :, :], v_dram[:, bass.ds(j * P, P)].rearrange("(n p) c -> p n c", p=P)).then_inc(qkv_loaded, 16)
                    for t in range(NT):
                        sp.wait_ge(oT_copied, CREDIT + j * NT + t + 1)
                        sp.dma_start(mixT_dram[bass.ds(j * P, P), t * P:(t + 1) * P], oT_sb[:, t % 2, :]).then_inc(stored[t % 2], 16)
                for s in range(2):
                    sp.wait_ge(stored[s], CREDIT + 16 * PAIRS * NT // 2)

            @block.tensor
            def _(pe):
                pe.wait_ge(consts, 1)

                def scores(j, u, c):
                    if u >= NU or c >= n_chunks[u]:
                        return
                    (t, h), n = units[u], first[u] + c
                    hs = slice(h * HD, (h + 1) * HD)
                    w = min(CH, (t + 1) * P - c * CH)
                    pe.wait_ge(z_read, CREDIT + j * NCH + max(n - ZR + 1, 0))
                    pe.matmul(z_ps[n % ZR][:, 0:w], q_sb[hs, t * P:(t + 1) * P], k_sb[hs, c * CH:c * CH + w],
                              start=True, stop=True).then_inc(z_done, 1)

                def turn(j, u, c):
                    t, n = units[u][0], first[u] + c
                    if c == 0:
                        pe.wait_ge(weighted, j * NU + u + 1)
                    pe.wait_ge(turned_copied, CREDIT + j * NCH + max(n - 1, 0))
                    for b in range(min(4, t + 1 - 4 * c)):
                        s0 = c * CH + b * P
                        last = pe.transpose(wT_ps[n % 2][:, b * P:(b + 1) * P], take[:, u % SLOTS, s0:s0 + P], ident[:, :])
                    last.then_inc(turned, 1)

                def weigh(j, u, c):
                    (t, h), n = units[u], first[u] + c
                    pe.wait_ge(turned_copied, CREDIT + j * NCH + n + 1)
                    if c == 0 and h == 0:
                        pe.wait_ge(o_copied, CREDIT + j * NT + max(t - 1, 0))
                    for b in range(min(4, t + 1 - 4 * c)):
                        s = 4 * c + b
                        last = pe.matmul(o_ps[t % 2][:, h * HD:(h + 1) * HD], wT[:, n % 2, b * P:(b + 1) * P],
                                         v_sb[:, s, h * HD:(h + 1) * HD], start=(s == 0), stop=(s == t))
                    last.then_inc(weighed, 1)

                def turn_out(j, t):
                    pe.wait_ge(o_copied, CREDIT + j * NT + t + 1)
                    pe.wait_ge(oT_copied, CREDIT + j * NT + t)
                    pe.transpose(oT_ps, o_sb[:, :], ident[:, :]).then_inc(o_turned, 1)

                with pe.Fori(0, PAIRS) as j:
                    pe.wait_ge(qkv_loaded, j * 48 + 48)
                    scores(j, 0, 0)
                    scores(j, 1, 0)
                    for u, (t, h) in enumerate(units):
                        turn(j, u, 0)
                        for c in range(n_chunks[u]):
                            scores(j, u + 2, c)
                            if c + 1 < n_chunks[u]:
                                turn(j, u, c + 1)
                            weigh(j, u, c)
                        for c in range(n_chunks[u], n_chunks[min(u + 2, NU - 1)]):
                            scores(j, u + 2, c)
                        if h == 1 and t >= 1:
                            turn_out(j, t - 1)
                    turn_out(j, NT - 1)

            @block.scalar
            def _(act):
                def copy_out(j, t):
                    act.wait_ge(weighed, CREDIT + j * NCH + first[2 * t + 2])
                    act.wait_ge(o_turned, CREDIT + j * NT + t)
                    act.copy(o_sb[:, :], o_ps[t % 2]).then_inc(o_copied, 1)

                def copy_turned(j, t):
                    act.wait_ge(o_turned, CREDIT + j * NT + t + 1)
                    if t >= 2:
                        act.wait_ge(stored[t % 2], CREDIT + j * (8 * NT) + 16 * (t // 2))
                    else:
                        act.wait_ge(stored[t % 2], CREDIT + j * (8 * NT))
                    act.copy(oT_sb[:, t % 2, :], oT_ps).then_inc(oT_copied, 1)

                with act.Fori(0, PAIRS) as j:
                    for u, (t, h) in enumerate(units):
                        act.wait_ge(weighed, CREDIT + j * NCH + first[max(u - SLOTS + 1, 0)])
                        if h == 0 and t >= 2:
                            copy_out(j, t - 2)
                        if h == 0 and t >= 3:
                            copy_turned(j, t - 3)
                        for c in range(n_chunks[u]):
                            n = first[u] + c
                            w = min(CH, (t + 1) * P - c * CH)
                            cols = slice(c * CH, c * CH + w)
                            act.wait_ge(z_done, j * NCH + n + 1)
                            act.activation(keep[:, u % SLOTS, cols], z_ps[n % ZR][:, 0:w], ACT.Sigmoid, scale=-SCALE)
                            act.activation(take[:, u % SLOTS, cols], z_ps[n % ZR][:, 0:w], ACT.Sigmoid, scale=SCALE).then_inc(z_read, 1)
                    copy_out(j, NT - 2)
                    copy_turned(j, NT - 3)
                    copy_turned(j, NT - 2)
                    copy_out(j, NT - 1)
                    copy_turned(j, NT - 1)

            @block.gpsimd
            def _(pool):
                identity(pool, ident[:, :]).then_inc(consts, 1)

                def mask(j, u):
                    t, slot = units[u][0], u % SLOTS
                    diag = slice(t * P, (t + 1) * P)
                    pool.wait_ge(z_read, CREDIT + j * NCH + first[u + 1])
                    pool.sem_inc(on_pool, 1)
                    for tile, fill in ((keep, 1.0), (take, 0.0)):
                        last = pool.affine_select(out=tile[:, slot, diag], in_=tile[:, slot, diag], compare_op=ALU.is_gt,
                                                  fill=fill, base=0, pattern=[[-1, P]], channel_multiplier=1)
                    last.then_inc(masked, 1)

                def weight(j, u):
                    t, slot = units[u][0], u % SLOTS
                    L = (t + 1) * P
                    pool.wait_ge(scanned, j * NU + u + 1)
                    pool.sem_inc(on_pool, 1)
                    pool.tensor_tensor(take[:, slot, 0:L - 1], take[:, slot, 0:L - 1], prod[:, slot, 1:L],
                                       ALU.mult).then_inc(weighted, 1)

                with pool.Fori(0, PAIRS) as j:
                    for u in range(NU):
                        mask(j, u)
                        weight(j, u)

            @block.vector
            def _(dve):
                def scan(j, u):
                    t, slot = units[u][0], u % SLOTS
                    L = (t + 1) * P
                    dve.wait_ge(masked, j * NU + u + 1)
                    rows = keep[:, slot, 0:L][:, ::-1]
                    dve.tensor_tensor_scan(prod[:, slot, 0:L][:, ::-1], rows, rows, 1.0, ALU.mult, ALU.bypass).then_inc(scanned, 1)

                with dve.Fori(0, PAIRS) as j:
                    scan(j, 0)
                    for u in range(NU):
                        for c in range(n_chunks[u]):
                            n = first[u] + c
                            w = min(CH, (units[u][0] + 1) * P - c * CH)
                            dve.wait_ge(turned, j * NCH + n + 1)
                            dve.wait_ge(weighed, CREDIT + j * NCH + max(n - 1, 0))
                            dve.tensor_copy(wT[:, n % 2, 0:w], wT_ps[n % 2][:, 0:w]).then_inc(turned_copied, 1)
                            if c == 0 and u + 1 < NU:
                                scan(j, u + 1)


def time_mixing(nc, program, w0, w_up, a0, a_up, g_up, k_k, k_a, r_k, ln_w, ln_b, pT_dram, mixT_dram):
    with ExitStack() as ctx:
        sb, pb, sem = makers(nc, ctx, program)
        C = HD
        GT = 512
        NG, NC = SEQ // GT, GT // C
        HC = NC // 2
        LEVELS = (2, 4, 8, 16, 32)
        LORA = 3 * SBW

        rkv = sb("rkv", [P, 3, GT])
        wd = sb("wd", [LW, GT])
        ad = sb("ad", [LA, GT])
        gd = sb("gd", [LG, GT])
        w_up_p = sb("w_up_p", [LW, P])
        a_up_p = sb("a_up_p", [LA, P])
        g_up_p = sb("g_up_p", [LG, P])
        vecs = sb("vecs", [P, 7])
        ident = sb("ident_r", [P, P])
        head_ones = sb("head_ones", [P, P])
        chunk_reset = sb("chunk_reset", [P, GT])
        zero_eps = sb("zero_eps", [P, 2])
        below = sb("below", [P, 2, C])
        lev = sb("lev", [P, 5, C])
        lev1T = sb("lev1T", [P, C])
        lev1 = sb("lev1", [P, C])
        eye = sb("eye", [P, C])
        t0, t1, t2, t3, t4, t5 = [sb(f"tmp{i}", [P, GT]) for i in range(6)]
        kk, a_g, g, kka, k2, bonus = [sb(n, [P, GT]) for n in ("kk", "a_g", "g", "kka", "k2", "bonus")]
        Lsum, Dec, DecP, DecI = [sb(n, [P, GT]) for n in ("Lsum", "Dec", "DecP", "DecI")]
        AR = sb("AR", [P, NC, 2, C])
        b_t, k_t, b_h, k_h = [sb(n, [P, GT]) for n in ("b_t", "k_t", "b_h", "k_h")]
        tok = sb("tok", [P, 4, NC, C])
        aT, bT, kT, vT = [tok[:, i, :, :] for i in range(4)]
        SB1 = sb("SB1", [P, NC, 2, C])
        SB2 = sb("SB2", [P, NC, 2, C])
        ATl = sb("ATl", [P, 5, NC, C])
        XX = sb("XX", [P, 2, NC, C])
        T1 = sb("T1", [P, NC, C])
        GW = sb("GW", [P, 2, NC, C])
        SA = sb("SA", [P, C])
        S = sb("S_state", [P, C])
        y = sb("y_sb", [P, GT])
        outp = sb("outp", [P, GT])
        PQ = [pb(f"PQ{i}", [P, 2, 512]) for i in range(4)]

        names = """weights consts loaded lora_ready lora_done g_done sig_ready kk2_ready norm_done root_ready
            L_ready exp_ready rk_ready bonus_done bonus_ready operands_ready turnedA_done turnedB_done tokA_ready
            tokB_ready scores1_done scores2_done scores1_ready scores2_ready A_done levels_ready X_ready T_done
            T_ready dX_done GW_done GW_ready sa_done saA_ready saB_ready dS_done S_ready y_done y_ready mean_done
            centred_ready var_done std_ready out_ready stored""".split()
        s_ = {n: sem(f"p4_{n}") for n in names}
        (weights, consts, loaded, lora_ready, lora_done, g_done, sig_ready, kk2_ready, norm_done, root_ready,
         L_ready, exp_ready, rk_ready, bonus_done, bonus_ready, operands_ready, turnedA_done, turnedB_done, tokA_ready,
         tokB_ready, scores1_done, scores2_done, scores1_ready, scores2_ready, A_done, levels_ready, X_ready, T_done,
         T_ready, dX_done, GW_done, GW_ready, sa_done, saA_ready, saB_ready, dS_done, S_ready, y_done, y_ready, mean_done,
         centred_ready, var_done, std_ready, out_ready, stored) = [s_[n] for n in names]
        on_sp, on_act, on_pe, on_dve, on_pool = program.gates_passed
        N_CONSTS = 2

        def chunks(tile):
            return tile[:, :].rearrange("p (c t) -> p c t", t=C)

        def two(bank_pair):
            return bank_pair[:, :, :].rearrange("p b (q x) -> p b q x", q=2)

        def two_sb(tile):
            return tile.rearrange("p q (b h) c -> p b q (h c)", b=2)

        give_credit(nc, out_ready, stored)
        with nc.Block() as block:
            @block.sync
            def _(sp):
                with sp.Fori(0, PAIRS) as j:
                    sp.wait_ge(out_ready, CREDIT + j * NG)
                    cols = bass.ds(j * P, P)
                    sp.dma_start(w_up_p[:, :], w_up[0, :, cols]).then_inc(weights, 16)
                    sp.dma_start(a_up_p[:, :], a_up[0, :, cols]).then_inc(weights, 16)
                    sp.dma_start(g_up_p[:, :], g_up[0, :, cols]).then_inc(weights, 16)
                    for i, vec in enumerate((w0[0], a0[0], k_k[0], k_a[0], r_k[0].rearrange("h d -> (h d)"), ln_w[0], ln_b[0])):
                        sp.dma_start(vecs[:, i:i + 1], vec[cols].unsqueeze(1)).then_inc(weights, 16)
                    with sp.Fori(0, NG) as gi:
                        n = j * NG + gi
                        sp.wait_ge(out_ready, CREDIT + n)
                        ts = bass.ds(gi * GT, GT)
                        for a in range(3):
                            sp.dma_start(rkv[:, a, :], pT_dram[bass.ds(j * P + a * SBW, P), ts]).then_inc(loaded, 16)
                        sp.dma_start(wd[:, :], pT_dram[LORA:LORA + LW, ts]).then_inc(loaded, 16)
                        sp.dma_start(ad[:, :], pT_dram[LORA + LW:LORA + LW + LA, ts]).then_inc(loaded, 16)
                        sp.dma_start(gd[:, :], pT_dram[LORA + LW + LA:LORA + LW + LA + LG, ts]).then_inc(loaded, 16)
                        sp.wait_ge(out_ready, CREDIT + n + 1)
                        sp.dma_start(mixT_dram[bass.ds(j * P + SBW, P), ts], outp[:, :]).then_inc(stored, 16)
                sp.wait_ge(stored, CREDIT + 16 * PAIRS * NG)

            @block.gpsimd
            def _(pool):
                def block_select(tile, op, base, pattern, mult, fill=0.0):
                    pool.affine_select(out=tile, in_=tile, compare_op=op, fill=fill, base=base,
                                       pattern=pattern, channel_multiplier=mult)
                    pool.drain()

                identity(pool, ident[:, :])
                pool.drain()
                pool.memset(head_ones[:, :], 0.0)
                pool.memset(chunk_reset[:, :], 1.0)
                pool.memset(below[:, :, :], 1.0)
                pool.memset(lev[:, :, :], 0.0)
                pool.memset(lev1[:, :], 0.0)
                pool.memset(lev1T[:, :], 0.0)
                pool.memset(zero_eps[:, 0:1], 0.0)
                pool.memset(zero_eps[:, 1:2], LN_X_EPS)
                pool.drain()
                pool.memset(chunks(chunk_reset)[:, :, 0:1], 0.0)
                for h in range(2):
                    hs = slice(h * C, (h + 1) * C)
                    pool.memset(head_ones[hs, hs], 1.0)
                    pool.tensor_copy(eye[hs, :], ident[hs, hs])
                    block_select(below[hs, 0, :], ALU.is_gt, 0, [[1, C]], -1)
                    block_select(below[hs, 1, :], ALU.is_ge, 0, [[1, C]], -1)
                    block_select(lev1T[hs, :].rearrange("p (n b) -> p n b", b=2)[:, :, 0], ALU.not_equal, -1, [[-2, C // 2]], 1, 1.0)
                    block_select(lev1[hs, :].rearrange("p (n b) -> p n b", b=2)[:, :, 1], ALU.not_equal, 0, [[-2, C // 2]], 1, 1.0)
                    for i, size in enumerate(LEVELS):
                        v = lev[hs, i, :].rearrange("p (n b s) -> p n b s", b=2, s=size)[:, :, 1, :]
                        nb = C // (2 * size)
                        pool.memset(v, 1.0)
                        pool.drain()
                        block_select(v, ALU.is_ge, 0, [[-2 * size, nb], [0, size]], 1)
                        block_select(v, ALU.is_ge, size - 1, [[2 * size, nb], [0, size]], -1)
                pool.drain()
                pool.sem_inc(consts, N_CONSTS)
                with pool.Fori(0, PAIRS * NG) as n:
                    pool.wait_ge(scores1_ready, n + 1)
                    pool.sem_inc(on_pool, 1)
                    for i in range(5):
                        pool.tensor_tensor(ATl[:, i, :, :], SB1[:, :, 0, :], lev[:, i, :].unsqueeze(1).to_broadcast([P, NC, C]),
                                           ALU.mult).then_inc(levels_ready, 1)

            @block.scalar
            def _(act):
                act.wait_ge(consts, N_CONSTS)
                with act.Fori(0, PAIRS) as j:
                    act.wait_ge(weights, j * 160 + 160)
                    with act.Fori(0, NG) as gi:
                        n = j * NG + gi
                        act.wait_ge(loaded, n * 96 + 96)
                        act.activation(wd[:, :], wd[:, :], ACT.Tanh)
                        act.activation(gd[:, :], gd[:, :], ACT.Sigmoid).then_inc(lora_ready, 1)
                        act.wait_ge(lora_done, n + 1)
                        act.activation(t0[:, :], PQ[0][:, 0, :], ACT.Sigmoid, bias=vecs[:, 0:1])
                        act.activation(a_g[:, :], PQ[0][:, 1, :], ACT.Sigmoid, bias=vecs[:, 1:2]).then_inc(sig_ready, 1)
                        act.wait_ge(L_ready, n + 1)
                        act.activation(Dec[:, :], Lsum[:, :], ACT.Exp)
                        act.activation(DecI[:, :], Lsum[:, :], ACT.Exp, scale=-1.0)
                        act.activation(DecP[:, :], t4[:, :], ACT.Exp).then_inc(exp_ready, 1)
                        act.wait_ge(norm_done, n + 1)
                        act.activation(t3[:, :], PQ[2][:, 0, :], ACT.Sqrt, bias=zero_eps[:, 0:1]).then_inc(root_ready, 1)
                        act.wait_ge(turnedA_done, n + 1)
                        act.copy(two_sb(tok[:, 0:2, :, :]), two(PQ[0])).then_inc(tokA_ready, 1)
                        act.wait_ge(turnedB_done, n + 1)
                        act.copy(two_sb(tok[:, 2:4, :, :]), two(PQ[1])).then_inc(tokB_ready, 1)
                        for i in range(5):
                            act.wait_ge(T_done, n * 5 + i + 1)
                            act.copy(T1[:, :, :].rearrange("p (b h) c -> p b (h c)", b=2), PQ[1][:, :, 0:256]).then_inc(T_ready, 1)
                        act.wait_ge(GW_done, n + 1)
                        act.copy(two_sb(GW[:, :, :, :]), two(PQ[1])).then_inc(GW_ready, 1)
                        for c in range(NC):
                            act.wait_ge(sa_done, n * NC + c + 1)
                            act.copy(SA[0:C, :], PQ[0][0:C, 0, c * C:(c + 1) * C]).then_inc(saA_ready, 1)
                        act.wait_ge(y_done, n + 1)
                        for h in range(2):
                            hs = slice(h * C, (h + 1) * C)
                            last = act.copy(y[hs, :], PQ[2][hs, h, :])
                        last.then_inc(y_ready, 1)
                        act.wait_ge(var_done, n + 1)
                        act.activation(t3[:, :], PQ[1][:, 1, :], ACT.Sqrt, bias=zero_eps[:, 1:2], scale=1.0 / HD).then_inc(std_ready, 1)

            @block.vector
            def _(dve):
                r, k, v = [rkv[:, a, :] for a in range(3)]
                w0_c, a0_c, kk_c, ka_c, rk_c, lnw_c, lnb_c = [vecs[:, i:i + 1] for i in range(7)]
                dve.wait_ge(consts, N_CONSTS)
                with dve.Fori(0, PAIRS) as j:
                    dve.wait_ge(weights, j * 160 + 160)
                    dve.memset(S[:, :], 0.0).then_inc(S_ready, 1)
                    with dve.Fori(0, NG) as gi:
                        n = j * NG + gi
                        dve.wait_ge(loaded, n * 96 + 96)
                        dve.tensor_scalar(t1[:, :], k, kk_c, None, ALU.mult)
                        dve.drain()
                        dve.tensor_tensor(t2[:, :], t1[:, :], t1[:, :], ALU.mult).then_inc(kk2_ready, 1)
                        dve.wait_ge(g_done, n + 1)
                        dve.tensor_copy(g[:, :], PQ[1][:, 0, :])
                        dve.wait_ge(sig_ready, n + 1)
                        dve.tensor_scalar(t0[:, :], t0[:, :], -EXP_HALF, None, ALU.mult)
                        dve.drain()
                        dve.tensor_tensor_scan(Lsum[:, :], chunk_reset[:, :], t0[:, :], 0.0, ALU.mult, ALU.add)
                        dve.drain()
                        dve.tensor_tensor(t4[:, :], Lsum[:, :], t0[:, :], ALU.subtract).then_inc(L_ready, 1)
                        dve.tensor_scalar(t5[:, :], a_g[:, :], -1.0, ka_c, ALU.add, ALU.mult)
                        dve.drain()
                        dve.scalar_tensor_tensor(k2[:, :], t5[:, :], 1.0, k, ALU.add, ALU.mult)
                        dve.wait_ge(root_ready, n + 1)
                        dve.tensor_scalar(t3[:, :], t3[:, :], 1e-12, None, ALU.max)
                        dve.drain()
                        dve.reciprocal(t3[:, :], t3[:, :])
                        dve.drain()
                        dve.tensor_tensor(kk[:, :], t1[:, :], t3[:, :], ALU.mult)
                        dve.drain()
                        dve.tensor_tensor(kka[:, :], kk[:, :], a_g[:, :], ALU.mult)
                        dve.scalar_tensor_tensor(t2[:, :], r, rk_c, k2[:, :], ALU.mult, ALU.mult).then_inc(rk_ready, 1)
                        dve.drain()
                        dve.wait_ge(exp_ready, n + 1)
                        dve.scalar_tensor_tensor(AR[:, :, 0, :], chunks(kk), -1.0, chunks(DecP), ALU.mult, ALU.mult)
                        dve.tensor_tensor(AR[:, :, 1, :], r.rearrange("p (c t) -> p c t", t=C), chunks(Dec), ALU.mult)
                        dve.tensor_tensor(b_t[:, :], kka[:, :], DecI[:, :], ALU.mult)
                        dve.tensor_tensor(k_t[:, :], k2[:, :], DecI[:, :], ALU.mult)
                        dve.drain()
                        end = chunks(Dec)[:, :, C - 1:C].to_broadcast([P, NC, C])
                        dve.tensor_tensor(chunks(b_h), chunks(b_t), end, ALU.mult)
                        dve.tensor_tensor(chunks(k_h), chunks(k_t), end, ALU.mult).then_inc(operands_ready, 1)
                        dve.wait_ge(bonus_done, n + 1)
                        dve.tensor_tensor(bonus[:, :], PQ[2][:, 1, :], v, ALU.mult).then_inc(bonus_ready, 1)
                        low = below[:, :, :].rearrange("p a t -> p (a t)").unsqueeze(1).to_broadcast([P, NC, 2 * C])
                        for done, ready, bank, out in ((scores1_done, scores1_ready, PQ[2], SB1), (scores2_done, scores2_ready, PQ[3], SB2)):
                            dve.wait_ge(done, n + 1)
                            dve.tensor_tensor(out[:, :, :, :].rearrange("p c a t -> p c (a t)"),
                                              bank[:, :, :].rearrange("p b (h x) -> p (b h) x", x=2 * C), low, ALU.mult).then_inc(ready, 1)
                        dve.drain()
                        dve.tensor_tensor(XX[:, 1, :, :], SB1[:, :, 0, :], lev1[:, :].unsqueeze(1).to_broadcast([P, NC, C]), ALU.mult)
                        dve.wait_ge(A_done, n + 1)
                        dve.tensor_tensor(XX[:, 0, :, :].rearrange("p (b h) c -> p b h c", b=2),
                                          two(PQ[0])[:, :, 0, :].rearrange("p b (h c) -> p b h c", c=C),
                                          lev1T[:, :].unsqueeze(1).unsqueeze(1).to_broadcast([P, 2, HC, C]), ALU.mult)
                        dve.drain()
                        both = XX[:, :, :, :].rearrange("p q n c -> p (q n) c")
                        dve.tensor_tensor(both, both, eye[:, :].unsqueeze(1).to_broadcast([P, 2 * NC, C]), ALU.add).then_inc(X_ready, 1)
                        for i in range(5):
                            dve.wait_ge(dX_done, n * 5 + i + 1)
                            dve.tensor_tensor(two_sb(XX[:, :, :, :]), two_sb(XX[:, :, :, :]), two(PQ[0]), ALU.add).then_inc(X_ready, 1)
                        for c in range(NC):
                            dve.wait_ge(sa_done, n * NC + c + 1)
                            dve.tensor_copy(SA[C:P, :], PQ[0][C:P, 1, c * C:(c + 1) * C]).then_inc(saB_ready, 1)
                            dve.wait_ge(dS_done, n * NC + c + 1)
                            for h in range(2):
                                hs = slice(h * C, (h + 1) * C)
                                last = dve.scalar_tensor_tensor(S[hs, :], S[hs, :], Dec[hs, (c + 1) * C - 1:(c + 1) * C],
                                                                PQ[3][hs, h, 0:C], ALU.mult, ALU.add)
                            last.then_inc(S_ready, 1)
                        dve.wait_ge(y_ready, n + 1)
                        dve.wait_ge(mean_done, n + 1)
                        dve.scalar_tensor_tensor(y[:, :], PQ[1][:, 0, :], -1.0 / HD, y[:, :], ALU.mult, ALU.add)
                        dve.drain()
                        dve.tensor_tensor(t2[:, :], y[:, :], y[:, :], ALU.mult).then_inc(centred_ready, 1)
                        dve.wait_ge(std_ready, n + 1)
                        dve.reciprocal(t3[:, :], t3[:, :])
                        dve.drain()
                        dve.tensor_tensor(y[:, :], y[:, :], t3[:, :], ALU.mult)
                        dve.drain()
                        dve.tensor_scalar(y[:, :], y[:, :], lnw_c, lnb_c, ALU.mult, ALU.add)
                        dve.drain()
                        dve.tensor_tensor(y[:, :], y[:, :], bonus[:, :], ALU.add)
                        dve.drain()
                        dve.wait_ge(stored, CREDIT + n * 16)
                        dve.tensor_tensor(outp[:, :], y[:, :], g[:, :], ALU.mult).then_inc(out_ready, 1)

            @block.tensor
            def _(pe):
                HS = [slice(0, C), slice(C, P)]

                def two_heads(one):
                    for c in range(HC):
                        one(0, c)
                        last = one(1, HC + c)
                    for c in range(HC):
                        one(1, c)
                        last = one(0, HC + c)
                    return last

                def place(bank_pair, q, h, c):
                    x = q * 256 + (c % HC) * C
                    return bank_pair[HS[h], c // HC, x:x + C]

                def at(tile, h, c):
                    return tile[HS[h], c * C:(c + 1) * C]

                def mm(out, lhsT, rhs, start=True, stop=True):
                    return pe.matmul(out, lhsT, rhs, start=start, stop=stop)

                pe.wait_ge(consts, N_CONSTS)
                with pe.Fori(0, PAIRS) as j:
                    pe.wait_ge(weights, j * 160 + 160)
                    pe.sem_inc(on_pe, 1)
                    with pe.Fori(0, NG) as gi:
                        n = j * NG + gi
                        pe.wait_ge(lora_ready, n + 1)
                        pe.sem_inc(on_pe, 1)
                        mm(PQ[0][:, 0, :], w_up_p[:, :], wd[:, :])
                        mm(PQ[0][:, 1, :], a_up_p[:, :], ad[:, :]).then_inc(lora_done, 1)
                        mm(PQ[1][:, 0, :], g_up_p[:, :], gd[:, :]).then_inc(g_done, 1)
                        pe.wait_ge(kk2_ready, n + 1)
                        pe.sem_inc(on_pe, 1)
                        mm(PQ[2][:, 0, :], head_ones[:, :], t2[:, :]).then_inc(norm_done, 1)
                        pe.wait_ge(rk_ready, n + 1)
                        pe.sem_inc(on_pe, 1)
                        mm(PQ[2][:, 1, :], head_ones[:, :], t2[:, :]).then_inc(bonus_done, 1)
                        pe.wait_ge(operands_ready, n + 1)
                        pe.sem_inc(on_pe, 1)
                        eyes = [ident[HS[h], HS[h]] for h in range(2)]
                        two_heads(lambda h, c: mm(place(PQ[0], 0, h, c), AR[HS[h], c, 0, :], eyes[h]))
                        two_heads(lambda h, c: mm(place(PQ[0], 1, h, c), at(b_h, h, c), eyes[h])).then_inc(turnedA_done, 1)
                        two_heads(lambda h, c: mm(place(PQ[1], 0, h, c), at(k_h, h, c), eyes[h]))
                        two_heads(lambda h, c: mm(place(PQ[1], 1, h, c), rkv[HS[h], 2, c * C:(c + 1) * C], eyes[h])).then_inc(turnedB_done, 1)
                        pe.wait_ge(bonus_ready, n + 1)
                        pe.sem_inc(on_pe, 1)

                        def score(bank_pair, left):
                            return two_heads(lambda h, c: mm(bank_pair[HS[h], c // HC, (c % HC) * 2 * C:(c % HC + 1) * 2 * C],
                                                             at(left, h, c), AR[HS[h], c, :, :]))

                        score(PQ[2], b_t).then_inc(scores1_done, 1)
                        score(PQ[3], k_t).then_inc(scores2_done, 1)
                        pe.wait_ge(tokA_ready, n + 1)
                        pe.sem_inc(on_pe, 1)
                        two_heads(lambda h, c: mm(place(PQ[0], 0, h, c), AR[HS[h], c, 0, :], at(b_t, h, c))).then_inc(A_done, 1)
                        pe.wait_ge(tokB_ready, n + 1)
                        pe.sem_inc(on_pe, 1)
                        for i in range(5):
                            pe.wait_ge(levels_ready, n * 5 + i + 1)
                            pe.sem_inc(on_pe, 1)
                            pe.wait_ge(X_ready, n * 6 + i + 1)
                            pe.sem_inc(on_pe, 1)
                            two_heads(lambda h, c: mm(place(PQ[1], 0, h, c), ATl[HS[h], i, c, :], XX[HS[h], 0, c, :])).then_inc(T_done, 1)
                            pe.wait_ge(T_ready, n * 5 + i + 1)
                            pe.sem_inc(on_pe, 1)
                            two_heads(lambda h, c: mm(place(PQ[0], 0, h, c), XX[HS[h], 1, c, :], T1[HS[h], c, :]))
                            two_heads(lambda h, c: mm(place(PQ[0], 1, h, c), T1[HS[h], c, :], XX[HS[h], 1, c, :])).then_inc(dX_done, 1)
                        pe.wait_ge(X_ready, n * 6 + 6)
                        pe.sem_inc(on_pe, 1)
                        pe.wait_ge(scores2_ready, n + 1)
                        pe.sem_inc(on_pe, 1)
                        two_heads(lambda h, c: mm(place(PQ[1], 0, h, c), tok[HS[h], 0, c, :], XX[HS[h], 1, c, :]))
                        two_heads(lambda h, c: mm(place(PQ[1], 1, h, c), SB2[HS[h], c, 0, :], tok[HS[h], 3, c, :])).then_inc(GW_done, 1)
                        pe.wait_ge(GW_ready, n + 1)
                        pe.sem_inc(on_pe, 1)
                        for c in range(NC):
                            cs = slice(c * C, (c + 1) * C)
                            for h in range(2):
                                mm(PQ[0][HS[h], h, cs], XX[HS[h], 1, c, :], GW[HS[h], 1, c, :], stop=False)
                            pe.wait_ge(S_ready, j * (NG * NC + 1) + gi * NC + c + 1)
                            pe.sem_inc(on_pe, 1)
                            for h in range(2):
                                last = mm(PQ[0][HS[h], h, cs], GW[HS[h], 0, c, :], S[HS[h], :], start=False)
                            last.then_inc(sa_done, 1)
                            for h in range(2):
                                mm(PQ[2][HS[h], h, cs], tok[HS[h], 3, c, :], SB2[HS[h], c, 1, :], stop=False)
                                mm(PQ[2][HS[h], h, cs], S[HS[h], :], AR[HS[h], c, 1, :], start=False, stop=False)
                                mm(PQ[3][HS[h], h, 0:C], tok[HS[h], 2, c, :], tok[HS[h], 3, c, :], stop=False)
                            pe.wait_ge(saA_ready, n * NC + c + 1)
                            pe.sem_inc(on_pe, 1)
                            pe.wait_ge(saB_ready, n * NC + c + 1)
                            pe.sem_inc(on_pe, 1)
                            for h in range(2):
                                last = mm(PQ[3][HS[h], h, 0:C], tok[HS[h], 1, c, :], SA[HS[h], :], start=False)
                            last.then_inc(dS_done, 1)
                            for h in range(2):
                                last = mm(PQ[2][HS[h], h, cs], SA[HS[h], :], SB1[HS[h], c, 1, :], start=False)
                        last.then_inc(y_done, 1)
                        pe.wait_ge(y_ready, n + 1)
                        pe.sem_inc(on_pe, 1)
                        mm(PQ[1][:, 0, :], head_ones[:, :], y[:, :]).then_inc(mean_done, 1)
                        pe.wait_ge(centred_ready, n + 1)
                        pe.sem_inc(on_pe, 1)
                        mm(PQ[1][:, 1, :], head_ones[:, :], t2[:, :]).then_inc(var_done, 1)


def mix_out_and_route(nc, program, E_all, ranks, gates, totals, x, w_out, norm2_gain, w_rg, w_re, mixT_dram, x1_dram, h2_dram):
    with ExitStack() as ctx:
        sb, pb, sem = makers(nc, ctx, program)
        NL = N_GROUPS + NE
        w_sb = sb("wo_sb", [P, KT, D])
        w_r = sb("w_r", [P, KT, NL])
        gain = sb("gain2", [P, D])
        mixT = sb("mixT_t", [P, 2, KT, P])
        x_t = sb("x_t5", [P, 2, D])
        h2 = sb("h2_t", [P, 2, D])
        h2T = sb("h2T", [P, KT, P])
        squares = sb("squares5", [P, D])
        ssum, root, rstd = [sb(n, [P, 1]) for n in ("ssum5", "root5", "rstd5")]
        eps = sb("eps5", [P, 1])
        ident = sb("ident5", [P, P])
        earlier = sb("earlier", [P, P])
        ones = sb("ones5", [P, P])
        iota_i = sb("iota_i", [P, NE], I32)
        iota = sb("iota_f", [P, NE])
        lg = sb("lg", [P, NL])
        gl8 = sb("gl8", [P, 8])
        gmax8, emax8 = sb("gmax8", [P, 8]), sb("emax8", [P, 8])
        gidx8, eidx8 = sb("gidx8", [P, 8], U32), sb("eidx8", [P, 8], U32)
        negmax, gidx, gidx_8, gsum, ggate = [sb(n, [P, 1]) for n in ("negmax", "gidx", "gidx_8", "gsum", "ggate")]
        gexp = sb("gexp", [P, N_GROUPS])
        onehot = sb("onehot", [P, N_GROUPS])
        sel = sb("sel", [P, N_GROUPS, PER_GROUP])
        in_group = sb("in_group", [P, PER_GROUP])
        lead, share, eidx, eid = [sb(n, [P, 2]) for n in ("lead", "share", "eidx", "eid")]
        E = sb("E", [P, 2, 2, NE])
        both = sb("both", [P, 2, NE])
        before = sb("before", [P, NE])
        picked = sb("picked", [P, 2, NE])
        o_ps = pb("o_ps5", [P, 2, 2, 512])
        hT_ps = pb("hT_ps5", [P, KT, P])
        lg_ps = pb("lg_ps", [P, 512])
        rank_ps = pb("rank_ps", [P, 512])

        names = """weights consts x1_ready rooted h2_ready turned hT_copied mixed logits_done routed_group
            gates_wanted exped shared picks_ready ranked ranks_ready counted""".split()
        (weights, consts, x1_ready, rooted, h2_ready, turned, hT_copied, mixed, logits_done, routed_group,
         gates_wanted, exped, shared, picks_ready, ranked, ranks_ready, counted) = [sem(f"p5_{n}") for n in names]
        loaded = [sem(f"p5_loaded{s}") for s in range(2)]
        stored = [sem(f"p5_stored{s}") for s in range(2)]
        on_sp, on_act, on_pe, on_dve, on_pool = program.gates_passed
        mixT_v = mixT_dram.rearrange("(k p) t -> p k t", p=P)
        give_credit(nc, hT_copied, routed_group, x1_ready, ranks_ready)
        with nc.Block() as block:
            @block.sync
            def _(sp):
                def load(t, s):
                    sp.dma_start(mixT[:, s, :, :], mixT_v[:, :, bass.ds(t * P, P)]).then_inc(loaded[s], 16)
                    sp.dma_start(x_t[:, s, :], x[0, bass.ds(t * P, P), :]).then_inc(loaded[s], 16)

                def store(t, s):
                    sp.wait_ge(h2_ready, t + 1)
                    sp.dma_start(x1_dram[bass.ds(t * P, P), :], x_t[:, s, :]).then_inc(stored[s], 16)
                    sp.dma_start(h2_dram[bass.ds(t * P, P), :], h2[:, s, :]).then_inc(stored[s], 16)

                load(0, 0)
                load(1, 1)
                sp.dma_start(w_sb[:, :, :], w_out[0].rearrange("(k p) c -> p k c", p=P)).then_inc(weights, 16)
                sp.dma_start(w_r[:, :, 0:N_GROUPS], w_rg[0].rearrange("(k p) c -> p k c", p=P)).then_inc(weights, 16)
                sp.dma_start(w_r[:, :, N_GROUPS:NL], w_re[0].rearrange("(k p) c -> p k c", p=P)).then_inc(weights, 16)
                sp.dma_start(gain[:, :], norm2_gain[0, :].partition_broadcast(P)).then_inc(weights, 16)
                with sp.Fori(0, NT // 2 - 1) as i:
                    for s in range(2):
                        t = i * 2 + s
                        store(t, s)
                        sp.wait_ge(stored[s], i * 32 + 32)
                        load(t + 2, s)
                for s in range(2):
                    store(NT - 2 + s, s)
                for s in range(2):
                    sp.wait_ge(stored[s], 16 * NT)

            @block.gpsimd
            def _(pool):
                identity(pool, ident[:, :])
                pool.memset(eps[:, :], NORM_EPS)
                pool.memset(ones[:, :], 1.0)
                pool.memset(earlier[:, :], 1.0)
                pool.memset(gl8[:, :], -3.4e38)
                pool.memset(before[:, :], 0.0)
                pool.iota(iota_i[:, :], pattern=[[1, NE]], base=0, channel_multiplier=0)
                pool.drain()
                pool.affine_select(out=earlier[:, :], in_=earlier[:, :], compare_op=ALU.is_gt, fill=0.0, base=0,
                                   pattern=[[1, P]], channel_multiplier=-1)
                pool.tensor_copy(iota[:, :], iota_i[:, :])
                pool.drain()
                pool.sem_inc(consts, 1)

            def tile_pairs(eng, one_tile):
                for s in range(2):
                    one_tile(s, s, 0, first=(s == 0), last=False)
                with eng.Fori(1, NT // 2 - 1) as i:
                    for s in range(2):
                        one_tile(i * 2 + s, s, i, first=False, last=False)
                for s in range(2):
                    one_tile(NT - 2 + s, s, NT // 2 - 1, first=False, last=(s == 1))

            @block.tensor
            def _(pe):
                def mix(t, s, n):
                    pe.wait_ge(loaded[s], n * 32 + 32)
                    pe.wait_ge(x1_ready, CREDIT + t - 1)
                    for half in range(2):
                        for k in range(KT):
                            done = pe.matmul(o_ps[:, s, half, :], mixT[:, s, k, :], w_sb[:, k, half * 512:(half + 1) * 512],
                                             start=(k == 0), stop=(k == KT - 1))
                    done.then_inc(mixed, 1)

                def rank(t, s):
                    pe.wait_ge(picks_ready, t + 1)
                    pe.wait_ge(ranks_ready, CREDIT + t)
                    pe.matmul(rank_ps[:, 0:NE], earlier[:, :], both[:, s, :], start=True, stop=False)
                    pe.matmul(rank_ps[:, 0:NE], ones[:, :], before[:, :], start=False, stop=True).then_inc(ranked, 1)

                def one_tile(t, s, n, first, last):
                    if not last:
                        mix(t + 1, 1 - s, n + s)
                    if not first:
                        rank(t - 1, 1 - s)
                    pe.wait_ge(h2_ready, t + 1)
                    pe.wait_ge(hT_copied, CREDIT + t)
                    for k in range(KT):
                        done = pe.transpose(hT_ps[:, k, :], h2[:, s, k * P:(k + 1) * P], ident[:, :])
                    done.then_inc(turned, 1)
                    pe.wait_ge(hT_copied, CREDIT + t + 1)
                    pe.wait_ge(routed_group, CREDIT + t)
                    for k in range(KT):
                        done = pe.matmul(lg_ps[:, 0:NL], h2T[:, k, :], w_r[:, k, :], start=(k == 0), stop=(k == KT - 1))
                    done.then_inc(logits_done, 1)

                pe.wait_ge(consts, 1)
                pe.wait_ge(weights, 64)
                mix(0, 0, 0)
                tile_pairs(pe, one_tile)
                rank(NT - 1, 1)
                pe.wait_ge(ranks_ready, CREDIT + NT)
                pe.matmul(rank_ps[:, 0:NE], ones[:, :], before[:, :], start=True, stop=True).then_inc(counted, 1)

            @block.scalar
            def _(act):
                act.wait_ge(consts, 1)
                with act.Fori(0, NT // 2) as i:
                    for s in range(2):
                        t = i * 2 + s
                        act.wait_ge(x1_ready, CREDIT + t + 1)
                        act.activation(squares[:, :], x_t[:, s, :], ACT.Square, accum_out=ssum[:, :])
                        act.drain()
                        act.activation(root[:, :], ssum[:, :], ACT.Sqrt, bias=eps[:, :], scale=1.0 / D).then_inc(rooted, 1)
                        act.wait_ge(turned, t + 1)
                        act.copy(h2T[:, :, :], hT_ps[:, :, :]).then_inc(hT_copied, 1)
                        act.wait_ge(routed_group, CREDIT + t + 1)
                        act.activation(gexp[:, :], gl8[:, 0:N_GROUPS], ACT.Exp, bias=negmax[:, :], accum_out=gsum[:, :])
                        act.drain()
                        act.sem_inc(exped, 1)
                        act.wait_ge(gates_wanted, t + 1)
                        act.activation(share[:, :], lead[:, :], ACT.Sigmoid).then_inc(shared, 1)

            @block.vector
            def _(dve):
                def finish(t, s):
                    dve.wait_ge(ranked, t + 1)
                    dve.tensor_tensor(picked[:, :, :], E[:, s, :, :], rank_ps[:, 0:NE].unsqueeze(1).to_broadcast([P, 2, NE]), ALU.mult)
                    dve.drain()
                    dve.reduce_sum(ranks[:, bass.ds(t * 2, 2)], picked[:, :, :], axis=AX_X)
                    dve.tensor_tensor(before[:, :], before[:, :], both[:, s, :], ALU.add).then_inc(ranks_ready, 1)
                    dve.drain()

                def one_tile(t, s, n, first, last):
                    dve.wait_ge(mixed, t + 1)
                    dve.tensor_tensor(x_t[:, s, :], x_t[:, s, :], o_ps[:, s, :, :].rearrange("p a b -> p (a b)"), ALU.add).then_inc(x1_ready, 1)
                    dve.wait_ge(rooted, t + 1)
                    dve.reciprocal(rstd[:, :], root[:, :])
                    dve.drain()
                    dve.scalar_tensor_tensor(h2[:, s, :], x_t[:, s, :], rstd[:, :], gain[:, :], ALU.mult, ALU.mult).then_inc(h2_ready, 1)
                    if not first:
                        finish(t - 1, 1 - s)
                    dve.wait_ge(logits_done, t + 1)
                    dve.tensor_copy(lg[:, :], lg_ps[:, 0:NL])
                    dve.tensor_copy(gl8[:, 0:N_GROUPS], lg_ps[:, 0:N_GROUPS])
                    dve.drain()
                    dve.max(gmax8[:, :], gl8[:, :])
                    dve.drain()
                    dve.max_index(gidx8[:, :], gmax8[:, :], gl8[:, :])
                    dve.tensor_scalar(negmax[:, :], gmax8[:, 0:1], -1.0, None, ALU.mult).then_inc(routed_group, 1)
                    dve.drain()
                    dve.tensor_copy(gidx[:, :], gidx8[:, 0:1])
                    dve.drain()
                    dve.tensor_scalar(onehot[:, :], iota[:, 0:N_GROUPS], gidx[:, :], None, ALU.is_equal)
                    dve.tensor_scalar(gidx_8[:, :], gidx[:, :], float(PER_GROUP), None, ALU.mult)
                    dve.drain()
                    dve.tensor_tensor(sel[:, :, :], lg[:, N_GROUPS:NL].rearrange("p (g e) -> p g e", g=N_GROUPS),
                                      onehot[:, :].unsqueeze(2).to_broadcast([P, N_GROUPS, PER_GROUP]), ALU.mult)
                    dve.drain()
                    dve.reduce_sum(in_group[:, :], sel[:, :, :].rearrange("p g e -> p e g"), axis=AX_X)
                    dve.drain()
                    dve.max(emax8[:, :], in_group[:, :])
                    dve.drain()
                    dve.max_index(eidx8[:, :], emax8[:, :], in_group[:, :])
                    dve.tensor_tensor(lead[:, 0:1], emax8[:, 0:1], emax8[:, 1:2], ALU.subtract)
                    dve.tensor_tensor(lead[:, 1:2], emax8[:, 1:2], emax8[:, 0:1], ALU.subtract).then_inc(gates_wanted, 1)
                    dve.drain()
                    dve.tensor_copy(eidx[:, :], eidx8[:, 0:2])
                    dve.drain()
                    dve.tensor_scalar(eid[:, :], eidx[:, :], gidx_8[:, :], None, ALU.add)
                    dve.drain()
                    dve.tensor_tensor(E[:, s, :, :], iota[:, :].unsqueeze(1).to_broadcast([P, 2, NE]),
                                      eid[:, :].unsqueeze(2).to_broadcast([P, 2, NE]), ALU.is_equal)
                    dve.drain()
                    dve.tensor_tensor(both[:, s, :], E[:, s, 0, :], E[:, s, 1, :], ALU.add).then_inc(picks_ready, 1)
                    dve.tensor_copy(E_all[:, bass.ds(t * 2, 2), :], E[:, s, :, :])
                    dve.wait_ge(exped, t + 1)
                    dve.reciprocal(ggate[:, :], gsum[:, :])
                    dve.drain()
                    dve.wait_ge(shared, t + 1)
                    dve.tensor_scalar(gates[:, bass.ds(t * 2, 2)], share[:, :], ggate[:, :], None, ALU.mult)

                dve.wait_ge(consts, 1)
                dve.wait_ge(weights, 64)
                tile_pairs(dve, one_tile)
                finish(NT - 1, 1)
                dve.wait_ge(counted, 1)
                dve.tensor_copy(totals[:, :], rank_ps[:, 0:NE])
                dve.drain()


def place_slots(nc, program, E_all, ranks, totals, n_blocks, first_block, row_slot):
    with ExitStack() as ctx:
        sb, pb, sem = makers(nc, ctx, program)
        up = sb("up", [P, NE])
        blocks_i = sb("blocks_i", [P, NE], I32)
        blocks, ends, starts = [sb(n, [P, NE]) for n in ("blocks", "ends", "starts")]
        rows_of = sb("rows_of", [P, 2 * NT, NE])
        row = sb("row", [P, 2 * NT])
        row_i, block_i, part_i = [sb(n, [P, 2 * NT], I32) for n in ("row_i", "block_i", "part_i")]
        block_f, part_f = [sb(n, [P, 2 * NT]) for n in ("block_f", "part_f")]
        cell = sb("cell", [P, 2 * NT], U32)
        ones = sb("ones6", [P, NE])
        slot = sb("slot", [P, NT, 2], I32)
        spare = sb("spare", [P, TABLE], I32)
        consts, placed, cleared, scattered, begun = [sem(f"p6_{n}") for n in ("consts", "placed", "cleared", "scattered", "begun")]
        with nc.Block() as block:
            @block.gpsimd
            def _(pool):
                pool.memset(ones[:, :], 1.0)
                pool.iota(spare[:, :], pattern=[[1, TABLE]], base=2 * SEQ, channel_multiplier=TABLE)
                pool.iota(slot[:, :, :], pattern=[[2 * P, NT], [1, 2]], base=0, channel_multiplier=2)
                pool.drain()
                pool.sem_inc(consts, 1)
                pool.wait_ge(cleared, 16)
                pool.wait_ge(placed, 1)
                for t in range(NT):
                    for k in range(2):
                        col = 2 * t + k
                        pool.indirect_dma_start(out=row_slot[:, :], out_offset=bass.IndirectOffsetOnAxis(ap=cell[:, col:col + 1], axis=0),
                                                in_=slot[:, t, k:k + 1], in_offset=None).then_inc(scattered, 16)
                pool.wait_ge(scattered, 16 * 2 * NT)

            @block.sync
            def _(sp):
                sp.wait_ge(consts, 1)
                sp.dma_start(row_slot.rearrange("(p c) o -> p (c o)", p=P), spare[:, :]).then_inc(cleared, 16)

            @block.vector
            def _(dve):
                dve.wait_ge(consts, 1)
                dve.tensor_scalar(up[:, :], totals[:, :], float(P - 1), None, ALU.add)
                dve.drain()
                dve.tensor_copy(blocks_i[:, :], up[:, :])
                dve.drain()
                dve.tensor_scalar(blocks_i[:, :], blocks_i[:, :], P.bit_length() - 1, None, ALU.arith_shift_right)
                dve.drain()
                dve.tensor_copy(blocks[:, :], blocks_i[:, :])
                dve.drain()
                dve.tensor_scalar(blocks[:, :], blocks[:, :], 1.0, None, ALU.max)
                dve.drain()
                dve.tensor_tensor_scan(ends[:, :], ones[:, :], blocks[:, :], 0.0, ALU.mult, ALU.add)
                dve.drain()
                dve.tensor_tensor(starts[:, :], ends[:, :], blocks[:, :], ALU.subtract)
                dve.tensor_copy(n_blocks[:, :], blocks[:, :])
                dve.drain()
                dve.tensor_copy(first_block[:, :], starts[:, :])
                dve.tensor_scalar(starts[:, :], starts[:, :], float(P), None, ALU.mult)
                dve.drain()
                dve.tensor_tensor(rows_of[:, :, :], E_all[:, :, :], starts[:, :].unsqueeze(1).to_broadcast([P, 2 * NT, NE]), ALU.mult)
                dve.drain()
                dve.reduce_sum(row[:, :], rows_of[:, :, :], axis=AX_X)
                dve.drain()
                dve.tensor_tensor(row[:, :], row[:, :], ranks[:, :], ALU.add)
                dve.drain()
                dve.tensor_copy(row_i[:, :], row[:, :])
                dve.drain()
                dve.tensor_scalar(block_i[:, :], row_i[:, :], P.bit_length() - 1, None, ALU.arith_shift_right)
                dve.tensor_scalar(part_i[:, :], row_i[:, :], P - 1, None, ALU.bitwise_and)
                dve.drain()
                dve.tensor_copy(block_f[:, :], block_i[:, :])
                dve.tensor_copy(part_f[:, :], part_i[:, :])
                dve.drain()
                dve.scalar_tensor_tensor(row[:, :], part_f[:, :], float(TABLE), block_f[:, :], ALU.mult, ALU.add)
                dve.drain()
                dve.tensor_copy(cell[:, :], row[:, :])
                dve.drain()
                dve.sem_inc(placed, 1)


def run_experts(nc, program, n_blocks, first_block, row_slot, w_g, w_u, w_d, h2_dram, y_dram):
    with ExitStack() as ctx:
        sb, pb, sem = makers(nc, ctx, program)
        FT = FF // P
        wg = sb("wg", [P, 2, KT, FF])
        wu = sb("wu", [P, 2, KT, FF])
        wd = sb("wd7", [P, 2, FT, D])
        slot_all = sb("slot_all", [P, TABLE], I32)
        tok_all = sb("tok_all", [P, TABLE], I32)
        tok = sb("tok7", [P, 1], I32)
        slot = sb("slot7", [P, 1], I32)
        xg = sb("xg", [P, D])
        xT = sb("xT", [P, KT, P])
        sil = sb("sil", [P, FF])
        h = sb("h7", [P, FF])
        hT = sb("hT7", [P, FT, P])
        y = sb("y7", [P, D])
        ident = sb("ident7", [P, P])
        xT_ps = pb("xT_ps7", [P, KT, P])
        g_ps = pb("g_ps7", [P, FF])
        u_ps = pb("u_ps7", [P, FF])
        hT_ps = pb("hT_ps7", [P, FT, P])
        y_ps = pb("y_ps7", [P, D])
        names = """consts slots_loaded tok_ready gathered turned xT_ready g_done u_done silu_ready h_ready h_turned hT_ready
            y_done y_copied expert_done stored y_free""".split()
        (consts, slots_loaded, tok_ready, gathered, turned, xT_ready, g_done, u_done, silu_ready, h_ready, h_turned, hT_ready,
         y_done, y_copied, expert_done, stored, y_free) = [sem(f"p7_{n}") for n in names]
        gu_loaded = [sem(f"p7_gu_loaded{s}") for s in range(2)]
        d_loaded = [sem(f"p7_d_loaded{s}") for s in range(2)]
        on_sp, on_act, on_pe, on_dve, on_pool = program.gates_passed

        def blocks_of(eng, e):
            count = eng.value_load(n_blocks[0:1, bass.ds(e, 1)], min_val=1, max_val=SEQ // P)
            start = eng.value_load(first_block[0:1, bass.ds(e, 1)], min_val=0, max_val=MAX_BLOCKS - 1)
            return count, start

        give_credit(nc, h_ready, h_turned, silu_ready, y_free, y_copied)
        with nc.Block() as block:
            @block.sync
            def _(sp):
                def load(e, s):
                    for dst, src in ((wg, w_g), (wu, w_u)):
                        sp.dma_start(dst[:, s, :, :], src[0, bass.ds(e, 1), :, :].rearrange("o (p k) f -> p (o k) f", p=P)).then_inc(gu_loaded[s], 16)
                    sp.dma_start(wd[:, s, :, :], w_d[0, bass.ds(e, 1), :, :].rearrange("o (p k) f -> p (o k) f", p=P)).then_inc(d_loaded[s], 16)

                sp.dma_start(slot_all[:, :], row_slot.rearrange("(p b) o -> p (b o)", p=P)).then_inc(slots_loaded, 16)
                def pass_stores(e):
                    count, start = blocks_of(sp, e)
                    with sp.Fori(0, count) as i:
                        sp.wait_ge(stored, (start + i) * 16 + 16)
                        sp.sem_inc(y_free, 1)

                load(0, 0)
                load(1, 1)
                with sp.Fori(0, NE // 2 - 1) as i2:
                    for s in range(2):
                        e = i2 * 2 + s
                        pass_stores(e)
                        sp.wait_ge(expert_done, e + 1)
                        load(e + 2, s)
                for e in (NE - 2, NE - 1):
                    pass_stores(e)

            @block.gpsimd
            def _(pool):
                identity(pool, ident[:, :])
                pool.drain()
                pool.sem_inc(consts, 1)
                pool.wait_ge(tok_ready, 1)

                def gather(b):
                    pool.tensor_copy(tok[:, :], tok_all[:, bass.ds(b, 1)])
                    pool.drain()
                    pool.indirect_dma_start(out=xg[:, :], out_offset=None, in_=h2_dram[:, :],
                                            in_offset=bass.IndirectOffsetOnAxis(ap=tok[:, 0:1], axis=0)).then_inc(gathered, 16)

                gather(0)
                pool.wait_ge(turned, 1)
                gather(1)
                with pool.Fori(0, NE) as e:
                    count, start = blocks_of(pool, e)
                    with pool.Fori(0, count) as i:
                        b = start + i
                        pool.wait_ge(turned, b + 2)
                        pool.sem_inc(on_pool, 1)
                        gather(b + 2)
                        pool.wait_ge(y_free, CREDIT + b)
                        pool.sem_inc(on_pool, 1)
                        pool.tensor_copy(slot[:, :], slot_all[:, bass.ds(b, 1)])
                        pool.drain()
                        pool.wait_ge(y_copied, CREDIT + b * 2 + 2)
                        pool.sem_inc(on_pool, 1)
                        pool.indirect_dma_start(out=y_dram[:, :], out_offset=bass.IndirectOffsetOnAxis(ap=slot[:, 0:1], axis=0),
                                                in_=y[:, :], in_offset=None).then_inc(stored, 16)
                pool.drain()

            @block.tensor
            def _(pe):
                def turn(b):
                    pe.wait_ge(gathered, b * 16 + 16)
                    for k in range(KT):
                        last = pe.transpose(xT_ps[:, k, :], xg[:, :].rearrange("t (p k) -> t k p", k=KT)[:, k, :], ident[:, :])
                    last.then_inc(turned, 1)

                def one_block(b, s):
                    pe.wait_ge(xT_ready, b * 2 + 2)
                    pe.wait_ge(silu_ready, CREDIT + b)
                    for k in range(KT):
                        last = pe.matmul(g_ps[:, :], xT[:, k, :], wg[:, s, k, :], start=(k == 0), stop=(k == KT - 1))
                    last.then_inc(g_done, 1)
                    pe.wait_ge(h_ready, CREDIT + b)
                    for k in range(KT):
                        last = pe.matmul(u_ps[:, :], xT[:, k, :], wu[:, s, k, :], start=(k == 0), stop=(k == KT - 1))
                    last.then_inc(u_done, 1)
                    turn(b + 1)
                    pe.wait_ge(h_ready, CREDIT + b + 1)
                    for f in range(FT):
                        last = pe.transpose(hT_ps[:, f, :], h[:, :].rearrange("t (p f) -> t f p", f=FT)[:, f, :], ident[:, :])
                    last.then_inc(h_turned, 1)
                    pe.wait_ge(hT_ready, b + 1)
                    pe.wait_ge(y_copied, CREDIT + b * 2)
                    for half in range(2):
                        for f in range(FT):
                            last = pe.matmul(y_ps[:, half * 512:(half + 1) * 512], hT[:, f, :], wd[:, s, f, half * 512:(half + 1) * 512],
                                             start=(f == 0), stop=(f == FT - 1))
                        last.then_inc(y_done, 1)

                pe.wait_ge(consts, 1)
                turn(0)
                with pe.Fori(0, NE // 2) as i2:
                    for s in range(2):
                        e = i2 * 2 + s
                        count, start = blocks_of(pe, e)
                        pe.wait_ge(gu_loaded[s], i2 * 32 + 32)
                        pe.wait_ge(d_loaded[s], i2 * 16 + 16)
                        pe.sem_inc(on_pe, 1)
                        with pe.Fori(0, count) as i:
                            one_block(start + i, s)
                        pe.drain()
                        pe.sem_inc(expert_done, 1)

            @block.scalar
            def _(act):
                def copy_xT(b):
                    act.wait_ge(turned, b + 1)
                    act.copy(xT[:, 0:KT // 2, :], xT_ps[:, 0:KT // 2, :]).then_inc(xT_ready, 1)

                copy_xT(0)
                with act.Fori(0, NE) as e:
                    count, start = blocks_of(act, e)
                    with act.Fori(0, count) as i:
                        b = start + i
                        act.wait_ge(g_done, b + 1)
                        act.wait_ge(h_ready, CREDIT + b)
                        act.activation(sil[:, :], g_ps[:, :], ACT.Silu).then_inc(silu_ready, 1)
                        act.wait_ge(u_done, b + 1)
                        copy_xT(b + 1)
                        act.wait_ge(h_turned, CREDIT + b + 1)
                        act.copy(hT[:, :, :], hT_ps[:, :, :]).then_inc(hT_ready, 1)
                        act.wait_ge(y_done, b * 2 + 1)
                        act.wait_ge(y_free, CREDIT + b)
                        act.copy(y[:, 0:512], y_ps[:, 0:512]).then_inc(y_copied, 1)

            @block.vector
            def _(dve):
                def copy_xT(b):
                    dve.wait_ge(turned, b + 1)
                    dve.tensor_copy(xT[:, KT // 2:KT, :], xT_ps[:, KT // 2:KT, :]).then_inc(xT_ready, 1)

                dve.wait_ge(slots_loaded, 16)
                dve.tensor_scalar(tok_all[:, :], slot_all[:, :], 2 * SEQ - 1, None, ALU.min)
                dve.drain()
                dve.tensor_scalar(tok_all[:, :], tok_all[:, :], 1, None, ALU.arith_shift_right).then_inc(tok_ready, 1)
                copy_xT(0)
                with dve.Fori(0, NE) as e:
                    count, start = blocks_of(dve, e)
                    with dve.Fori(0, count) as i:
                        b = start + i
                        dve.wait_ge(u_done, b + 1)
                        dve.wait_ge(silu_ready, CREDIT + b + 1)
                        dve.wait_ge(h_turned, CREDIT + b)
                        dve.tensor_tensor(h[:, :], sil[:, :], u_ps[:, :], ALU.mult).then_inc(h_ready, 1)
                        copy_xT(b + 1)
                        dve.wait_ge(y_done, b * 2 + 2)
                        dve.wait_ge(y_free, CREDIT + b)
                        dve.tensor_copy(y[:, 512:1024], y_ps[:, 512:1024]).then_inc(y_copied, 1)


def combine(nc, program, gates, x1_dram, y_dram, out):
    with ExitStack() as ctx:
        sb, pb, sem = makers(nc, ctx, program)
        rows = sb("rows8", [P, 2, 2, D])
        x1 = sb("x1_8", [P, 2, D])
        gate_t = sb("gate_t", [P, 2, 2])
        loaded = [sem(f"p8_loaded{s}") for s in range(2)]
        stored = [sem(f"p8_stored{s}") for s in range(2)]
        summed = sem("p8_summed")
        on_sp, on_act, on_pe, on_dve, on_pool = program.gates_passed
        y_tiles = y_dram[0:2 * SEQ, :].rearrange("(t k) d -> t (k d)", k=2)
        with nc.Block() as block:
            @block.sync
            def _(sp):
                def load(t, s):
                    sp.dma_start(x1[:, s, :], x1_dram[bass.ds(t * P, P), :]).then_inc(loaded[s], 16)
                    sp.dma_start(rows[:, s, :, :].rearrange("p k d -> p (k d)"), y_tiles[bass.ds(t * P, P), :]).then_inc(loaded[s], 16)

                def store(t, s):
                    sp.wait_ge(summed, t + 1)
                    sp.dma_start(out[0, bass.ds(t * P, P), :], x1[:, s, :]).then_inc(stored[s], 16)

                load(0, 0)
                load(1, 1)
                with sp.Fori(0, NT // 2 - 1) as i:
                    for s in range(2):
                        t = i * 2 + s
                        store(t, s)
                        sp.wait_ge(stored[s], i * 16 + 16)
                        load(t + 2, s)
                for s in range(2):
                    store(NT - 2 + s, s)
                for s in range(2):
                    sp.wait_ge(stored[s], 8 * NT)

            @block.vector
            def _(dve):
                with dve.Fori(0, NT // 2) as i:
                    for s in range(2):
                        t = i * 2 + s
                        dve.tensor_copy(gate_t[:, s, :], gates[:, bass.ds(t * 2, 2)])
                        dve.drain()
                        dve.wait_ge(loaded[s], i * 32 + 32)
                        dve.scalar_tensor_tensor(rows[:, s, 0, :], rows[:, s, 0, :], gate_t[:, s, 0:1], x1[:, s, :], ALU.mult, ALU.add)
                        dve.drain()
                        dve.scalar_tensor_tensor(x1[:, s, :], rows[:, s, 1, :], gate_t[:, s, 1:2], rows[:, s, 0, :], ALU.mult, ALU.add).then_inc(summed, 1)


def hybrid_block(nc, x, norm1_gain, w_in, sb_q_gain, sb_k_gain, rw_shift_mu, rw_w0, rw_w_up, rw_a0, rw_a_up, rw_g_up,
                 rw_k_k, rw_k_a, rw_r_k, rw_ln_w, rw_ln_b, w_out, norm2_gain, w_router_group, w_router_expert,
                 w_exp_gate, w_exp_up, w_exp_down, out):
    def dram(name, shape, dt=F32):
        return nc.dram_tensor(name, shape, dt, kind="Internal").ap()

    qT, kT, v = dram("qT", (SBW, SEQ)), dram("kT", (SBW, SEQ)), dram("v", (SEQ, SBW))
    pT = dram("pT", (RW_COLS, SEQ))
    mixT = dram("mixT", (D, SEQ))
    x1, h2 = dram("x1", (SEQ, D)), dram("h2", (SEQ, D))
    row_slot = dram("row_slot", (TABLE * P, 1), I32)
    y = dram("y", (2 * SEQ + TABLE * P, D))
    with ExitStack() as stack:
        program = Program(nc, stack)
        with nc.sbuf_tensor("h_all", [P, KT, SEQ], F32) as h_all:
            project_tokens(nc, program, h_all, x, norm1_gain, w_in, sb_q_gain, sb_k_gain, qT, kT, v)
            project_channels(nc, program, h_all, w_in, rw_shift_mu, pT)
        stick_breaking(nc, program, qT, kT, v, mixT)
        time_mixing(nc, program, rw_w0, rw_w_up, rw_a0, rw_a_up, rw_g_up, rw_k_k, rw_k_a, rw_r_k, rw_ln_w, rw_ln_b, pT, mixT)
        with ExitStack() as ctx:
            sb, _, _ = makers(nc, ctx, program)
            gates = sb("gates", [P, 2 * NT])
            n_blocks, first_block = sb("n_blocks", [P, NE], I32), sb("first_block", [P, NE], I32)
            with ExitStack() as routing:
                sb, _, _ = makers(nc, routing, program)
                E_all, ranks, totals = sb("E_all", [P, 2 * NT, NE]), sb("ranks", [P, 2 * NT]), sb("totals", [P, NE])
                mix_out_and_route(nc, program, E_all, ranks, gates, totals, x, w_out, norm2_gain, w_router_group, w_router_expert, mixT, x1, h2)
                place_slots(nc, program, E_all, ranks, totals, n_blocks, first_block, row_slot)
            run_experts(nc, program, n_blocks, first_block, row_slot, w_exp_gate, w_exp_up, w_exp_down, h2, y)
            combine(nc, program, gates, x1, y, out)


_INPUTS = ("x norm1_gain w_in sb_q_gain sb_k_gain rw_shift_mu rw_w0 rw_w_up rw_a0 rw_a_up rw_g_up rw_k_k rw_k_a rw_r_k "
           "rw_ln_w rw_ln_b w_out norm2_gain w_router_group w_router_expert w_exp_gate w_exp_up w_exp_down").split()


def kernel(**inputs):
    import concourse.bacc as bacc
    import numpy as np
    from concourse.bass_utils import run_bass_kernel_spmd

    nc = bacc.Bacc("TRN2", target_bir_lowering=False, num_devices=1)
    arrays, aps = {}, []
    for name in _INPUTS:
        a = np.ascontiguousarray(inputs[name])
        arrays[f"in_{name}"] = a
        aps.append(nc.dram_tensor(f"in_{name}", a.shape, mybir.dt.from_np(a.dtype), kind="ExternalInput").ap())
    out = nc.dram_tensor("out", (1, SEQ, D), F32, kind="ExternalOutput").ap()
    hybrid_block(nc, *aps, out)
    r = run_bass_kernel_spmd(nc, [arrays], core_ids=[0])
    return r.results[0]["out"]
```

```python
from contextlib import ExitStack

import concourse.bass as bass
from concourse import mybir

F32 = mybir.dt.float32
I32 = mybir.dt.int32
U32 = mybir.dt.uint32
ALU = mybir.AluOpType
ACT = mybir.ActivationFunctionType
AX_X = mybir.AxisListType.X

P = 128
SEQ, D = 2048, 1024
NT = SEQ // P
KT = D // P
HD = 64
SBW = D // 2
SB_COLS = 3 * SBW
LW, LA, LG = 32, 32, 96
RW_COLS = 3 * SBW + LW + LA + LG
IN_COLS = SB_COLS + RW_COLS
PAIRS = SBW // P
N_GROUPS, PER_GROUP = 4, 8
NE = N_GROUPS * PER_GROUP
FF = 512
MAX_BLOCKS = 2 * SEQ // P + NE
TABLE = MAX_BLOCKS + SEQ // P + 1
NORM_EPS, LN_X_EPS = 1e-6, 64e-5
EXP_HALF = 0.6065306597126334


class Program:

    def __init__(self, nc, stack):
        self.stack = stack
        self.gates_passed = [stack.enter_context(nc.semaphore(f"gates_passed_{e}")) for e in "sp act pe dve pool".split()]


CREDIT = 16


def give_credit(nc, *semaphores):
    with nc.Block() as block:
        @block.sync
        def _(sp):
            for s in semaphores:
                sp.sem_inc(s, CREDIT)


def makers(nc, ctx, program):
    def sb(name, shape, dt=F32):
        return ctx.enter_context(nc.sbuf_tensor(name, shape, dt))

    def pb(name, shape):
        return ctx.enter_context(nc.psum_tensor(name, shape, F32))

    def sem(name):
        return program.stack.enter_context(nc.semaphore(name))

    return sb, pb, sem


def identity(pool, tile):
    pool.memset(tile, 0.0)
    pool.drain()
    return pool.affine_select(out=tile, in_=tile, compare_op=ALU.not_equal, fill=1.0, base=0,
                              pattern=[[-1, P]], channel_multiplier=1)


def project_tokens(nc, program, h_all, x, norm1_gain, w_in, sb_q_gain, sb_k_gain, qT_dram, kT_dram, v_dram):
    with ExitStack() as ctx:
        sb, pb, sem = makers(nc, ctx, program)
        w_sb = sb("w_sb", [P, KT, SB_COLS])
        x_t = sb("x_t", [P, 2, D])
        squares = sb("squares", [P, D])
        hT = sb("hT", [P, 2, KT, P])
        gain = sb("gain", [P, KT])
        qkv = sb("qkv", [P, 2, 3, SBW])
        qk_sq = sb("qk_sq", [P, 2 * SBW])
        qkT = sb("qkT", [P, 8, P])
        qk_gain = sb("qk_gain", [P, 2, HD])
        ssum = sb("ssum", [P, 1])
        root = sb("root", [P, 1])
        rstd = sb("rstd", [P, 1])
        qk_sum = sb("qk_sum", [P, 16])
        qk_root = sb("qk_root", [P, 16])
        qk_rstd = sb("qk_rstd", [P, 16])
        eps = sb("eps", [P, 1])
        ident = sb("ident", [P, P])
        xT_ps = pb("xT_ps", [P, KT, P])
        qkv_ps = pb("qkv_ps", [P, 3, SBW])
        qkT_ps = pb("qkT_ps", [P, 8, P])

        consts = sem("p1_consts")
        weights = sem("p1_weights")
        x_loaded = [sem(f"p1_x_loaded{s}") for s in range(2)]
        rooted = sem("p1_rooted")
        scaled = sem("p1_scaled")
        x_turned = sem("p1_x_turned")
        h_ready = sem("p1_h_ready")
        h_kept = sem("p1_h_kept")
        projected = sem("p1_projected")
        qkv_copied = sem("p1_qkv_copied")
        qk_summed = sem("p1_qk_summed")
        qk_rooted = sem("p1_qk_rooted")
        qk_ready = sem("p1_qk_ready")
        qk_turned = sem("p1_qk_turned")
        qkT_ready = sem("p1_qkT_ready")
        stored = sem("p1_stored")
        on_sp, on_act, on_pe, on_dve, on_pool = program.gates_passed
        qT_v = qT_dram.rearrange("(c p) t -> p c t", p=P)
        kT_v = kT_dram.rearrange("(c p) t -> p c t", p=P)
        give_credit(nc, h_ready, qkT_ready, qk_turned, qkv_copied, scaled, stored)
        with nc.Block() as block:
            @block.sync
            def _(sp):
                def load(t, s):
                    sp.dma_start(x_t[:, s, :], x[0, bass.ds(t * P, P), :]).then_inc(x_loaded[s], 16)

                def store(t, s):
                    sp.wait_ge(qkT_ready, CREDIT + t * 2 + 2)
                    sp.dma_start(qT_v[:, :, bass.ds(t * P, P)], qkT[:, 0:4, :]).then_inc(stored, 16)
                    sp.dma_start(kT_v[:, :, bass.ds(t * P, P)], qkT[:, 4:8, :]).then_inc(stored, 16)
                    sp.dma_start(v_dram[bass.ds(t * P, P), :], qkv[:, s, 2, :]).then_inc(stored, 16)

                with nc.allow_non_contiguous_dma("a small vector, once"):
                    sp.dma_start(gain[:, :], norm1_gain[0, :].rearrange("(k p) -> p k", p=P)).then_inc(weights, 16)
                sp.dma_start(qk_gain[:, 0, :], sb_q_gain[0, :].partition_broadcast(P)).then_inc(weights, 16)
                sp.dma_start(qk_gain[:, 1, :], sb_k_gain[0, :].partition_broadcast(P)).then_inc(weights, 16)
                load(0, 0)
                load(1, 1)
                for k in range(KT):
                    sp.dma_start(w_sb[:, k, :], w_in[0, k * P:(k + 1) * P, 0:SB_COLS]).then_inc(weights, 16)
                with sp.Fori(0, NT // 2 - 1) as i:
                    for s in range(2):
                        t = i * 2 + s
                        sp.wait_ge(x_turned, t + 1)
                        load(t + 2, s)
                        store(t, s)
                for t in (NT - 2, NT - 1):
                    store(t, t % 2)
                sp.wait_ge(stored, CREDIT + NT * 48)

            @block.gpsimd
            def _(pool):
                pool.memset(eps[:, :], NORM_EPS)
                identity(pool, ident[:, :]).then_inc(consts, 1)
                pool.drain()
                pool.sem_inc(consts, 1)
                with pool.Fori(0, NT // 2) as i:
                    for s in range(2):
                        t = i * 2 + s
                        pool.wait_ge(h_ready, CREDIT + t * 2 + 2)
                        pool.sem_inc(on_pool, 1)
                        pool.tensor_copy(h_all[:, :, bass.ds(t * P, P)], hT[:, s, :, :]).then_inc(h_kept, 1)

            def tile_pairs(eng, one_tile):
                for s in range(2):
                    one_tile(s, s, first=(s == 0), last=False)
                with eng.Fori(1, NT // 2 - 1) as i:
                    for s in range(2):
                        one_tile(i * 2 + s, s, first=False, last=False)
                for s in range(2):
                    one_tile(NT - 2 + s, s, first=False, last=(s == 1))

            @block.scalar
            def _(act):
                def norm(t, s, n):
                    act.wait_ge(scaled, CREDIT + t)
                    act.wait_ge(x_loaded[s], n * 16 + 16)
                    act.activation(squares[:, :], x_t[:, s, :], ACT.Square, accum_out=ssum[:, :])
                    act.drain()
                    act.activation(root[:, :], ssum[:, :], ACT.Sqrt, bias=eps[:, :], scale=1.0 / D).then_inc(rooted, 1)

                def copy_turned(t):
                    act.wait_ge(qk_turned, CREDIT + t + 1)
                    act.wait_ge(stored, CREDIT + t * 48)
                    for half in range(2):
                        act.copy(qkT[:, 4 * half:4 * half + 4, :], qkT_ps[:, 4 * half:4 * half + 4, :]).then_inc(qkT_ready, 1)

                def one_tile(t, s, first, last):
                    for part in range(3):
                        if part == 0:
                            act.wait_ge(qk_turned, CREDIT + t - 1)
                        if part == 2 and not first:
                            copy_turned(t - 1)
                        if part == 2 and not first:
                            act.wait_ge(stored, CREDIT + (t - 1) * 48)
                        act.wait_ge(projected, t * 3 + part + 1)
                        act.copy(qkv[:, s, part, :], qkv_ps[:, part, :]).then_inc(qkv_copied, 1)
                    act.wait_ge(qk_summed, t + 1)
                    act.activation(qk_root[:, :], qk_sum[:, :], ACT.Sqrt, bias=eps[:, :], scale=1.0 / HD).then_inc(qk_rooted, 1)

                act.wait_ge(consts, 2)
                norm(0, 0, 0)
                norm(1, 1, 0)
                for s in range(2):
                    one_tile(s, s, first=(s == 0), last=False)
                    norm(s + 2, s, 1)
                with act.Fori(1, NT // 2 - 1) as i:
                    for s in range(2):
                        one_tile(i * 2 + s, s, first=False, last=False)
                        norm(i * 2 + s + 2, s, i + 1)
                for s in range(2):
                    one_tile(NT - 2 + s, s, first=False, last=False)
                copy_turned(NT - 1)

            @block.vector
            def _(dve):
                def scale_x(t, s):
                    dve.wait_ge(rooted, t + 1)
                    dve.reciprocal(rstd[:, :], root[:, :])
                    dve.drain()
                    dve.tensor_scalar(x_t[:, s, :], x_t[:, s, :], rstd[:, :], None, ALU.mult).then_inc(scaled, 1)

                def keep_h(t, s):
                    dve.wait_ge(x_turned, t + 1)
                    dve.wait_ge(h_kept, t + 1)
                    for half in range(2):
                        ks = slice(4 * half, 4 * half + 4)
                        dve.tensor_tensor(hT[:, s, ks, :], xT_ps[:, ks, :],
                                          gain[:, ks].unsqueeze(2).to_broadcast([P, 4, P]), ALU.mult).then_inc(h_ready, 1)

                def one_tile(t, s, first, last):
                    if not last:
                        keep_h(t + 1, 1 - s)
                    heads = qkv[:, s, 0:2, :].rearrange("p a (h d) -> p (a h) d", d=HD)
                    dve.wait_ge(qkv_copied, CREDIT + t * 3 + 2)
                    dve.tensor_tensor(qk_sq[:, :], qkv[:, s, 0:2, :], qkv[:, s, 0:2, :], ALU.mult)
                    dve.drain()
                    dve.reduce_sum(qk_sum[:, :], qk_sq[:, :].rearrange("p (h d) -> p h d", d=HD), axis=AX_X).then_inc(qk_summed, 1)
                    dve.wait_ge(qk_rooted, t + 1)
                    dve.reciprocal(qk_rstd[:, :], qk_root[:, :])
                    dve.drain()
                    dve.tensor_tensor(heads, heads, qk_rstd[:, :].unsqueeze(2).to_broadcast([P, 16, HD]), ALU.mult)
                    dve.drain()
                    for a in range(2):
                        part = qkv[:, s, a, :].rearrange("p (h d) -> p h d", d=HD)
                        done = dve.tensor_tensor(part, part, qk_gain[:, a, :].unsqueeze(1).to_broadcast([P, 8, HD]), ALU.mult)
                    done.then_inc(qk_ready, 1)
                    if not (isinstance(t, int) and t + 2 >= NT):
                        scale_x(t + 2, s)

                dve.sem_inc(h_kept, 2)
                dve.wait_ge(weights, 16 * (3 + KT))
                scale_x(0, 0)
                dve.wait_ge(x_turned, 1)
                for half in range(2):
                    ks = slice(4 * half, 4 * half + 4)
                    dve.tensor_tensor(hT[:, 0, ks, :], xT_ps[:, ks, :],
                                      gain[:, ks].unsqueeze(2).to_broadcast([P, 4, P]), ALU.mult).then_inc(h_ready, 1)
                scale_x(1, 1)
                tile_pairs(dve, one_tile)

            @block.tensor
            def _(pe):
                def turn_x(t, s):
                    pe.wait_ge(scaled, CREDIT + t + 1)
                    pe.wait_ge(h_ready, CREDIT + t * 2)
                    for k in range(KT):
                        done = pe.transpose(xT_ps[:, k, :], x_t[:, s, k * P:(k + 1) * P], ident[:, :])
                    done.then_inc(x_turned, 1)

                def turn_qk(t, s):
                    pe.wait_ge(qk_ready, t + 1)
                    pe.wait_ge(qkT_ready, CREDIT + t * 2)
                    for c in range(8):
                        done = pe.transpose(qkT_ps[:, c, :], qkv[:, s, c // 4, (c % 4) * P:(c % 4 + 1) * P], ident[:, :])
                    done.then_inc(qk_turned, 1)

                def one_tile(t, s, first, last):
                    pe.wait_ge(h_ready, CREDIT + t * 2 + 2)
                    for part in range(3):
                        pe.wait_ge(qkv_copied, CREDIT + t * 3 - 2 + part)
                        for k in range(KT):
                            done = pe.matmul(qkv_ps[:, part, :], hT[:, s, k, :], w_sb[:, k, part * SBW:(part + 1) * SBW],
                                             start=(k == 0), stop=(k == KT - 1))
                        done.then_inc(projected, 1)
                        if part == 0 and not first:
                            turn_qk(t - 1, 1 - s)
                        if part == 1 and not last:
                            turn_x(t + 1, 1 - s)

                pe.wait_ge(consts, 2)
                turn_x(0, 0)
                tile_pairs(pe, one_tile)
                turn_qk(NT - 1, 1)


def project_channels(nc, program, h_all, w_in, rw_shift_mu, pT_dram):
    with ExitStack() as ctx:
        sb, pb, sem = makers(nc, ctx, program)
        NFULL = RW_COLS // P
        REST = RW_COLS - NFULL * P
        LOOPED = NFULL // 2 * 2
        GT = 512
        NG = SEQ // GT
        w = sb("w_ch", [P, 2, KT, P])
        mu = sb("mu", [P, NFULL + 1])
        p_raw = sb("p_raw", [P, 1 + SEQ])
        diff = sb("diff", [P, SEQ])
        shifted = sb("shifted", [P, 2, SEQ])
        mu_c = sb("mu_c", [P, 1])
        p_ps = pb("p_ps", [P, 2, NG, GT])
        mu_loaded = sem("p2_mu_loaded")
        w_loaded = [sem(f"p2_w_loaded{s}") for s in range(2)]
        projected = sem("p2_projected")
        copied = sem("p2_copied")
        mixed = sem("p2_mixed")
        stored = [sem(f"p2_stored{s}") for s in range(2)]
        zeroed = sem("p2_zeroed")
        on_sp, on_act, on_pe, on_dve, on_pool = program.gates_passed
        NCH = NFULL + 1
        give_credit(nc, mixed)
        with nc.Block() as block:
            @block.sync
            def _(sp):
                def load(c, s, width=P):
                    src = w_in[0, :, bass.ds(c * P + SB_COLS, width)].rearrange("(k p) c -> p k c", p=P)
                    sp.dma_start(w[:, s, :, 0:width], src).then_inc(w_loaded[s], 16)

                def store(c, s, width=P):
                    sp.wait_ge(mixed, CREDIT + c + 1)
                    sp.dma_start(pT_dram[bass.ds(c * P, width), :], shifted[0:width, s, :]).then_inc(stored[s], 16)

                load(0, 0)
                load(1, 1)
                with nc.allow_non_contiguous_dma("a small vector, once"):
                    sp.dma_start(mu[:, 0:NFULL], rw_shift_mu[0, 0:NFULL * P].rearrange("(k p) -> p k", p=P)).then_inc(mu_loaded, 16)
                    sp.dma_start(mu[0:REST, NFULL:NFULL + 1], rw_shift_mu[0, NFULL * P:RW_COLS].rearrange("(k p) -> p k", k=1)).then_inc(mu_loaded, 16)
                with sp.Fori(0, LOOPED // 2 - 1) as i:
                    for s in range(2):
                        c = i * 2 + s
                        sp.wait_ge(projected, (c + 1) * NG)
                        load(c + 2, s)
                        store(c, s)
                for c in range(LOOPED - 2, NCH):
                    if c + 2 < NCH:
                        sp.wait_ge(projected, (c + 1) * NG)
                        load(c + 2, c % 2, P if c + 2 < NFULL else REST)
                    store(c, c % 2, P if c < NFULL else REST)
                for s in range(2):
                    sp.wait_ge(stored[s], 16 * (NCH // 2) + 16)

            @block.tensor
            def _(pe):
                def chunk(c, s, n, width=P):
                    pe.wait_ge(w_loaded[s], n * 16 + 16)
                    for g in range(NG):
                        pe.wait_ge(copied, c * NG + g + 1)
                        for k in range(KT):
                            last = pe.matmul(p_ps[0:width, s, g, :], w[:, s, k, 0:width], h_all[:, k, g * GT:(g + 1) * GT],
                                             start=(k == 0), stop=(k == KT - 1))
                        last.then_inc(projected, 1)

                with pe.Fori(0, LOOPED // 2) as i:
                    for s in range(2):
                        chunk(i * 2 + s, s, i)
                for c in range(LOOPED, NCH):
                    chunk(c, c % 2, c // 2, P if c < NFULL else REST)

            @block.scalar
            def _(act):
                act.sem_inc(copied, 2 * NG)
                act.wait_ge(zeroed, 1)

                def chunk(c, s, n, width=P):
                    act.wait_ge(mixed, CREDIT + c)
                    for g in range(NG):
                        act.wait_ge(projected, c * NG + g + 1)
                        act.copy(p_raw[0:width, 1 + g * GT:1 + (g + 1) * GT], p_ps[0:width, s, g, :]).then_inc(copied, 1)

                with act.Fori(0, LOOPED // 2) as i:
                    for s in range(2):
                        chunk(i * 2 + s, s, i)
                for c in range(LOOPED, NCH):
                    chunk(c, c % 2, c // 2, P if c < NFULL else REST)

            @block.vector
            def _(dve):
                dve.memset(p_raw[:, 0:1], 0.0).then_inc(zeroed, 1)
                dve.wait_ge(mu_loaded, 32)
                dve.sem_inc(stored[0], 16)
                dve.sem_inc(stored[1], 16)

                def chunk(c, s, n, width=P):
                    dve.wait_ge(copied, (c + 1) * NG + 2 * NG)
                    dve.tensor_tensor(diff[0:width, :], p_raw[0:width, 0:SEQ], p_raw[0:width, 1:1 + SEQ], ALU.subtract)
                    dve.tensor_copy(mu_c[0:width, :], mu[0:width, bass.ds(c, 1)])
                    dve.drain()
                    dve.wait_ge(stored[s], n * 16 + 16)
                    dve.scalar_tensor_tensor(shifted[0:width, s, :], diff[0:width, :], mu_c[0:width, :],
                                             p_raw[0:width, 1:1 + SEQ], ALU.mult, ALU.add).then_inc(mixed, 1)

                with dve.Fori(0, LOOPED // 2) as i:
                    for s in range(2):
                        chunk(i * 2 + s, s, i)
                for c in range(LOOPED, NCH):
                    chunk(c, c % 2, c // 2, P if c < NFULL else REST)


def stick_breaking(nc, program, qT_dram, kT_dram, v_dram, mixT_dram):
    with ExitStack() as ctx:
        sb, pb, sem = makers(nc, ctx, program)
        CH = 512
        SLOTS = 3
        ZR = 3
        SCALE = HD ** -0.5
        units = [(t, h) for t in range(NT) for h in range(2)]
        n_chunks = [((t + 1) * P + CH - 1) // CH for t, _ in units]
        first = [sum(n_chunks[:u]) for u in range(len(units) + 1)]
        NU, NCH = len(units), first[-1]

        q_sb = sb("q_sb", [P, SEQ])
        k_sb = sb("k_sb", [P, SEQ])
        v_sb = sb("v_sb", [P, NT, P])
        keep = sb("keep", [P, SLOTS, SEQ])
        take = sb("take", [P, SLOTS, SEQ])
        prod = sb("prod", [P, SLOTS, SEQ])
        wT = sb("wT", [P, 2, CH])
        o_sb = sb("o_sb", [P, P])
        oT_sb = sb("oT_sb", [P, 2, P])
        ident = sb("ident_a", [P, P])
        z_ps = [pb(f"z_ps{i}", [P, CH]) for i in range(ZR)]
        wT_ps = [pb(f"wT_ps{i}", [P, CH]) for i in range(2)]
        o_banks = pb("o_banks", [P, 3, CH])
        o_ps = [o_banks[:, 0, 0:P], o_banks[:, 1, 0:P]]
        oT_ps = o_banks[:, 2, 0:P]

        consts = sem("p3_consts")
        qkv_loaded = sem("p3_qkv_loaded")
        z_done = sem("p3_z_done")
        z_read = sem("p3_z_read")
        masked = sem("p3_masked")
        scanned = sem("p3_scanned")
        weighted = sem("p3_weighted")
        turned = sem("p3_turned")
        turned_copied = sem("p3_turned_copied")
        weighed = sem("p3_weighed")
        o_copied = sem("p3_o_copied")
        o_turned = sem("p3_o_turned")
        oT_copied = sem("p3_oT_copied")
        stored = [sem(f"p3_stored{s}") for s in range(2)]
        on_sp, on_act, on_pe, on_dve, on_pool = program.gates_passed

        give_credit(nc, oT_copied, o_copied, o_turned, *stored, turned_copied, weighed, z_read)
        with nc.Block() as block:
            @block.sync
            def _(sp):
                with sp.Fori(0, PAIRS) as j:
                    sp.wait_ge(weighed, CREDIT + j * NCH)
                    sp.dma_start(q_sb[:, :], qT_dram[bass.ds(j * P, P), :]).then_inc(qkv_loaded, 16)
                    sp.dma_start(k_sb[:, :], kT_dram[bass.ds(j * P, P), :]).then_inc(qkv_loaded, 16)
                    sp.dma_start(v_sb[:, :, :], v_dram[:, bass.ds(j * P, P)].rearrange("(n p) c -> p n c", p=P)).then_inc(qkv_loaded, 16)
                    for t in range(NT):
                        sp.wait_ge(oT_copied, CREDIT + j * NT + t + 1)
                        sp.dma_start(mixT_dram[bass.ds(j * P, P), t * P:(t + 1) * P], oT_sb[:, t % 2, :]).then_inc(stored[t % 2], 16)
                for s in range(2):
                    sp.wait_ge(stored[s], CREDIT + 16 * PAIRS * NT // 2)

            @block.tensor
            def _(pe):
                pe.wait_ge(consts, 1)

                def scores(j, u, c):
                    if u >= NU or c >= n_chunks[u]:
                        return
                    (t, h), n = units[u], first[u] + c
                    hs = slice(h * HD, (h + 1) * HD)
                    w = min(CH, (t + 1) * P - c * CH)
                    pe.wait_ge(z_read, CREDIT + j * NCH + max(n - ZR + 1, 0))
                    pe.matmul(z_ps[n % ZR][:, 0:w], q_sb[hs, t * P:(t + 1) * P], k_sb[hs, c * CH:c * CH + w],
                              start=True, stop=True).then_inc(z_done, 1)

                def turn(j, u, c):
                    t, n = units[u][0], first[u] + c
                    if c == 0:
                        pe.wait_ge(weighted, j * NU + u + 1)
                    pe.wait_ge(turned_copied, CREDIT + j * NCH + max(n - 1, 0))
                    for b in range(min(4, t + 1 - 4 * c)):
                        s0 = c * CH + b * P
                        last = pe.transpose(wT_ps[n % 2][:, b * P:(b + 1) * P], take[:, u % SLOTS, s0:s0 + P], ident[:, :])
                    last.then_inc(turned, 1)

                def weigh(j, u, c):
                    (t, h), n = units[u], first[u] + c
                    pe.wait_ge(turned_copied, CREDIT + j * NCH + n + 1)
                    if c == 0 and h == 0:
                        pe.wait_ge(o_copied, CREDIT + j * NT + max(t - 1, 0))
                    for b in range(min(4, t + 1 - 4 * c)):
                        s = 4 * c + b
                        last = pe.matmul(o_ps[t % 2][:, h * HD:(h + 1) * HD], wT[:, n % 2, b * P:(b + 1) * P],
                                         v_sb[:, s, h * HD:(h + 1) * HD], start=(s == 0), stop=(s == t))
                    last.then_inc(weighed, 1)

                def turn_out(j, t):
                    pe.wait_ge(o_copied, CREDIT + j * NT + t + 1)
                    pe.wait_ge(oT_copied, CREDIT + j * NT + t)
                    pe.transpose(oT_ps, o_sb[:, :], ident[:, :]).then_inc(o_turned, 1)

                with pe.Fori(0, PAIRS) as j:
                    pe.wait_ge(qkv_loaded, j * 48 + 48)
                    scores(j, 0, 0)
                    scores(j, 1, 0)
                    for u, (t, h) in enumerate(units):
                        turn(j, u, 0)
                        for c in range(n_chunks[u]):
                            scores(j, u + 2, c)
                            if c + 1 < n_chunks[u]:
                                turn(j, u, c + 1)
                            weigh(j, u, c)
                        for c in range(n_chunks[u], n_chunks[min(u + 2, NU - 1)]):
                            scores(j, u + 2, c)
                        if h == 1 and t >= 1:
                            turn_out(j, t - 1)
                    turn_out(j, NT - 1)

            @block.scalar
            def _(act):
                def copy_out(j, t):
                    act.wait_ge(weighed, CREDIT + j * NCH + first[2 * t + 2])
                    act.wait_ge(o_turned, CREDIT + j * NT + t)
                    act.copy(o_sb[:, :], o_ps[t % 2]).then_inc(o_copied, 1)

                def copy_turned(j, t):
                    act.wait_ge(o_turned, CREDIT + j * NT + t + 1)
                    if t >= 2:
                        act.wait_ge(stored[t % 2], CREDIT + j * (8 * NT) + 16 * (t // 2))
                    else:
                        act.wait_ge(stored[t % 2], CREDIT + j * (8 * NT))
                    act.copy(oT_sb[:, t % 2, :], oT_ps).then_inc(oT_copied, 1)

                with act.Fori(0, PAIRS) as j:
                    for u, (t, h) in enumerate(units):
                        act.wait_ge(weighed, CREDIT + j * NCH + first[max(u - SLOTS + 1, 0)])
                        if h == 0 and t >= 2:
                            copy_out(j, t - 2)
                        if h == 0 and t >= 3:
                            copy_turned(j, t - 3)
                        for c in range(n_chunks[u]):
                            n = first[u] + c
                            w = min(CH, (t + 1) * P - c * CH)
                            cols = slice(c * CH, c * CH + w)
                            act.wait_ge(z_done, j * NCH + n + 1)
                            act.activation(keep[:, u % SLOTS, cols], z_ps[n % ZR][:, 0:w], ACT.Sigmoid, scale=-SCALE)
                            act.activation(take[:, u % SLOTS, cols], z_ps[n % ZR][:, 0:w], ACT.Sigmoid, scale=SCALE).then_inc(z_read, 1)
                    copy_out(j, NT - 2)
                    copy_turned(j, NT - 3)
                    copy_turned(j, NT - 2)
                    copy_out(j, NT - 1)
                    copy_turned(j, NT - 1)

            @block.gpsimd
            def _(pool):
                identity(pool, ident[:, :]).then_inc(consts, 1)

                def mask(j, u):
                    t, slot = units[u][0], u % SLOTS
                    diag = slice(t * P, (t + 1) * P)
                    pool.wait_ge(z_read, CREDIT + j * NCH + first[u + 1])
                    pool.sem_inc(on_pool, 1)
                    for tile, fill in ((keep, 1.0), (take, 0.0)):
                        last = pool.affine_select(out=tile[:, slot, diag], in_=tile[:, slot, diag], compare_op=ALU.is_gt,
                                                  fill=fill, base=0, pattern=[[-1, P]], channel_multiplier=1)
                    last.then_inc(masked, 1)

                def weight(j, u):
                    t, slot = units[u][0], u % SLOTS
                    L = (t + 1) * P
                    pool.wait_ge(scanned, j * NU + u + 1)
                    pool.sem_inc(on_pool, 1)
                    pool.tensor_tensor(take[:, slot, 0:L - 1], take[:, slot, 0:L - 1], prod[:, slot, 1:L],
                                       ALU.mult).then_inc(weighted, 1)

                with pool.Fori(0, PAIRS) as j:
                    for u in range(NU):
                        mask(j, u)
                        weight(j, u)

            @block.vector
            def _(dve):
                def scan(j, u):
                    t, slot = units[u][0], u % SLOTS
                    L = (t + 1) * P
                    dve.wait_ge(masked, j * NU + u + 1)
                    rows = keep[:, slot, 0:L][:, ::-1]
                    dve.tensor_tensor_scan(prod[:, slot, 0:L][:, ::-1], rows, rows, 1.0, ALU.mult, ALU.bypass).then_inc(scanned, 1)

                with dve.Fori(0, PAIRS) as j:
                    scan(j, 0)
                    for u in range(NU):
                        for c in range(n_chunks[u]):
                            n = first[u] + c
                            w = min(CH, (units[u][0] + 1) * P - c * CH)
                            dve.wait_ge(turned, j * NCH + n + 1)
                            dve.wait_ge(weighed, CREDIT + j * NCH + max(n - 1, 0))
                            dve.tensor_copy(wT[:, n % 2, 0:w], wT_ps[n % 2][:, 0:w]).then_inc(turned_copied, 1)
                            if c == 0 and u + 1 < NU:
                                scan(j, u + 1)


class Stream:

    def __init__(self, p, sb, pb):
        C, NC, GT = HD, 512 // HD, 512
        self.p = p
        self.rkv = sb(f"rkv{p}", [P, 3, GT])
        self.w_up, self.a_up, self.g_up = [sb(f"{n}{p}", [w, P]) for n, w in (("w_up_p", LW), ("a_up_p", LA), ("g_up_p", LG))]
        self.vecs = sb(f"vecs{p}", [P, 5])
        self.lnv = sb(f"lnv{p}", [P, 2])
        self.logw, self.kraw, self.sq, self.root = [sb(f"{n}{p}", [P, GT]) for n in ("logw", "kraw", "sq", "root")]
        self.a_g, self.k2, self.rk, self.kka = [sb(f"{n}{p}", [P, GT]) for n in ("a_g", "k2", "rk", "kka")]
        self.Lsum, self.Dec, self.DecP, self.DecI = [sb(f"{n}{p}", [P, GT]) for n in ("Lsum", "Dec", "DecP", "DecI")]
        self.g, self.bonus, self.dev, self.std = [sb(f"{n}{p}", [P, GT]) for n in ("g", "bonus", "dev", "std")]
        self.r_t = sb(f"r_t{p}", [P, NC, C])
        self.ends = sb(f"ends{p}", [P, NC])
        self.AR = sb(f"AR{p}", [P, NC, 2, C])
        self.b_t, self.k_t, self.b_h, self.k_h = [sb(f"{n}{p}", [P, GT]) for n in ("b_t", "k_t", "b_h", "k_h")]
        self.tok = sb(f"tok{p}", [P, 4, NC, C])
        self.SB1 = sb(f"SB1_{p}", [P, NC, 2, C])
        self.SB2 = sb(f"SB2_{p}", [P, NC, 2, C])
        self.ATl = sb(f"ATl{p}", [P, 5, NC, C])
        self.XX = sb(f"XX{p}", [P, 2, NC, C])
        self.T1 = sb(f"T1_{p}", [P, NC, C])
        self.GW = sb(f"GW{p}", [P, 2, NC, C])
        self.SA = sb(f"SA{p}", [P, C])
        self.S = sb(f"S_state{p}", [P, C])
        self.y = sb(f"y_sb{p}", [P, GT])
        self.outp = sb(f"outp{p}", [P, GT])
        self.QA, self.QB = pb(f"QA{p}", [P, 2, 512]), pb(f"QB{p}", [P, 2, 512])


def time_mixing(nc, program, w0, w_up, a0, a_up, g_up, k_k, k_a, r_k, ln_w, ln_b, pT_dram, mixT_dram):
    with ExitStack() as ctx:
        sb, pb, sem = makers(nc, ctx, program)
        C = HD
        GT = 512
        NG, NC = SEQ // GT, GT // C
        HC = NC // 2
        LEVELS = (2, 4, 8, 16, 32)
        NL = len(LEVELS)
        LORA = 3 * SBW
        N2 = PAIRS // 2

        wd = sb("wd", [LW, GT])
        ad = sb("ad", [LA, GT])
        gd = sb("gd", [LG, GT])
        ident = sb("ident_r", [P, P])
        head_ones = sb("head_ones", [P, P])
        chunk_reset = sb("chunk_reset", [P, GT])
        zero_eps = sb("zero_eps", [P, 2])
        below = sb("below", [P, 2, C])
        lev = sb("lev", [P, NL, C])
        lev1T = sb("lev1T", [P, C])
        lev1 = sb("lev1", [P, C])
        eye = sb("eye", [P, C])
        streams = [Stream(p, sb, pb) for p in range(2)]

        names = """weights lnw_loaded consts loaded0 loaded1 lora_loaded gate_loaded lora_ready gate_ready kk2_ready pre_done pre_read
            L_ready exp_ready root_ready operands_ready bonus_done bonus_read bonus_ready turnedA_done turnedB_done tokA_ready
            tokB_ready scores1_done scores2_done scores1_ready scores2_ready A_done level0_ready levels_ready X_ready T_done
            T_ready dX_done GW_done GW_ready sa_done saA_ready saB_ready dS_done S_ready y_done y_ready g_done g_ready mean_done
            centred_ready var_done std_ready out_ready stored0 stored1""".split()
        (weights, lnw_loaded, consts, loaded0, loaded1, lora_loaded, gate_loaded, lora_ready, gate_ready, kk2_ready, pre_done, pre_read,
         L_ready, exp_ready, root_ready, operands_ready, bonus_done, bonus_read, bonus_ready, turnedA_done, turnedB_done, tokA_ready,
         tokB_ready, scores1_done, scores2_done, scores1_ready, scores2_ready, A_done, level0_ready, levels_ready, X_ready, T_done,
         T_ready, dX_done, GW_done, GW_ready, sa_done, saA_ready, saB_ready, dS_done, S_ready, y_done, y_ready, g_done, g_ready, mean_done,
         centred_ready, var_done, std_ready, out_ready, stored0, stored1) = [sem(f"p4_{n}") for n in names]
        loaded, stored = (loaded0, loaded1), (stored0, stored1)
        on_sp, on_act, on_pe, on_dve, on_pool = program.gates_passed
        N_CONSTS = 2
        N_WEIGHTS = 7 * 2
        N_LNW = 3 * 2

        def chunks(tile):
            return tile[:, :].rearrange("p (c t) -> p c t", t=C)

        def two(bank_pair):
            return bank_pair[:, :, :].rearrange("p b (q x) -> p b q x", q=2)

        def two_sb(tile):
            return tile.rearrange("p q (b h) c -> p b q (h c)", b=2)

        def at(n, st, K=1, x=0):
            return (n * K + x) * 2 + st.p + 1

        PRE = 3
        TURNS = N2 * NG
        give_credit(nc, out_ready, std_ready, g_ready, g_done, *stored)
        with nc.Block() as block:
            @block.sync
            def _(sp):
                def load_next(i, g, n):
                    ts = bass.ds(g * GT, GT)
                    sp.dma_start(wd[:, :], pT_dram[LORA:LORA + LW, ts]).then_inc(lora_loaded, 16)
                    sp.dma_start(ad[:, :], pT_dram[LORA + LW:LORA + LW + LA, ts]).then_inc(lora_loaded, 16)
                    for st in streams:
                        cols = bass.ds((i * 2 + st.p) * P, P)
                        sp.dma_start(st.w_up[:, :], w_up[0, :, cols]).then_inc(weights, 16)
                        sp.dma_start(st.a_up[:, :], a_up[0, :, cols]).then_inc(weights, 16)
                        for x, vec in enumerate((w0[0], a0[0], k_k[0], k_a[0], r_k[0].rearrange("h d -> (h d)"))):
                            sp.dma_start(st.vecs[:, x:x + 1], vec[cols].unsqueeze(1)).then_inc(weights, 16)

                def load_rkv(st, i, g):
                    for a in range(3):
                        sp.dma_start(st.rkv[:, a, :], pT_dram[bass.ds((i * 2 + st.p) * P + a * SBW, P), bass.ds(g * GT, GT)]).then_inc(loaded[st.p], 16)

                def turn(i, g, n, next_i, next_g):
                    sp.wait_ge(g_done, CREDIT + n * 2)
                    sp.sem_inc(on_sp, 1)
                    sp.wait_ge(out_ready, CREDIT + n * 2)
                    sp.sem_inc(on_sp, 1)
                    sp.dma_start(gd[:, :], pT_dram[LORA + LW + LA:LORA + LW + LA + LG, bass.ds(g * GT, GT)]).then_inc(gate_loaded, 16)
                    for st in streams:
                        cols = bass.ds((i * 2 + st.p) * P, P)
                        sp.dma_start(st.g_up[:, :], g_up[0, :, cols]).then_inc(lnw_loaded, 16)
                        for x, vec in enumerate((ln_w[0], ln_b[0])):
                            sp.dma_start(st.lnv[:, x:x + 1], vec[cols].unsqueeze(1)).then_inc(lnw_loaded, 16)
                    sp.wait_ge(operands_ready, at(n, streams[1]))
                    sp.sem_inc(on_sp, 1)
                    load_next(next_i, next_g, n + 1)
                    for st in streams:
                        sp.wait_ge(turnedB_done, at(n, st))
                        sp.sem_inc(on_sp, 1)
                        sp.wait_ge(bonus_ready, at(n, st))
                        sp.sem_inc(on_sp, 1)
                        load_rkv(st, next_i, next_g)
                    for st in streams:
                        sp.wait_ge(out_ready, CREDIT + at(n, st))
                        sp.sem_inc(on_sp, 1)
                        sp.dma_start(mixT_dram[bass.ds((i * 2 + st.p) * P + SBW, P), bass.ds(g * GT, GT)], st.outp[:, :]).then_inc(stored[st.p], 16)

                load_next(0, 0, 0)
                for st in streams:
                    load_rkv(st, 0, 0)

                def turns_of(i, after):
                    with sp.Fori(0, NG - 1) as g:
                        turn(i, g, i * NG + g, i, g + 1)
                    turn(i, NG - 1, i * NG + NG - 1, after, 0)

                with sp.Fori(0, N2 - 1) as i:
                    turns_of(i, i + 1)
                turns_of(N2 - 1, 0)
                for st in streams:
                    sp.wait_ge(stored[st.p], CREDIT + 16 * TURNS)

            @block.gpsimd
            def _(pool):
                def block_select(tile, op, base, pattern, mult, fill=0.0):
                    pool.affine_select(out=tile, in_=tile, compare_op=op, fill=fill, base=base,
                                       pattern=pattern, channel_multiplier=mult)
                    pool.drain()

                identity(pool, ident[:, :])
                pool.drain()
                pool.memset(head_ones[:, :], 0.0)
                pool.memset(chunk_reset[:, :], 1.0)
                pool.memset(below[:, :, :], 1.0)
                pool.memset(lev[:, :, :], 0.0)
                pool.memset(lev1[:, :], 0.0)
                pool.memset(lev1T[:, :], 0.0)
                pool.memset(zero_eps[:, 0:1], 0.0)
                pool.memset(zero_eps[:, 1:2], LN_X_EPS)
                pool.drain()
                pool.memset(chunks(chunk_reset)[:, :, 0:1], 0.0)
                for h in range(2):
                    hs = slice(h * C, (h + 1) * C)
                    pool.memset(head_ones[hs, hs], 1.0)
                    pool.tensor_copy(eye[hs, :], ident[hs, hs])
                    block_select(below[hs, 0, :], ALU.is_gt, 0, [[1, C]], -1)
                    block_select(below[hs, 1, :], ALU.is_ge, 0, [[1, C]], -1)
                    block_select(lev1T[hs, :].rearrange("p (n b) -> p n b", b=2)[:, :, 0], ALU.not_equal, -1, [[-2, C // 2]], 1, 1.0)
                    block_select(lev1[hs, :].rearrange("p (n b) -> p n b", b=2)[:, :, 1], ALU.not_equal, 0, [[-2, C // 2]], 1, 1.0)
                    for x, size in enumerate(LEVELS):
                        v = lev[hs, x, :].rearrange("p (n b s) -> p n b s", b=2, s=size)[:, :, 1, :]
                        nb = C // (2 * size)
                        pool.memset(v, 1.0)
                        pool.drain()
                        block_select(v, ALU.is_ge, 0, [[-2 * size, nb], [0, size]], 1)
                        block_select(v, ALU.is_ge, size - 1, [[2 * size, nb], [0, size]], -1)
                pool.drain()
                pool.sem_inc(consts, N_CONSTS)

                def prepare_first(m, st):
                    pool.wait_ge(loaded[st.p], m * 48 + 48)
                    pool.sem_inc(on_pool, 1)
                    pool.wait_ge(weights, m * (16 * N_WEIGHTS) + 16 * N_WEIGHTS)
                    pool.sem_inc(on_pool, 1)
                    pool.tensor_scalar(st.kraw[:, :], st.rkv[:, 1, :], st.vecs[:, 2:3], None, ALU.mult)
                    pool.drain()
                    pool.tensor_tensor(st.sq[:, :], st.kraw[:, :], st.kraw[:, :], ALU.mult).then_inc(kk2_ready, 1)

                def prepare_k(m, st):
                    pool.wait_ge(pre_read, at(m, st, PRE, 1))
                    pool.sem_inc(on_pool, 1)
                    pool.tensor_scalar(st.k2[:, :], st.a_g[:, :], -1.0, st.vecs[:, 3:4], ALU.add, ALU.mult)
                    pool.tensor_scalar(st.rk[:, :], st.rkv[:, 0, :], st.vecs[:, 4:5], None, ALU.mult)
                    pool.drain()
                    pool.tensor_scalar(st.k2[:, :], st.k2[:, :], 1.0, None, ALU.add)
                    pool.drain()
                    pool.tensor_tensor(st.k2[:, :], st.k2[:, :], st.rkv[:, 1, :], ALU.mult)
                    pool.drain()
                    pool.tensor_tensor(st.rk[:, :], st.rk[:, :], st.k2[:, :], ALU.mult)

                def prepare_operands(m, st):
                    pool.wait_ge(root_ready, at(m, st))
                    pool.sem_inc(on_pool, 1)
                    pool.wait_ge(exp_ready, at(m, st))
                    pool.sem_inc(on_pool, 1)
                    pool.tensor_tensor(st.kraw[:, :], st.kraw[:, :], st.root[:, :], ALU.mult)
                    pool.tensor_tensor(st.k_t[:, :], st.k2[:, :], st.DecI[:, :], ALU.mult)
                    pool.tensor_tensor(st.AR[:, :, 1, :], st.rkv[:, 0, :].rearrange("p (c t) -> p c t", t=C), chunks(st.Dec), ALU.mult)
                    pool.drain()
                    end = chunks(st.Dec)[:, :, C - 1:C].to_broadcast([P, NC, C])
                    pool.tensor_tensor(st.AR[:, :, 0, :], chunks(st.kraw), chunks(st.DecP), ALU.mult)
                    pool.tensor_tensor(st.kka[:, :], st.kraw[:, :], st.a_g[:, :], ALU.mult)
                    pool.tensor_tensor(chunks(st.k_h), chunks(st.k_t), end, ALU.mult)
                    pool.tensor_scalar(st.DecI[:, :], st.DecI[:, :], -1.0, None, ALU.mult)
                    pool.drain()
                    pool.tensor_tensor(st.b_t[:, :], st.kka[:, :], st.DecI[:, :], ALU.mult)
                    pool.drain()
                    pool.tensor_tensor(chunks(st.b_h), chunks(st.b_t), end, ALU.mult).then_inc(operands_ready, 1)

                for prepare in (prepare_first, prepare_k, prepare_operands):
                    for st in streams:
                        prepare(0, st)
                with pool.Fori(0, TURNS) as n:
                    for st in streams:
                        pool.wait_ge(bonus_read, at(n, st))
                        pool.sem_inc(on_pool, 1)
                        pool.wait_ge(out_ready, CREDIT - 1 + 2 * n + st.p)
                        pool.sem_inc(on_pool, 1)
                        pool.tensor_tensor(st.bonus[:, :], st.kka[:, :], st.rkv[:, 2, :], ALU.mult).then_inc(bonus_ready, 1)
                    for st in streams:
                        pool.wait_ge(scores1_ready, at(n, st))
                        pool.sem_inc(on_pool, 1)
                        for x in range(NL):
                            done = pool.tensor_tensor(st.ATl[:, x, :, :], st.SB1[:, :, 0, :], lev[:, x, :].unsqueeze(1).to_broadcast([P, NC, C]), ALU.mult)
                            if x == 0:
                                done.then_inc(level0_ready, 1)
                                pool.tensor_copy(st.r_t[:, :, :], st.AR[:, :, 1, :])
                                pool.tensor_copy(st.ends[:, :].unsqueeze(2), chunks(st.Dec)[:, :, C - 1:C])
                        done.then_inc(levels_ready, 1)
                    for st in streams:
                        prepare_first(n + 1, st)
                    for st in streams:
                        prepare_k(n + 1, st)
                    for st in streams:
                        pool.wait_ge(GW_done, at(n, st))
                        pool.sem_inc(on_pool, 1)
                        prepare_operands(n + 1, st)

            @block.scalar
            def _(act):
                act.wait_ge(consts, N_CONSTS)

                def wide(st):
                    return st.QB[:, :, 256:512]

                def halves(tile):
                    return tile[:, :].rearrange("p (b x) -> p b x", b=2)

                def bottleneck(m):
                    act.wait_ge(lora_loaded, m * 32 + 32)
                    act.activation(wd[:, :], wd[:, :], ACT.Tanh).then_inc(lora_ready, 1)

                def prepare(m, st, k):
                    act.wait_ge(pre_done, at(m, st, PRE, k))
                    if k == 0:
                        act.activation(halves(st.logw), wide(st), ACT.Sigmoid, bias=st.vecs[:, 0:1]).then_inc(pre_read, 1)
                    if k == 1:
                        act.activation(halves(st.a_g), wide(st), ACT.Sigmoid, bias=st.vecs[:, 1:2]).then_inc(pre_read, 1)
                    if k == 2:
                        act.activation(halves(st.root), wide(st), ACT.Sqrt, bias=zero_eps[:, 0:1]).then_inc(pre_read, 1)

                def exponentials(m, st):
                    act.wait_ge(L_ready, at(m, st))
                    act.activation(st.Dec[:, :], st.Lsum[:, :], ACT.Exp)
                    act.activation(st.DecI[:, :], st.Lsum[:, :], ACT.Exp, scale=-1.0)
                    act.activation(st.DecP[:, :], st.logw[:, :], ACT.Exp).then_inc(exp_ready, 1)

                bottleneck(0)
                act.wait_ge(weights, 16 * N_WEIGHTS)
                for k in range(PRE):
                    for st in streams:
                        prepare(0, st, k)
                for st in streams:
                    exponentials(0, st)
                with act.Fori(0, TURNS) as n:
                    for st in streams:
                        act.wait_ge(bonus_done, at(n, st))
                        act.copy(st.kka[:, :], st.QB[:, 1, :]).then_inc(bonus_read, 1)
                        act.wait_ge(turnedA_done, at(n, st))
                        act.copy(two_sb(st.tok[:, 0:2, :, :]), two(st.QA)).then_inc(tokA_ready, 1)
                    for st in streams:
                        act.wait_ge(turnedB_done, at(n, st))
                        act.copy(two_sb(st.tok[:, 2:4, :, :]), two(st.QB)).then_inc(tokB_ready, 1)
                    act.wait_ge(gate_loaded, n * 16 + 16)
                    act.activation(gd[:, :], gd[:, :], ACT.Sigmoid).then_inc(gate_ready, 1)
                    bottleneck(n + 1)
                    for x in range(NL):
                        for st in streams:
                            act.wait_ge(T_done, at(n, st, NL, x))
                            act.copy(st.T1[:, :, :].rearrange("p (b h) c -> p b (h c)", b=2), st.QB[:, :, 0:256]).then_inc(T_ready, 1)
                        if 1 <= x <= PRE:
                            if x == 1:
                                act.wait_ge(weights, n * (16 * N_WEIGHTS) + 2 * 16 * N_WEIGHTS)
                            for st in streams:
                                prepare(n + 1, st, x - 1)
                        if x == PRE:
                            for st in streams:
                                exponentials(n + 1, st)
                    for st in streams:
                        act.wait_ge(GW_done, at(n, st))
                        act.copy(two_sb(st.GW[:, :, :, :]), two(st.QB)).then_inc(GW_ready, 1)
                    for c in range(NC):
                        for st in streams:
                            act.wait_ge(sa_done, at(n, st, NC, c))
                            act.copy(st.SA[0:C, :], st.QA[0:C, 0, 0:C]).then_inc(saA_ready, 1)
                    for st in streams:
                        act.wait_ge(y_done, at(n, st))
                        for h in range(2):
                            hs = slice(h * C, (h + 1) * C)
                            done = act.copy(st.y[hs, :], st.QB[hs, h, :])
                        done.then_inc(y_ready, 1)
                    for st in streams:
                        act.wait_ge(g_done, CREDIT + at(n, st))
                        act.copy(st.g[:, :], st.QB[:, 0, :]).then_inc(g_ready, 1)
                    for st in streams:
                        act.wait_ge(var_done, at(n, st))
                        act.activation(st.std[:, :], st.QA[:, 1, :], ACT.Sqrt, bias=zero_eps[:, 1:2], scale=1.0 / HD).then_inc(std_ready, 1)

            @block.vector
            def _(dve):
                def decay(m, st):
                    dve.wait_ge(pre_read, at(m, st, PRE, 0))
                    dve.tensor_scalar(st.logw[:, :], st.logw[:, :], -EXP_HALF, None, ALU.mult)
                    dve.drain()
                    dve.tensor_tensor_scan(st.Lsum[:, :], chunk_reset[:, :], st.logw[:, :], 0.0, ALU.mult, ALU.add)
                    dve.drain()
                    dve.tensor_tensor(st.logw[:, :], st.Lsum[:, :], st.logw[:, :], ALU.subtract).then_inc(L_ready, 1)

                def norm(m, st):
                    dve.wait_ge(pre_read, at(m, st, PRE, 2))
                    dve.tensor_scalar(st.root[:, :], st.root[:, :], 1e-12, -1.0, ALU.max, ALU.mult)
                    dve.drain()
                    dve.reciprocal(st.root[:, :], st.root[:, :]).then_inc(root_ready, 1)

                def group(i, g):
                    n = i * NG + g
                    low = below[:, :, :].rearrange("p a t -> p (a t)").unsqueeze(1).to_broadcast([P, NC, 2 * C])
                    for st in streams:
                        for done, ready, banks, to in ((scores1_done, scores1_ready, st.QA, st.SB1), (scores2_done, scores2_ready, st.QB, st.SB2)):
                            dve.wait_ge(done, at(n, st))
                            dve.tensor_tensor(to[:, :, :, :].rearrange("p c a t -> p c (a t)"),
                                              banks[:, :, :].rearrange("p b (h x) -> p (b h) x", x=2 * C), low, ALU.mult).then_inc(ready, 1)
                    dve.drain()
                    for st in streams:
                        dve.tensor_tensor(st.XX[:, 1, :, :], st.SB1[:, :, 0, :], lev1[:, :].unsqueeze(1).to_broadcast([P, NC, C]), ALU.mult)
                        dve.wait_ge(A_done, at(n, st))
                        dve.tensor_tensor(st.XX[:, 0, :, :].rearrange("p (b h) c -> p b h c", b=2),
                                          two(st.QA)[:, :, 0, :].rearrange("p b (h c) -> p b h c", c=C),
                                          lev1T[:, :].unsqueeze(1).unsqueeze(1).to_broadcast([P, 2, HC, C]), ALU.mult)
                        dve.drain()
                        both = st.XX[:, :, :, :].rearrange("p q n c -> p (q n) c")
                        dve.tensor_tensor(both, both, eye[:, :].unsqueeze(1).to_broadcast([P, 2 * NC, C]), ALU.add).then_inc(X_ready, 1)
                    for x in range(NL):
                        for st in streams:
                            dve.wait_ge(dX_done, at(n, st, NL, x))
                            if x < NL - 1:
                                dve.tensor_tensor(two_sb(st.XX[:, :, :, :]), two_sb(st.XX[:, :, :, :]), two(st.QA), ALU.add).then_inc(X_ready, 1)
                            else:
                                XT = st.XX[:, 1, :, :].rearrange("p (b h) c -> p b (h c)", b=2)
                                dve.tensor_tensor(XT, XT, two(st.QA)[:, :, 1, :], ALU.add).then_inc(X_ready, 1)
                        if x == 1:
                            for st in streams:
                                decay(n + 1, st)
                    for st in streams:
                        norm(n + 1, st)
                    for c in range(NC):
                        for st in streams:
                            dve.wait_ge(sa_done, at(n, st, NC, c))
                            dve.tensor_copy(st.SA[C:P, :], st.QA[C:P, 1, 0:C]).then_inc(saB_ready, 1)
                        for st in streams:
                            dve.wait_ge(dS_done, at(n, st, NC, c))
                            for h in range(2):
                                hs = slice(h * C, (h + 1) * C)
                                done = dve.scalar_tensor_tensor(st.S[hs, :], st.S[hs, :], st.ends[hs, c:c + 1],
                                                                st.QA[hs, h, C:2 * C], ALU.mult, ALU.add)
                            done.then_inc(S_ready, 1)
                    for st in streams:
                        dve.wait_ge(mean_done, at(n, st))
                        dve.scalar_tensor_tensor(st.y[:, :], st.QA[:, 0, :], -1.0 / HD, st.y[:, :], ALU.mult, ALU.add)
                        dve.drain()
                        dve.tensor_tensor(st.dev[:, :], st.y[:, :], st.y[:, :], ALU.mult).then_inc(centred_ready, 1)
                    for st in streams:
                        dve.wait_ge(std_ready, CREDIT + at(n, st))
                        dve.reciprocal(st.std[:, :], st.std[:, :])
                        dve.drain()
                        dve.tensor_tensor(st.y[:, :], st.y[:, :], st.std[:, :], ALU.mult)
                        dve.drain()
                        dve.wait_ge(lnw_loaded, n * (16 * N_LNW) + 16 * N_LNW)
                        dve.tensor_scalar(st.y[:, :], st.y[:, :], st.lnv[:, 0:1], st.lnv[:, 1:2], ALU.mult, ALU.add)
                        dve.drain()
                        dve.wait_ge(bonus_ready, at(n, st))
                        dve.tensor_tensor(st.y[:, :], st.y[:, :], st.bonus[:, :], ALU.add)
                        dve.drain()
                        dve.wait_ge(stored[st.p], CREDIT + n * 16)
                        dve.wait_ge(g_ready, CREDIT + at(n, st))
                        dve.tensor_tensor(st.outp[:, :], st.y[:, :], st.g[:, :], ALU.mult).then_inc(out_ready, 1)

                dve.wait_ge(consts, N_CONSTS)
                for st in streams:
                    decay(0, st)
                for st in streams:
                    norm(0, st)
                with dve.Fori(0, N2) as i:
                    for st in streams:
                        dve.memset(st.S[:, :], 0.0).then_inc(S_ready, 1)
                    with dve.Fori(0, NG) as g:
                        group(i, g)

            @block.tensor
            def _(pe):
                HS = [slice(0, C), slice(C, P)]

                def two_heads(one):
                    for c in range(HC):
                        one(0, c)
                        one(1, HC + c)
                    for c in range(HC):
                        one(1, c)
                        done = one(0, HC + c)
                    return done

                def place(bank_pair, q, h, c):
                    x = q * 256 + (c % HC) * C
                    return bank_pair[HS[h], c // HC, x:x + C]

                def part(tile, h, c):
                    return tile[HS[h], c * C:(c + 1) * C]

                def mm(out, lhsT, rhs, start=True, stop=True):
                    return pe.matmul(out, lhsT, rhs, start=start, stop=stop)

                def prepare(m, st, k):
                    if k == 0:
                        pe.wait_ge(lora_ready, m + 1)
                        pe.sem_inc(on_pe, 1)
                        pe.wait_ge(weights, m * (16 * N_WEIGHTS) + 16 * N_WEIGHTS)
                        pe.sem_inc(on_pe, 1)
                    if k == 2:
                        pe.wait_ge(kk2_ready, at(m, st))
                        pe.sem_inc(on_pe, 1)
                    left, right = ((st.w_up, wd), (st.a_up, ad), (head_ones, st.sq))[k]
                    for b in range(2):
                        done = mm(st.QB[:, b, 256:512], left[:, :], right[:, b * 256:(b + 1) * 256])
                    done.then_inc(pre_done, 1)

                def group(i, g):
                    n = i * NG + g
                    eyes = [ident[HS[h], HS[h]] for h in range(2)]
                    for st in streams:
                        pe.wait_ge(operands_ready, at(n, st))
                        pe.sem_inc(on_pe, 1)
                        pe.wait_ge(g_ready, CREDIT - 1 + 2 * n + st.p)
                        pe.sem_inc(on_pe, 1)
                        mm(st.QB[:, 1, :], head_ones[:, :], st.rk[:, :]).then_inc(bonus_done, 1)
                        pe.wait_ge(std_ready, CREDIT - 1 + 2 * n + st.p)
                        pe.sem_inc(on_pe, 1)
                        two_heads(lambda h, c: mm(place(st.QA, 0, h, c), st.AR[HS[h], c, 0, :], eyes[h]))
                        two_heads(lambda h, c: mm(place(st.QA, 1, h, c), part(st.b_h, h, c), eyes[h])).then_inc(turnedA_done, 1)
                    for st in streams:
                        pe.wait_ge(bonus_read, at(n, st))
                        pe.sem_inc(on_pe, 1)
                        two_heads(lambda h, c: mm(place(st.QB, 0, h, c), part(st.k_h, h, c), eyes[h]))
                        two_heads(lambda h, c: mm(place(st.QB, 1, h, c), st.rkv[HS[h], 2, c * C:(c + 1) * C], eyes[h])).then_inc(turnedB_done, 1)

                    def score(st, banks, left):
                        return two_heads(lambda h, c: mm(banks[HS[h], c // HC, (c % HC) * 2 * C:(c % HC + 1) * 2 * C],
                                                         part(left, h, c), st.AR[HS[h], c, :, :]))

                    for st in streams:
                        pe.wait_ge(tokA_ready, at(n, st))
                        pe.sem_inc(on_pe, 1)
                        score(st, st.QA, st.b_t).then_inc(scores1_done, 1)
                        pe.wait_ge(tokB_ready, at(n, st))
                        pe.sem_inc(on_pe, 1)
                        score(st, st.QB, st.k_t).then_inc(scores2_done, 1)
                    for st in streams:
                        pe.wait_ge(scores1_ready, at(n, st))
                        pe.sem_inc(on_pe, 1)
                        two_heads(lambda h, c: mm(place(st.QA, 0, h, c), st.AR[HS[h], c, 0, :], part(st.b_t, h, c))).then_inc(A_done, 1)
                    for x in range(NL):
                        for st in streams:
                            if x == 0:
                                pe.wait_ge(level0_ready, at(n, st))
                                pe.sem_inc(on_pe, 1)
                                pe.wait_ge(scores2_ready, at(n, st))
                                pe.sem_inc(on_pe, 1)
                            if x == 1:
                                pe.wait_ge(levels_ready, at(n, st))
                                pe.sem_inc(on_pe, 1)
                            pe.wait_ge(X_ready, at(n, st, NL + 1, x))
                            pe.sem_inc(on_pe, 1)
                            if 2 <= x <= PRE + 1:
                                pe.wait_ge(pre_read, at(n + 1, st, PRE, x - 2))
                                pe.sem_inc(on_pe, 1)
                            two_heads(lambda h, c: mm(place(st.QB, 0, h, c), st.ATl[HS[h], x, c, :], st.XX[HS[h], 0, c, :])).then_inc(T_done, 1)
                        for st in streams:
                            pe.wait_ge(T_ready, at(n, st, NL, x))
                            pe.sem_inc(on_pe, 1)
                            if 1 <= x <= PRE:
                                prepare(n + 1, st, x - 1)
                            if x < NL - 1:
                                two_heads(lambda h, c: mm(place(st.QA, 0, h, c), st.XX[HS[h], 1, c, :], st.T1[HS[h], c, :]))
                            two_heads(lambda h, c: mm(place(st.QA, 1, h, c), st.T1[HS[h], c, :], st.XX[HS[h], 1, c, :])).then_inc(dX_done, 1)
                    for st in streams:
                        pe.wait_ge(X_ready, at(n, st, NL + 1, NL))
                        pe.sem_inc(on_pe, 1)
                        two_heads(lambda h, c: mm(place(st.QB, 0, h, c), st.tok[HS[h], 0, c, :], st.XX[HS[h], 1, c, :]))
                        two_heads(lambda h, c: mm(place(st.QB, 1, h, c), st.SB2[HS[h], c, 0, :], st.tok[HS[h], 3, c, :])).then_inc(GW_done, 1)
                    for st in streams:
                        pe.wait_ge(GW_ready, at(n, st))
                        pe.sem_inc(on_pe, 1)
                    for c in range(NC):
                        cs = slice(c * C, (c + 1) * C)
                        for st in streams:
                            pe.wait_ge(S_ready, i * (2 + NG * NC * 2) + at(g, st, NC, c))
                            pe.sem_inc(on_pe, 1)
                            for h in range(2):
                                mm(st.QA[HS[h], h, 0:C], st.XX[HS[h], 1, c, :], st.GW[HS[h], 1, c, :], stop=False)
                                done = mm(st.QA[HS[h], h, 0:C], st.GW[HS[h], 0, c, :], st.S[HS[h], :], start=False)
                            done.then_inc(sa_done, 1)
                            for h in range(2):
                                mm(st.QB[HS[h], h, cs], st.tok[HS[h], 3, c, :], st.SB2[HS[h], c, 1, :], stop=False)
                                mm(st.QB[HS[h], h, cs], st.S[HS[h], :], st.r_t[HS[h], c, :], start=False, stop=False)
                        for st in streams:
                            pe.wait_ge(saA_ready, at(n, st, NC, c))
                            pe.sem_inc(on_pe, 1)
                            pe.wait_ge(saB_ready, at(n, st, NC, c))
                            pe.sem_inc(on_pe, 1)
                            for h in range(2):
                                mm(st.QA[HS[h], h, C:2 * C], st.tok[HS[h], 2, c, :], st.tok[HS[h], 3, c, :], stop=False)
                                done = mm(st.QA[HS[h], h, C:2 * C], st.tok[HS[h], 1, c, :], st.SA[HS[h], :], start=False)
                            done.then_inc(dS_done, 1)
                            for h in range(2):
                                done = mm(st.QB[HS[h], h, cs], st.SA[HS[h], :], st.SB1[HS[h], c, 1, :], start=False)
                            if c == NC - 1:
                                done.then_inc(y_done, 1)
                    for st in streams:
                        pe.wait_ge(S_ready, i * (2 + NG * NC * 2) + at(g, st, NC, NC))
                        pe.sem_inc(on_pe, 1)
                        pe.wait_ge(y_ready, at(n, st))
                        pe.sem_inc(on_pe, 1)
                        mm(st.QA[:, 0, :], head_ones[:, :], st.y[:, :]).then_inc(mean_done, 1)
                    for st in streams:
                        pe.wait_ge(gate_ready, n + 1)
                        pe.sem_inc(on_pe, 1)
                        pe.wait_ge(lnw_loaded, n * (16 * N_LNW) + 16 * N_LNW)
                        pe.sem_inc(on_pe, 1)
                        mm(st.QB[:, 0, :], st.g_up[:, :], gd[:, :]).then_inc(g_done, 1)
                    for st in streams:
                        pe.wait_ge(centred_ready, at(n, st))
                        pe.sem_inc(on_pe, 1)
                        mm(st.QA[:, 1, :], head_ones[:, :], st.dev[:, :]).then_inc(var_done, 1)

                pe.wait_ge(consts, N_CONSTS)
                for k in range(PRE):
                    for st in streams:
                        if k > 0:
                            pe.wait_ge(pre_read, at(0, st, PRE, k - 1))
                        prepare(0, st, k)
                for st in streams:
                    pe.wait_ge(pre_read, at(0, st, PRE, PRE - 1))
                with pe.Fori(0, N2) as i:
                    with pe.Fori(0, NG) as g:
                        group(i, g)


class ExpertWeights:

    def __init__(self, nc, ctx, program, w_g, w_u, w_d):
        sb, _, sem = makers(nc, ctx, program)
        self.dram = (w_g, w_u, w_d)
        self.wg = sb("wg", [P, 2, KT, FF])
        self.wu = sb("wu", [P, 2, KT, FF])
        self.wd = sb("wd7", [P, 2, FF // P, D])
        self.gu_loaded = [sem(f"gu_loaded{s}") for s in range(2)]
        self.d_loaded = [sem(f"d_loaded{s}") for s in range(2)]

    def load(self, sp, e, s):
        w_g, w_u, w_d = self.dram
        for to, src in ((self.wg, w_g), (self.wu, w_u)):
            sp.dma_start(to[:, s, :, :], src[0, bass.ds(e, 1), :, :].rearrange("o (p k) f -> p (o k) f", p=P)).then_inc(self.gu_loaded[s], 16)
        sp.dma_start(self.wd[:, s, :, :], w_d[0, bass.ds(e, 1), :, :].rearrange("o (f p) d -> p (o f) d", p=P)).then_inc(self.d_loaded[s], 16)


def mix_out_and_route(nc, program, E_all, ranks, gates, totals, x, w_out, norm2_gain, w_rg, w_re, experts, mixT_dram, x1_dram, h2_dram):
    with ExitStack() as ctx:
        sb, pb, sem = makers(nc, ctx, program)
        NL = N_GROUPS + NE
        w_sb = sb("wo_sb", [P, KT, D])
        w_r = sb("w_r", [P, KT, NL])
        gain = sb("gain2", [P, D])
        mixT = sb("mixT_t", [P, 2, KT, P])
        x_t = sb("x_t5", [P, 2, D])
        h2 = sb("h2_t", [P, 2, D])
        h2T = sb("h2T", [P, KT, P])
        squares = sb("squares5", [P, D])
        ssum, root, rstd = [sb(n, [P, 1]) for n in ("ssum5", "root5", "rstd5")]
        eps = sb("eps5", [P, 1])
        ident = sb("ident5", [P, P])
        earlier = sb("earlier", [P, P])
        ones = sb("ones5", [P, P])
        iota_i = sb("iota_i", [P, NE], I32)
        iota = sb("iota_f", [P, NE])
        lg = sb("lg", [P, NL])
        gl8 = sb("gl8", [P, 8])
        gmax8, emax8 = sb("gmax8", [P, 8]), sb("emax8", [P, 8])
        gidx8, eidx8 = sb("gidx8", [P, 8], U32), sb("eidx8", [P, 8], U32)
        negmax, gidx, gidx_8, gsum, ggate = [sb(n, [P, 1]) for n in ("negmax", "gidx", "gidx_8", "gsum", "ggate")]
        gexp = sb("gexp", [P, N_GROUPS])
        onehot = sb("onehot", [P, N_GROUPS])
        sel = sb("sel", [P, N_GROUPS, PER_GROUP])
        in_group = sb("in_group", [P, PER_GROUP])
        lead, share, eidx, eid = [sb(n, [P, 2]) for n in ("lead", "share", "eidx", "eid")]
        E = sb("E", [P, 2, 2, NE])
        both = sb("both", [P, 2, NE])
        before = sb("before", [P, NE])
        picked = sb("picked", [P, 2, NE])
        o_ps = pb("o_ps5", [P, 2, 2, 512])
        hT_ps = pb("hT_ps5", [P, KT, P])
        lg_ps = pb("lg_ps", [P, 512])
        rank_ps = pb("rank_ps", [P, 512])

        names = """weights consts x1_ready rooted h2_ready turned hT_copied mixed logits_done routed_group
            gates_wanted exped shared picks_ready ranked ranks_ready counted""".split()
        (weights, consts, x1_ready, rooted, h2_ready, turned, hT_copied, mixed, logits_done, routed_group,
         gates_wanted, exped, shared, picks_ready, ranked, ranks_ready, counted) = [sem(f"p5_{n}") for n in names]
        loaded = [sem(f"p5_loaded{s}") for s in range(2)]
        stored = [sem(f"p5_stored{s}") for s in range(2)]
        on_sp, on_act, on_pe, on_dve, on_pool = program.gates_passed
        mixT_v = mixT_dram.rearrange("(k p) t -> p k t", p=P)
        give_credit(nc, hT_copied, routed_group, x1_ready, ranks_ready)
        with nc.Block() as block:
            @block.sync
            def _(sp):
                def load(t, s):
                    sp.dma_start(mixT[:, s, :, :], mixT_v[:, :, bass.ds(t * P, P)]).then_inc(loaded[s], 16)
                    sp.dma_start(x_t[:, s, :], x[0, bass.ds(t * P, P), :]).then_inc(loaded[s], 16)

                def store(t, s):
                    sp.wait_ge(h2_ready, t + 1)
                    sp.dma_start(x1_dram[bass.ds(t * P, P), :], x_t[:, s, :]).then_inc(stored[s], 16)
                    sp.dma_start(h2_dram[bass.ds(t * P, P), :], h2[:, s, :]).then_inc(stored[s], 16)

                load(0, 0)
                load(1, 1)
                sp.dma_start(w_sb[:, :, :], w_out[0].rearrange("(k p) c -> p k c", p=P)).then_inc(weights, 16)
                sp.dma_start(w_r[:, :, 0:N_GROUPS], w_rg[0].rearrange("(k p) c -> p k c", p=P)).then_inc(weights, 16)
                sp.dma_start(w_r[:, :, N_GROUPS:NL], w_re[0].rearrange("(k p) c -> p k c", p=P)).then_inc(weights, 16)
                sp.dma_start(gain[:, :], norm2_gain[0, :].partition_broadcast(P)).then_inc(weights, 16)
                experts.load(sp, 0, 0)
                experts.load(sp, 1, 1)
                with sp.Fori(0, NT // 2 - 1) as i:
                    for s in range(2):
                        t = i * 2 + s
                        store(t, s)
                        sp.wait_ge(stored[s], i * 32 + 32)
                        load(t + 2, s)
                for s in range(2):
                    store(NT - 2 + s, s)
                for s in range(2):
                    sp.wait_ge(stored[s], 16 * NT)

            @block.gpsimd
            def _(pool):
                identity(pool, ident[:, :])
                pool.memset(eps[:, :], NORM_EPS)
                pool.memset(ones[:, :], 1.0)
                pool.memset(earlier[:, :], 1.0)
                pool.memset(gl8[:, :], -3.4e38)
                pool.memset(before[:, :], 0.0)
                pool.iota(iota_i[:, :], pattern=[[1, NE]], base=0, channel_multiplier=0)
                pool.drain()
                pool.affine_select(out=earlier[:, :], in_=earlier[:, :], compare_op=ALU.is_gt, fill=0.0, base=0,
                                   pattern=[[1, P]], channel_multiplier=-1)
                pool.tensor_copy(iota[:, :], iota_i[:, :])
                pool.drain()
                pool.sem_inc(consts, 1)

            def tile_pairs(eng, one_tile):
                for s in range(2):
                    one_tile(s, s, 0, first=(s == 0), last=False)
                with eng.Fori(1, NT // 2 - 1) as i:
                    for s in range(2):
                        one_tile(i * 2 + s, s, i, first=False, last=False)
                for s in range(2):
                    one_tile(NT - 2 + s, s, NT // 2 - 1, first=False, last=(s == 1))

            @block.tensor
            def _(pe):
                def mix(t, s, n):
                    pe.wait_ge(loaded[s], n * 32 + 32)
                    pe.wait_ge(x1_ready, CREDIT + t - 1)
                    for half in range(2):
                        for k in range(KT):
                            done = pe.matmul(o_ps[:, s, half, :], mixT[:, s, k, :], w_sb[:, k, half * 512:(half + 1) * 512],
                                             start=(k == 0), stop=(k == KT - 1))
                    done.then_inc(mixed, 1)

                def rank(t, s):
                    pe.wait_ge(picks_ready, t + 1)
                    pe.wait_ge(ranks_ready, CREDIT + t)
                    pe.matmul(rank_ps[:, 0:NE], earlier[:, :], both[:, s, :], start=True, stop=False)
                    pe.matmul(rank_ps[:, 0:NE], ones[:, :], before[:, :], start=False, stop=True).then_inc(ranked, 1)

                def one_tile(t, s, n, first, last):
                    if not last:
                        mix(t + 1, 1 - s, n + s)
                    if not first:
                        rank(t - 1, 1 - s)
                    pe.wait_ge(h2_ready, t + 1)
                    pe.wait_ge(hT_copied, CREDIT + t)
                    for k in range(KT):
                        done = pe.transpose(hT_ps[:, k, :], h2[:, s, k * P:(k + 1) * P], ident[:, :])
                    done.then_inc(turned, 1)
                    pe.wait_ge(hT_copied, CREDIT + t + 1)
                    pe.wait_ge(routed_group, CREDIT + t)
                    for k in range(KT):
                        done = pe.matmul(lg_ps[:, 0:NL], h2T[:, k, :], w_r[:, k, :], start=(k == 0), stop=(k == KT - 1))
                    done.then_inc(logits_done, 1)

                pe.wait_ge(consts, 1)
                pe.wait_ge(weights, 64)
                mix(0, 0, 0)
                tile_pairs(pe, one_tile)
                rank(NT - 1, 1)
                pe.wait_ge(ranks_ready, CREDIT + NT)
                pe.matmul(rank_ps[:, 0:NE], ones[:, :], before[:, :], start=True, stop=True).then_inc(counted, 1)

            @block.scalar
            def _(act):
                act.wait_ge(consts, 1)
                with act.Fori(0, NT // 2) as i:
                    for s in range(2):
                        t = i * 2 + s
                        act.wait_ge(x1_ready, CREDIT + t + 1)
                        act.activation(squares[:, :], x_t[:, s, :], ACT.Square, accum_out=ssum[:, :])
                        act.drain()
                        act.activation(root[:, :], ssum[:, :], ACT.Sqrt, bias=eps[:, :], scale=1.0 / D).then_inc(rooted, 1)
                        act.wait_ge(turned, t + 1)
                        act.copy(h2T[:, :, :], hT_ps[:, :, :]).then_inc(hT_copied, 1)
                        act.wait_ge(routed_group, CREDIT + t + 1)
                        act.activation(gexp[:, :], gl8[:, 0:N_GROUPS], ACT.Exp, bias=negmax[:, :], accum_out=gsum[:, :])
                        act.drain()
                        act.sem_inc(exped, 1)
                        act.wait_ge(gates_wanted, t + 1)
                        act.activation(share[:, :], lead[:, :], ACT.Sigmoid).then_inc(shared, 1)

            @block.vector
            def _(dve):
                def finish(t, s):
                    dve.wait_ge(ranked, t + 1)
                    dve.tensor_tensor(picked[:, :, :], E[:, s, :, :], rank_ps[:, 0:NE].unsqueeze(1).to_broadcast([P, 2, NE]), ALU.mult)
                    dve.drain()
                    dve.reduce_sum(ranks[:, bass.ds(t * 2, 2)], picked[:, :, :], axis=AX_X)
                    dve.tensor_tensor(before[:, :], before[:, :], both[:, s, :], ALU.add).then_inc(ranks_ready, 1)
                    dve.drain()

                def one_tile(t, s, n, first, last):
                    dve.wait_ge(mixed, t + 1)
                    dve.tensor_tensor(x_t[:, s, :], x_t[:, s, :], o_ps[:, s, :, :].rearrange("p a b -> p (a b)"), ALU.add).then_inc(x1_ready, 1)
                    dve.wait_ge(rooted, t + 1)
                    dve.reciprocal(rstd[:, :], root[:, :])
                    dve.drain()
                    dve.scalar_tensor_tensor(h2[:, s, :], x_t[:, s, :], rstd[:, :], gain[:, :], ALU.mult, ALU.mult).then_inc(h2_ready, 1)
                    if not first:
                        finish(t - 1, 1 - s)
                    dve.wait_ge(logits_done, t + 1)
                    dve.tensor_copy(lg[:, :], lg_ps[:, 0:NL])
                    dve.tensor_copy(gl8[:, 0:N_GROUPS], lg_ps[:, 0:N_GROUPS])
                    dve.drain()
                    dve.max(gmax8[:, :], gl8[:, :])
                    dve.drain()
                    dve.max_index(gidx8[:, :], gmax8[:, :], gl8[:, :])
                    dve.tensor_scalar(negmax[:, :], gmax8[:, 0:1], -1.0, None, ALU.mult).then_inc(routed_group, 1)
                    dve.drain()
                    dve.tensor_copy(gidx[:, :], gidx8[:, 0:1])
                    dve.drain()
                    dve.tensor_scalar(onehot[:, :], iota[:, 0:N_GROUPS], gidx[:, :], None, ALU.is_equal)
                    dve.tensor_scalar(gidx_8[:, :], gidx[:, :], float(PER_GROUP), None, ALU.mult)
                    dve.drain()
                    dve.tensor_tensor(sel[:, :, :], lg[:, N_GROUPS:NL].rearrange("p (g e) -> p g e", g=N_GROUPS),
                                      onehot[:, :].unsqueeze(2).to_broadcast([P, N_GROUPS, PER_GROUP]), ALU.mult)
                    dve.drain()
                    dve.reduce_sum(in_group[:, :], sel[:, :, :].rearrange("p g e -> p e g"), axis=AX_X)
                    dve.drain()
                    dve.max(emax8[:, :], in_group[:, :])
                    dve.drain()
                    dve.max_index(eidx8[:, :], emax8[:, :], in_group[:, :])
                    dve.tensor_tensor(lead[:, 0:1], emax8[:, 0:1], emax8[:, 1:2], ALU.subtract)
                    dve.tensor_tensor(lead[:, 1:2], emax8[:, 1:2], emax8[:, 0:1], ALU.subtract).then_inc(gates_wanted, 1)
                    dve.drain()
                    dve.tensor_copy(eidx[:, :], eidx8[:, 0:2])
                    dve.drain()
                    dve.tensor_scalar(eid[:, :], eidx[:, :], gidx_8[:, :], None, ALU.add)
                    dve.drain()
                    dve.tensor_tensor(E[:, s, :, :], iota[:, :].unsqueeze(1).to_broadcast([P, 2, NE]),
                                      eid[:, :].unsqueeze(2).to_broadcast([P, 2, NE]), ALU.is_equal)
                    dve.drain()
                    dve.tensor_tensor(both[:, s, :], E[:, s, 0, :], E[:, s, 1, :], ALU.add).then_inc(picks_ready, 1)
                    dve.tensor_copy(E_all[:, bass.ds(t * 2, 2), :], E[:, s, :, :])
                    dve.wait_ge(exped, t + 1)
                    dve.reciprocal(ggate[:, :], gsum[:, :])
                    dve.drain()
                    dve.wait_ge(shared, t + 1)
                    dve.tensor_scalar(gates[:, bass.ds(t * 2, 2)], share[:, :], ggate[:, :], None, ALU.mult)

                dve.wait_ge(consts, 1)
                dve.wait_ge(weights, 64)
                tile_pairs(dve, one_tile)
                finish(NT - 1, 1)
                dve.wait_ge(counted, 1)
                dve.tensor_copy(totals[:, :], rank_ps[:, 0:NE])
                dve.drain()


def place_slots(nc, program, E_all, ranks, totals, n_blocks, first_block, row_slot):
    with ExitStack() as ctx:
        sb, pb, sem = makers(nc, ctx, program)
        up = sb("up", [P, NE])
        blocks_i = sb("blocks_i", [P, NE], I32)
        blocks, ends, starts = [sb(n, [P, NE]) for n in ("blocks", "ends", "starts")]
        rows_of = sb("rows_of", [P, 2 * NT, NE])
        row = sb("row", [P, 2 * NT])
        row_i, block_i, part_i = [sb(n, [P, 2 * NT], I32) for n in ("row_i", "block_i", "part_i")]
        block_f, part_f = [sb(n, [P, 2 * NT]) for n in ("block_f", "part_f")]
        cell = sb("cell", [P, 2 * NT], U32)
        ones = sb("ones6", [P, NE])
        slot = sb("slot", [P, NT, 2], I32)
        spare = sb("spare", [P, TABLE], I32)
        consts, placed, cleared, scattered, begun = [sem(f"p6_{n}") for n in ("consts", "placed", "cleared", "scattered", "begun")]
        with nc.Block() as block:
            @block.gpsimd
            def _(pool):
                pool.memset(ones[:, :], 1.0)
                pool.iota(spare[:, :], pattern=[[1, TABLE]], base=2 * SEQ, channel_multiplier=TABLE)
                pool.iota(slot[:, :, :], pattern=[[2 * P, NT], [1, 2]], base=0, channel_multiplier=2)
                pool.drain()
                pool.sem_inc(consts, 1)
                pool.wait_ge(cleared, 16)
                pool.wait_ge(placed, 1)
                for t in range(NT):
                    for k in range(2):
                        col = 2 * t + k
                        pool.indirect_dma_start(out=row_slot[:, :], out_offset=bass.IndirectOffsetOnAxis(ap=cell[:, col:col + 1], axis=0),
                                                in_=slot[:, t, k:k + 1], in_offset=None).then_inc(scattered, 16)
                pool.wait_ge(scattered, 16 * 2 * NT)

            @block.sync
            def _(sp):
                sp.wait_ge(consts, 1)
                sp.dma_start(row_slot.rearrange("(p c) o -> p (c o)", p=P), spare[:, :]).then_inc(cleared, 16)

            @block.vector
            def _(dve):
                dve.wait_ge(consts, 1)
                dve.tensor_scalar(up[:, :], totals[:, :], float(P - 1), None, ALU.add)
                dve.drain()
                dve.tensor_copy(blocks_i[:, :], up[:, :])
                dve.drain()
                dve.tensor_scalar(blocks_i[:, :], blocks_i[:, :], P.bit_length() - 1, None, ALU.arith_shift_right)
                dve.drain()
                dve.tensor_copy(blocks[:, :], blocks_i[:, :])
                dve.drain()
                dve.tensor_scalar(blocks[:, :], blocks[:, :], 1.0, None, ALU.max)
                dve.drain()
                dve.tensor_tensor_scan(ends[:, :], ones[:, :], blocks[:, :], 0.0, ALU.mult, ALU.add)
                dve.drain()
                dve.tensor_tensor(starts[:, :], ends[:, :], blocks[:, :], ALU.subtract)
                dve.tensor_copy(n_blocks[:, :], blocks[:, :])
                dve.drain()
                dve.tensor_copy(first_block[:, :], starts[:, :])
                dve.tensor_scalar(starts[:, :], starts[:, :], float(P), None, ALU.mult)
                dve.drain()
                dve.tensor_tensor(rows_of[:, :, :], E_all[:, :, :], starts[:, :].unsqueeze(1).to_broadcast([P, 2 * NT, NE]), ALU.mult)
                dve.drain()
                dve.reduce_sum(row[:, :], rows_of[:, :, :], axis=AX_X)
                dve.drain()
                dve.tensor_tensor(row[:, :], row[:, :], ranks[:, :], ALU.add)
                dve.drain()
                dve.tensor_copy(row_i[:, :], row[:, :])
                dve.drain()
                dve.tensor_scalar(block_i[:, :], row_i[:, :], P.bit_length() - 1, None, ALU.arith_shift_right)
                dve.tensor_scalar(part_i[:, :], row_i[:, :], P - 1, None, ALU.bitwise_and)
                dve.drain()
                dve.tensor_copy(block_f[:, :], block_i[:, :])
                dve.tensor_copy(part_f[:, :], part_i[:, :])
                dve.drain()
                dve.scalar_tensor_tensor(row[:, :], part_f[:, :], float(TABLE), block_f[:, :], ALU.mult, ALU.add)
                dve.drain()
                dve.tensor_copy(cell[:, :], row[:, :])
                dve.drain()
                dve.sem_inc(placed, 1)


def run_experts(nc, program, n_blocks, first_block, row_slot, experts, h2_dram, y_dram):
    with ExitStack() as ctx:
        sb, pb, sem = makers(nc, ctx, program)
        FT = FF // P
        FH = FF // 2
        wg, wu, wd = experts.wg, experts.wu, experts.wd
        gu_loaded, d_loaded = experts.gu_loaded, experts.d_loaded
        slot_all = sb("slot_all", [P, TABLE], I32)
        tok_all = sb("tok_all", [P, TABLE], I32)
        tok = sb("tok7", [P, 1], I32)
        slot = sb("slot7", [P, 1], I32)
        xg = sb("xg", [P, D])
        xT = sb("xT", [P, KT, P])
        sil = sb("sil", [P, FF])
        h = sb("h7", [P, FF])
        hT = sb("hT7", [P, FT, P])
        y = sb("y7", [P, D])
        ident = sb("ident7", [P, P])
        xT_ps = pb("xT_ps7", [P, KT, P])
        g_ps = pb("g_ps7", [P, FF])
        u_ps = pb("u_ps7", [P, 2, 512])
        hT_ps = pb("hT_ps7", [P, FT, P])
        y_ps = pb("y_ps7", [P, D])
        names = """consts slots_loaded tok_ready gathered turned xT_ready g_done u_done silu_ready h_ready h_turned hT_ready
            y_done y_copied expert_done stored y_free""".split()
        (consts, slots_loaded, tok_ready, gathered, turned, xT_ready, g_done, u_done, silu_ready, h_ready, h_turned, hT_ready,
         y_done, y_copied, expert_done, stored, y_free) = [sem(f"p7_{n}") for n in names]
        on_sp, on_act, on_pe, on_dve, on_pool = program.gates_passed

        def blocks_of(eng, e):
            count = eng.value_load(n_blocks[0:1, bass.ds(e, 1)], min_val=1, max_val=SEQ // P)
            start = eng.value_load(first_block[0:1, bass.ds(e, 1)], min_val=0, max_val=MAX_BLOCKS - 1)
            return count, start

        give_credit(nc, h_ready, h_turned, silu_ready, y_free, y_copied)
        with nc.Block() as block:
            @block.sync
            def _(sp):
                sp.dma_start(slot_all[:, :], row_slot.rearrange("(p b) o -> p (b o)", p=P)).then_inc(slots_loaded, 16)
                def pass_stores(e):
                    count, start = blocks_of(sp, e)
                    with sp.Fori(0, count) as i:
                        sp.wait_ge(stored, (start + i) * 16 + 16)
                        sp.sem_inc(y_free, 1)

                with sp.Fori(0, NE // 2 - 1) as i2:
                    for s in range(2):
                        e = i2 * 2 + s
                        pass_stores(e)
                        sp.wait_ge(expert_done, e + 1)
                        experts.load(sp, e + 2, s)
                for e in (NE - 2, NE - 1):
                    pass_stores(e)

            @block.gpsimd
            def _(pool):
                identity(pool, ident[:, :])
                pool.drain()
                pool.sem_inc(consts, 1)
                pool.wait_ge(tok_ready, 1)

                def gather(b):
                    pool.tensor_copy(tok[:, :], tok_all[:, bass.ds(b, 1)])
                    pool.drain()
                    pool.indirect_dma_start(out=xg[:, :], out_offset=None, in_=h2_dram[:, :],
                                            in_offset=bass.IndirectOffsetOnAxis(ap=tok[:, 0:1], axis=0)).then_inc(gathered, 16)

                gather(0)
                pool.wait_ge(turned, 1)
                gather(1)
                with pool.Fori(0, NE) as e:
                    count, start = blocks_of(pool, e)
                    with pool.Fori(0, count) as i:
                        b = start + i
                        pool.wait_ge(turned, b + 2)
                        pool.sem_inc(on_pool, 1)
                        gather(b + 2)
                        pool.wait_ge(y_free, CREDIT + b)
                        pool.sem_inc(on_pool, 1)
                        pool.tensor_copy(slot[:, :], slot_all[:, bass.ds(b, 1)])
                        pool.drain()
                        pool.wait_ge(y_copied, CREDIT + b * 2 + 2)
                        pool.sem_inc(on_pool, 1)
                        pool.indirect_dma_start(out=y_dram[:, :], out_offset=bass.IndirectOffsetOnAxis(ap=slot[:, 0:1], axis=0),
                                                in_=y[:, :], in_offset=None).then_inc(stored, 16)
                pool.drain()

            @block.tensor
            def _(pe):
                def turn(b):
                    pe.wait_ge(gathered, b * 16 + 16)
                    for k in range(KT):
                        last = pe.transpose(xT_ps[:, k, :], xg[:, :].rearrange("t (p k) -> t k p", k=KT)[:, k, :], ident[:, :])
                    last.then_inc(turned, 1)

                def one_block(b, s):
                    pe.wait_ge(xT_ready, b * 2 + 2)
                    pe.wait_ge(silu_ready, CREDIT + b)
                    for k in range(KT):
                        last = pe.matmul(g_ps[:, :], xT[:, k, :], wg[:, s, k, :], start=(k == 0), stop=(k == KT - 1))
                    last.then_inc(g_done, 1)
                    pe.wait_ge(h_ready, CREDIT + b * 2)
                    for half in range(2):
                        for k in range(KT):
                            last = pe.matmul(u_ps[:, half, 0:FH], xT[:, k, :], wu[:, s, k, half * FH:(half + 1) * FH],
                                             start=(k == 0), stop=(k == KT - 1))
                        last.then_inc(u_done, 1)

                    def turn_h(half):
                        pe.wait_ge(h_ready, CREDIT + b * 2 + half + 1)
                        for f in range(2 * half, 2 * half + 2):
                            done = pe.transpose(hT_ps[:, f, :], h[:, f * P:(f + 1) * P], ident[:, :])
                        done.then_inc(h_turned, 1)

                    turn_h(0)
                    turn(b + 1)
                    pe.wait_ge(hT_ready, b * 2 + 1)
                    turn_h(1)
                    pe.wait_ge(y_copied, CREDIT + b * 2)
                    for fh in range(2):
                        if fh == 1:
                            pe.wait_ge(hT_ready, b * 2 + 2)
                        for half in range(2):
                            for f in range(2 * fh, 2 * fh + 2):
                                last = pe.matmul(y_ps[:, half * 512:(half + 1) * 512], hT[:, f, :], wd[:, s, f, half * 512:(half + 1) * 512],
                                                 start=(f == 0), stop=(f == FT - 1))
                            if fh == 1:
                                last.then_inc(y_done, 1)

                pe.wait_ge(consts, 1)
                turn(0)
                with pe.Fori(0, NE // 2) as i2:
                    for s in range(2):
                        e = i2 * 2 + s
                        count, start = blocks_of(pe, e)
                        pe.wait_ge(gu_loaded[s], i2 * 32 + 32)
                        pe.wait_ge(d_loaded[s], i2 * 16 + 16)
                        pe.sem_inc(on_pe, 1)
                        with pe.Fori(0, count) as i:
                            one_block(start + i, s)
                        pe.drain()
                        pe.sem_inc(expert_done, 1)

            @block.scalar
            def _(act):
                def copy_xT(b):
                    act.wait_ge(turned, b + 1)
                    act.copy(xT[:, 0:KT // 2, :], xT_ps[:, 0:KT // 2, :]).then_inc(xT_ready, 1)

                copy_xT(0)
                with act.Fori(0, NE) as e:
                    count, start = blocks_of(act, e)
                    with act.Fori(0, count) as i:
                        b = start + i
                        act.wait_ge(g_done, b + 1)
                        act.wait_ge(h_ready, CREDIT + b * 2)
                        act.activation(sil[:, :], g_ps[:, :], ACT.Silu).then_inc(silu_ready, 1)
                        act.wait_ge(h_turned, CREDIT + b * 2 + 1)
                        act.copy(hT[:, 0:2, :], hT_ps[:, 0:2, :]).then_inc(hT_ready, 1)
                        copy_xT(b + 1)
                        act.wait_ge(h_turned, CREDIT + b * 2 + 2)
                        act.copy(hT[:, 2:4, :], hT_ps[:, 2:4, :]).then_inc(hT_ready, 1)
                        act.wait_ge(y_done, b * 2 + 1)
                        act.wait_ge(y_free, CREDIT + b)
                        act.copy(y[:, 0:512], y_ps[:, 0:512]).then_inc(y_copied, 1)

            @block.vector
            def _(dve):
                def copy_xT(b):
                    dve.wait_ge(turned, b + 1)
                    dve.tensor_copy(xT[:, KT // 2:KT, :], xT_ps[:, KT // 2:KT, :]).then_inc(xT_ready, 1)

                dve.wait_ge(slots_loaded, 16)
                dve.tensor_scalar(tok_all[:, :], slot_all[:, :], 2 * SEQ - 1, None, ALU.min)
                dve.drain()
                dve.tensor_scalar(tok_all[:, :], tok_all[:, :], 1, None, ALU.arith_shift_right).then_inc(tok_ready, 1)
                copy_xT(0)
                with dve.Fori(0, NE) as e:
                    count, start = blocks_of(dve, e)
                    with dve.Fori(0, count) as i:
                        b = start + i
                        dve.wait_ge(silu_ready, CREDIT + b + 1)
                        dve.wait_ge(h_turned, CREDIT + b * 2)
                        for half in range(2):
                            cols = slice(half * FH, (half + 1) * FH)
                            dve.wait_ge(u_done, b * 2 + half + 1)
                            dve.tensor_tensor(h[:, cols], sil[:, cols], u_ps[:, half, 0:FH], ALU.mult).then_inc(h_ready, 1)
                        copy_xT(b + 1)
                        dve.wait_ge(y_done, b * 2 + 2)
                        dve.wait_ge(y_free, CREDIT + b)
                        dve.tensor_copy(y[:, 512:1024], y_ps[:, 512:1024]).then_inc(y_copied, 1)


def combine(nc, program, gates, x1_dram, y_dram, out):
    with ExitStack() as ctx:
        sb, pb, sem = makers(nc, ctx, program)
        rows = sb("rows8", [P, 2, 2, D])
        x1 = sb("x1_8", [P, 2, D])
        gate_t = sb("gate_t", [P, 2, 2])
        loaded = [sem(f"p8_loaded{s}") for s in range(2)]
        stored = [sem(f"p8_stored{s}") for s in range(2)]
        summed = sem("p8_summed")
        on_sp, on_act, on_pe, on_dve, on_pool = program.gates_passed
        y_tiles = y_dram[0:2 * SEQ, :].rearrange("(t k) d -> t (k d)", k=2)
        with nc.Block() as block:
            @block.sync
            def _(sp):
                def load(t, s):
                    sp.dma_start(x1[:, s, :], x1_dram[bass.ds(t * P, P), :]).then_inc(loaded[s], 16)
                    sp.dma_start(rows[:, s, :, :].rearrange("p k d -> p (k d)"), y_tiles[bass.ds(t * P, P), :]).then_inc(loaded[s], 16)

                def store(t, s):
                    sp.wait_ge(summed, t + 1)
                    sp.dma_start(out[0, bass.ds(t * P, P), :], x1[:, s, :]).then_inc(stored[s], 16)

                load(0, 0)
                load(1, 1)
                with sp.Fori(0, NT // 2 - 1) as i:
                    for s in range(2):
                        t = i * 2 + s
                        store(t, s)
                        sp.wait_ge(stored[s], i * 16 + 16)
                        load(t + 2, s)
                for s in range(2):
                    store(NT - 2 + s, s)
                for s in range(2):
                    sp.wait_ge(stored[s], 8 * NT)

            @block.vector
            def _(dve):
                with dve.Fori(0, NT // 2) as i:
                    for s in range(2):
                        t = i * 2 + s
                        dve.tensor_copy(gate_t[:, s, :], gates[:, bass.ds(t * 2, 2)])
                        dve.drain()
                        dve.wait_ge(loaded[s], i * 32 + 32)
                        dve.scalar_tensor_tensor(rows[:, s, 0, :], rows[:, s, 0, :], gate_t[:, s, 0:1], x1[:, s, :], ALU.mult, ALU.add)
                        dve.drain()
                        dve.scalar_tensor_tensor(x1[:, s, :], rows[:, s, 1, :], gate_t[:, s, 1:2], rows[:, s, 0, :], ALU.mult, ALU.add).then_inc(summed, 1)


def hybrid_block(nc, x, norm1_gain, w_in, sb_q_gain, sb_k_gain, rw_shift_mu, rw_w0, rw_w_up, rw_a0, rw_a_up, rw_g_up,
                 rw_k_k, rw_k_a, rw_r_k, rw_ln_w, rw_ln_b, w_out, norm2_gain, w_router_group, w_router_expert,
                 w_exp_gate, w_exp_up, w_exp_down, out):
    def dram(name, shape, dt=F32):
        return nc.dram_tensor(name, shape, dt, kind="Internal").ap()

    qT, kT, v = dram("qT", (SBW, SEQ)), dram("kT", (SBW, SEQ)), dram("v", (SEQ, SBW))
    pT = dram("pT", (RW_COLS, SEQ))
    mixT = dram("mixT", (D, SEQ))
    x1, h2 = dram("x1", (SEQ, D)), dram("h2", (SEQ, D))
    row_slot = dram("row_slot", (TABLE * P, 1), I32)
    y = dram("y", (2 * SEQ + TABLE * P, D))
    with ExitStack() as stack:
        program = Program(nc, stack)
        with nc.sbuf_tensor("h_all", [P, KT, SEQ], F32) as h_all:
            project_tokens(nc, program, h_all, x, norm1_gain, w_in, sb_q_gain, sb_k_gain, qT, kT, v)
            project_channels(nc, program, h_all, w_in, rw_shift_mu, pT)
        stick_breaking(nc, program, qT, kT, v, mixT)
        time_mixing(nc, program, rw_w0, rw_w_up, rw_a0, rw_a_up, rw_g_up, rw_k_k, rw_k_a, rw_r_k, rw_ln_w, rw_ln_b, pT, mixT)
        with ExitStack() as ctx:
            sb, _, _ = makers(nc, ctx, program)
            gates = sb("gates", [P, 2 * NT])
            n_blocks, first_block = sb("n_blocks", [P, NE], I32), sb("first_block", [P, NE], I32)
            experts = ExpertWeights(nc, ctx, program, w_exp_gate, w_exp_up, w_exp_down)
            with ExitStack() as routing:
                sb, _, _ = makers(nc, routing, program)
                E_all, ranks, totals = sb("E_all", [P, 2 * NT, NE]), sb("ranks", [P, 2 * NT]), sb("totals", [P, NE])
                mix_out_and_route(nc, program, E_all, ranks, gates, totals, x, w_out, norm2_gain, w_router_group, w_router_expert, experts, mixT, x1, h2)
                place_slots(nc, program, E_all, ranks, totals, n_blocks, first_block, row_slot)
            run_experts(nc, program, n_blocks, first_block, row_slot, experts, h2, y)
            combine(nc, program, gates, x1, y, out)


_INPUTS = ("x norm1_gain w_in sb_q_gain sb_k_gain rw_shift_mu rw_w0 rw_w_up rw_a0 rw_a_up rw_g_up rw_k_k rw_k_a rw_r_k "
           "rw_ln_w rw_ln_b w_out norm2_gain w_router_group w_router_expert w_exp_gate w_exp_up w_exp_down").split()


def kernel(**inputs):
    import concourse.bacc as bacc
    import numpy as np
    from concourse.bass_utils import run_bass_kernel_spmd

    nc = bacc.Bacc("TRN2", target_bir_lowering=False, num_devices=1)
    arrays, aps = {}, []
    for name in _INPUTS:
        a = np.ascontiguousarray(inputs[name])
        arrays[f"in_{name}"] = a
        aps.append(nc.dram_tensor(f"in_{name}", a.shape, mybir.dt.from_np(a.dtype), kind="ExternalInput").ap())
    out = nc.dram_tensor("out", (1, SEQ, D), F32, kind="ExternalOutput").ap()
    hybrid_block(nc, *aps, out)
    r = run_bass_kernel_spmd(nc, [arrays], core_ids=[0])
    return r.results[0]["out"]
```

```python
from contextlib import ExitStack

import concourse.bass as bass
from concourse import mybir

F32 = mybir.dt.float32
I32 = mybir.dt.int32
U32 = mybir.dt.uint32
ALU = mybir.AluOpType
ACT = mybir.ActivationFunctionType
AX_X = mybir.AxisListType.X

P = 128
SEQ, D = 2048, 1024
NT = SEQ // P
KT = D // P
HD = 64
SBW = D // 2
SB_COLS = 3 * SBW
LW, LA, LG = 32, 32, 96
RW_COLS = 3 * SBW + LW + LA + LG
IN_COLS = SB_COLS + RW_COLS
PAIRS = SBW // P
N_GROUPS, PER_GROUP = 4, 8
NE = N_GROUPS * PER_GROUP
FF = 512
MAX_BLOCKS = 2 * SEQ // P + NE
TABLE = MAX_BLOCKS + SEQ // P + 1
NORM_EPS, LN_X_EPS = 1e-6, 64e-5
EXP_HALF = 0.6065306597126334


class Program:

    def __init__(self, nc, stack):
        self.stack = stack
        self.gates_passed = [stack.enter_context(nc.semaphore(f"gates_passed_{e}")) for e in "sp act pe dve pool".split()]


CREDIT = 16


def give_credit(nc, *semaphores):
    with nc.Block() as block:
        @block.sync
        def _(sp):
            for s in semaphores:
                sp.sem_inc(s, CREDIT)


def makers(nc, ctx, program):
    def sb(name, shape, dt=F32):
        return ctx.enter_context(nc.sbuf_tensor(name, shape, dt))

    def pb(name, shape):
        return ctx.enter_context(nc.psum_tensor(name, shape, F32))

    def sem(name):
        return program.stack.enter_context(nc.semaphore(name))

    return sb, pb, sem


def identity(pool, tile):
    pool.memset(tile, 0.0)
    pool.drain()
    return pool.affine_select(out=tile, in_=tile, compare_op=ALU.not_equal, fill=1.0, base=0,
                              pattern=[[-1, P]], channel_multiplier=1)


def project_tokens(nc, program, h_all, x, norm1_gain, w_in, sb_q_gain, sb_k_gain, qT_dram, kT_dram, v_dram):
    with ExitStack() as ctx:
        sb, pb, sem = makers(nc, ctx, program)
        w_sb = sb("w_sb", [P, KT, SB_COLS])
        x_t = sb("x_t", [P, 2, D])
        squares = sb("squares", [P, D])
        hT = sb("hT", [P, 2, KT, P])
        gain = sb("gain", [P, KT])
        qkv = sb("qkv", [P, 2, 3, SBW])
        qk_sq = sb("qk_sq", [P, 2 * SBW])
        qkT = sb("qkT", [P, 8, P])
        qk_gain = sb("qk_gain", [P, 2, HD])
        ssum = sb("ssum", [P, 1])
        root = sb("root", [P, 1])
        rstd = sb("rstd", [P, 1])
        qk_sum = sb("qk_sum", [P, 16])
        qk_root = sb("qk_root", [P, 16])
        qk_rstd = sb("qk_rstd", [P, 16])
        eps = sb("eps", [P, 1])
        ident = sb("ident", [P, P])
        xT_ps = pb("xT_ps", [P, KT, P])
        qkv_ps = pb("qkv_ps", [P, 3, SBW])
        qkT_ps = pb("qkT_ps", [P, 8, P])

        consts = sem("p1_consts")
        gains = sem("p1_gains")
        w_loaded = [sem(f"p1_w_loaded{part}") for part in range(3)]
        x_loaded = [sem(f"p1_x_loaded{s}") for s in range(2)]
        rooted = sem("p1_rooted")
        scaled = sem("p1_scaled")
        x_turned = sem("p1_x_turned")
        h_ready = sem("p1_h_ready")
        h_kept = sem("p1_h_kept")
        projected = sem("p1_projected")
        qkv_copied = sem("p1_qkv_copied")
        qk_summed = sem("p1_qk_summed")
        qk_rooted = sem("p1_qk_rooted")
        qk_ready = sem("p1_qk_ready")
        qk_turned = sem("p1_qk_turned")
        qkT_ready = sem("p1_qkT_ready")
        stored = sem("p1_stored")
        on_sp, on_act, on_pe, on_dve, on_pool = program.gates_passed
        qT_v = qT_dram.rearrange("(c p) t -> p c t", p=P)
        kT_v = kT_dram.rearrange("(c p) t -> p c t", p=P)
        give_credit(nc, h_ready, qkT_ready, qk_turned, qkv_copied, scaled, stored)
        with nc.Block() as block:
            @block.sync
            def _(sp):
                def load(t, s):
                    sp.dma_start(x_t[:, s, :], x[0, bass.ds(t * P, P), :]).then_inc(x_loaded[s], 16)

                def store(t, s):
                    sp.wait_ge(qkT_ready, CREDIT + t * 2 + 2)
                    sp.dma_start(qT_v[:, :, bass.ds(t * P, P)], qkT[:, 0:4, :]).then_inc(stored, 16)
                    sp.dma_start(kT_v[:, :, bass.ds(t * P, P)], qkT[:, 4:8, :]).then_inc(stored, 16)
                    sp.dma_start(v_dram[bass.ds(t * P, P), :], qkv[:, s, 2, :]).then_inc(stored, 16)

                with nc.allow_non_contiguous_dma("a small vector, once"):
                    sp.dma_start(gain[:, :], norm1_gain[0, :].rearrange("(k p) -> p k", p=P)).then_inc(gains, 16)
                sp.dma_start(qk_gain[:, 0, :], sb_q_gain[0, :].partition_broadcast(P)).then_inc(gains, 16)
                sp.dma_start(qk_gain[:, 1, :], sb_k_gain[0, :].partition_broadcast(P)).then_inc(gains, 16)
                load(0, 0)
                for part in range(3):
                    cols = slice(part * SBW, (part + 1) * SBW)
                    sp.dma_start(w_sb[:, :, cols], w_in[0, :, cols].rearrange("(k p) c -> p k c", p=P)).then_inc(w_loaded[part], 16)
                    if part == 0:
                        load(1, 1)
                with sp.Fori(0, NT // 2 - 1) as i:
                    for s in range(2):
                        t = i * 2 + s
                        sp.wait_ge(x_turned, t + 1)
                        load(t + 2, s)
                        store(t, s)
                for t in (NT - 2, NT - 1):
                    store(t, t % 2)
                sp.wait_ge(stored, CREDIT + NT * 48)

            @block.gpsimd
            def _(pool):
                pool.memset(eps[:, :], NORM_EPS)
                identity(pool, ident[:, :]).then_inc(consts, 1)
                pool.drain()
                pool.sem_inc(consts, 1)
                with pool.Fori(0, NT // 2) as i:
                    for s in range(2):
                        t = i * 2 + s
                        pool.wait_ge(h_ready, CREDIT + t * 2 + 2)
                        pool.sem_inc(on_pool, 1)
                        pool.tensor_copy(h_all[:, :, bass.ds(t * P, P)], hT[:, s, :, :]).then_inc(h_kept, 1)

            def tile_pairs(eng, one_tile):
                for s in range(2):
                    one_tile(s, s, first=(s == 0), last=False)
                with eng.Fori(1, NT // 2 - 1) as i:
                    for s in range(2):
                        one_tile(i * 2 + s, s, first=False, last=False)
                for s in range(2):
                    one_tile(NT - 2 + s, s, first=False, last=(s == 1))

            @block.scalar
            def _(act):
                def norm(t, s, n):
                    act.wait_ge(scaled, CREDIT + t)
                    act.wait_ge(x_loaded[s], n * 16 + 16)
                    act.activation(squares[:, :], x_t[:, s, :], ACT.Square, accum_out=ssum[:, :])
                    act.drain()
                    act.activation(root[:, :], ssum[:, :], ACT.Sqrt, bias=eps[:, :], scale=1.0 / D).then_inc(rooted, 1)

                def copy_turned(t):
                    act.wait_ge(qk_turned, CREDIT + t + 1)
                    act.wait_ge(stored, CREDIT + t * 48)
                    for half in range(2):
                        act.copy(qkT[:, 4 * half:4 * half + 4, :], qkT_ps[:, 4 * half:4 * half + 4, :]).then_inc(qkT_ready, 1)

                def one_tile(t, s, first, last):
                    for part in range(3):
                        if part == 0:
                            act.wait_ge(qk_turned, CREDIT + t - 1)
                        if part == 2 and not first:
                            copy_turned(t - 1)
                        if part == 2 and not first:
                            act.wait_ge(stored, CREDIT + (t - 1) * 48)
                        act.wait_ge(projected, t * 3 + part + 1)
                        act.copy(qkv[:, s, part, :], qkv_ps[:, part, :]).then_inc(qkv_copied, 1)
                    act.wait_ge(qk_summed, t + 1)
                    act.activation(qk_root[:, :], qk_sum[:, :], ACT.Sqrt, bias=eps[:, :], scale=1.0 / HD).then_inc(qk_rooted, 1)

                act.wait_ge(consts, 2)
                norm(0, 0, 0)
                norm(1, 1, 0)
                for s in range(2):
                    one_tile(s, s, first=(s == 0), last=False)
                    norm(s + 2, s, 1)
                with act.Fori(1, NT // 2 - 1) as i:
                    for s in range(2):
                        one_tile(i * 2 + s, s, first=False, last=False)
                        norm(i * 2 + s + 2, s, i + 1)
                for s in range(2):
                    one_tile(NT - 2 + s, s, first=False, last=False)
                copy_turned(NT - 1)

            @block.vector
            def _(dve):
                def scale_x(t, s):
                    dve.wait_ge(rooted, t + 1)
                    dve.reciprocal(rstd[:, :], root[:, :])
                    dve.drain()
                    dve.tensor_scalar(x_t[:, s, :], x_t[:, s, :], rstd[:, :], None, ALU.mult).then_inc(scaled, 1)

                def keep_h(t, s):
                    dve.wait_ge(x_turned, t + 1)
                    dve.wait_ge(h_kept, t + 1)
                    for half in range(2):
                        ks = slice(4 * half, 4 * half + 4)
                        dve.tensor_tensor(hT[:, s, ks, :], xT_ps[:, ks, :],
                                          gain[:, ks].unsqueeze(2).to_broadcast([P, 4, P]), ALU.mult).then_inc(h_ready, 1)

                def one_tile(t, s, first, last):
                    if not last:
                        keep_h(t + 1, 1 - s)
                    heads = qkv[:, s, 0:2, :].rearrange("p a (h d) -> p (a h) d", d=HD)
                    dve.wait_ge(qkv_copied, CREDIT + t * 3 + 2)
                    dve.tensor_tensor(qk_sq[:, :], qkv[:, s, 0:2, :], qkv[:, s, 0:2, :], ALU.mult)
                    dve.drain()
                    dve.reduce_sum(qk_sum[:, :], qk_sq[:, :].rearrange("p (h d) -> p h d", d=HD), axis=AX_X).then_inc(qk_summed, 1)
                    dve.wait_ge(qk_rooted, t + 1)
                    dve.reciprocal(qk_rstd[:, :], qk_root[:, :])
                    dve.drain()
                    dve.tensor_tensor(heads, heads, qk_rstd[:, :].unsqueeze(2).to_broadcast([P, 16, HD]), ALU.mult)
                    dve.drain()
                    for a in range(2):
                        part = qkv[:, s, a, :].rearrange("p (h d) -> p h d", d=HD)
                        done = dve.tensor_tensor(part, part, qk_gain[:, a, :].unsqueeze(1).to_broadcast([P, 8, HD]), ALU.mult)
                    done.then_inc(qk_ready, 1)
                    if not (isinstance(t, int) and t + 2 >= NT):
                        scale_x(t + 2, s)

                dve.sem_inc(h_kept, 2)
                dve.wait_ge(gains, 16 * 3)
                scale_x(0, 0)
                dve.wait_ge(x_turned, 1)
                for half in range(2):
                    ks = slice(4 * half, 4 * half + 4)
                    dve.tensor_tensor(hT[:, 0, ks, :], xT_ps[:, ks, :],
                                      gain[:, ks].unsqueeze(2).to_broadcast([P, 4, P]), ALU.mult).then_inc(h_ready, 1)
                scale_x(1, 1)
                tile_pairs(dve, one_tile)

            @block.tensor
            def _(pe):
                def turn_x(t, s):
                    pe.wait_ge(scaled, CREDIT + t + 1)
                    pe.wait_ge(h_ready, CREDIT + t * 2)
                    for k in range(KT):
                        done = pe.transpose(xT_ps[:, k, :], x_t[:, s, k * P:(k + 1) * P], ident[:, :])
                    done.then_inc(x_turned, 1)

                def turn_qk(t, s):
                    pe.wait_ge(qk_ready, t + 1)
                    pe.wait_ge(qkT_ready, CREDIT + t * 2)
                    for c in range(8):
                        done = pe.transpose(qkT_ps[:, c, :], qkv[:, s, c // 4, (c % 4) * P:(c % 4 + 1) * P], ident[:, :])
                    done.then_inc(qk_turned, 1)

                def one_tile(t, s, first, last):
                    pe.wait_ge(h_ready, CREDIT + t * 2 + 2)
                    for part in range(3):
                        if first:
                            pe.wait_ge(w_loaded[part], 16)
                        pe.wait_ge(qkv_copied, CREDIT + t * 3 - 2 + part)
                        for k in range(KT):
                            done = pe.matmul(qkv_ps[:, part, :], hT[:, s, k, :], w_sb[:, k, part * SBW:(part + 1) * SBW],
                                             start=(k == 0), stop=(k == KT - 1))
                        done.then_inc(projected, 1)
                        if part == 0 and not first:
                            turn_qk(t - 1, 1 - s)
                        if part == 1 and not last:
                            turn_x(t + 1, 1 - s)

                pe.wait_ge(consts, 2)
                turn_x(0, 0)
                tile_pairs(pe, one_tile)
                turn_qk(NT - 1, 1)


def project_channels(nc, program, h_all, w_in, rw_shift_mu, pT_dram):
    with ExitStack() as ctx:
        sb, pb, sem = makers(nc, ctx, program)
        NFULL = RW_COLS // P
        REST = RW_COLS - NFULL * P
        LOOPED = NFULL // 2 * 2
        GT = 512
        NG = SEQ // GT
        w = sb("w_ch", [P, 2, KT, P])
        mu = sb("mu", [P, NFULL + 1])
        p_raw = sb("p_raw", [P, 1 + SEQ])
        diff = sb("diff", [P, SEQ])
        shifted = sb("shifted", [P, 2, SEQ])
        mu_c = sb("mu_c", [P, 1])
        p_ps = pb("p_ps", [P, 2, NG, GT])
        mu_loaded = sem("p2_mu_loaded")
        w_loaded = [sem(f"p2_w_loaded{s}") for s in range(2)]
        projected = sem("p2_projected")
        copied = sem("p2_copied")
        mixed = sem("p2_mixed")
        stored = [sem(f"p2_stored{s}") for s in range(2)]
        zeroed = sem("p2_zeroed")
        on_sp, on_act, on_pe, on_dve, on_pool = program.gates_passed
        NCH = NFULL + 1
        give_credit(nc, mixed)
        with nc.Block() as block:
            @block.sync
            def _(sp):
                def load(c, s, width=P):
                    src = w_in[0, :, bass.ds(c * P + SB_COLS, width)].rearrange("(k p) c -> p k c", p=P)
                    sp.dma_start(w[:, s, :, 0:width], src).then_inc(w_loaded[s], 16)

                def store(c, s, width=P):
                    sp.wait_ge(mixed, CREDIT + c + 1)
                    sp.dma_start(pT_dram[bass.ds(c * P, width), :], shifted[0:width, s, :]).then_inc(stored[s], 16)

                load(0, 0)
                load(1, 1)
                with nc.allow_non_contiguous_dma("a small vector, once"):
                    sp.dma_start(mu[:, 0:NFULL], rw_shift_mu[0, 0:NFULL * P].rearrange("(k p) -> p k", p=P)).then_inc(mu_loaded, 16)
                    sp.dma_start(mu[0:REST, NFULL:NFULL + 1], rw_shift_mu[0, NFULL * P:RW_COLS].rearrange("(k p) -> p k", k=1)).then_inc(mu_loaded, 16)
                with sp.Fori(0, LOOPED // 2 - 1) as i:
                    for s in range(2):
                        c = i * 2 + s
                        sp.wait_ge(projected, (c + 1) * NG)
                        load(c + 2, s)
                        store(c, s)
                for c in range(LOOPED - 2, NCH):
                    if c + 2 < NCH:
                        sp.wait_ge(projected, (c + 1) * NG)
                        load(c + 2, c % 2, P if c + 2 < NFULL else REST)
                    store(c, c % 2, P if c < NFULL else REST)
                for s in range(2):
                    sp.wait_ge(stored[s], 16 * (NCH // 2) + 16)

            @block.tensor
            def _(pe):
                def chunk(c, s, n, width=P):
                    pe.wait_ge(w_loaded[s], n * 16 + 16)
                    for g in range(NG):
                        pe.wait_ge(copied, c * NG + g + 1)
                        for k in range(KT):
                            last = pe.matmul(p_ps[0:width, s, g, :], w[:, s, k, 0:width], h_all[:, k, g * GT:(g + 1) * GT],
                                             start=(k == 0), stop=(k == KT - 1))
                        last.then_inc(projected, 1)

                with pe.Fori(0, LOOPED // 2) as i:
                    for s in range(2):
                        chunk(i * 2 + s, s, i)
                for c in range(LOOPED, NCH):
                    chunk(c, c % 2, c // 2, P if c < NFULL else REST)

            @block.scalar
            def _(act):
                act.sem_inc(copied, 2 * NG)
                act.wait_ge(zeroed, 1)

                def chunk(c, s, n, width=P):
                    act.wait_ge(mixed, CREDIT + c)
                    for g in range(NG):
                        act.wait_ge(projected, c * NG + g + 1)
                        act.copy(p_raw[0:width, 1 + g * GT:1 + (g + 1) * GT], p_ps[0:width, s, g, :]).then_inc(copied, 1)

                with act.Fori(0, LOOPED // 2) as i:
                    for s in range(2):
                        chunk(i * 2 + s, s, i)
                for c in range(LOOPED, NCH):
                    chunk(c, c % 2, c // 2, P if c < NFULL else REST)

            @block.vector
            def _(dve):
                dve.memset(p_raw[:, 0:1], 0.0).then_inc(zeroed, 1)
                dve.wait_ge(mu_loaded, 32)
                dve.sem_inc(stored[0], 16)
                dve.sem_inc(stored[1], 16)

                def chunk(c, s, n, width=P):
                    dve.wait_ge(copied, (c + 1) * NG + 2 * NG)
                    dve.tensor_tensor(diff[0:width, :], p_raw[0:width, 0:SEQ], p_raw[0:width, 1:1 + SEQ], ALU.subtract)
                    dve.tensor_copy(mu_c[0:width, :], mu[0:width, bass.ds(c, 1)])
                    dve.drain()
                    dve.wait_ge(stored[s], n * 16 + 16)
                    dve.scalar_tensor_tensor(shifted[0:width, s, :], diff[0:width, :], mu_c[0:width, :],
                                             p_raw[0:width, 1:1 + SEQ], ALU.mult, ALU.add).then_inc(mixed, 1)

                with dve.Fori(0, LOOPED // 2) as i:
                    for s in range(2):
                        chunk(i * 2 + s, s, i)
                for c in range(LOOPED, NCH):
                    chunk(c, c % 2, c // 2, P if c < NFULL else REST)


def stick_breaking(nc, program, qT_dram, kT_dram, v_dram, mixT_dram):
    with ExitStack() as ctx:
        sb, pb, sem = makers(nc, ctx, program)
        CH = 512
        SLOTS = 3
        ZR = 3
        SCALE = HD ** -0.5
        order = [t for a in range(NT // 2) for t in (a, a + NT // 2)]
        tiles = [(pair, t) for pair in range(2) for t in order]
        units = [(o, h) for o in range(len(tiles)) for h in range(2)]
        n_chunks = [((tiles[o][1] + 1) * P + CH - 1) // CH for o, _ in units]
        first = [sum(n_chunks[:u]) for u in range(len(units) + 1)]
        NU, NCH, NO = len(units), first[-1], len(tiles)
        ROUNDS = PAIRS // 2

        q_sb = sb("q_sb", [P, 2, SEQ])
        k_sb = sb("k_sb", [P, 2, SEQ])
        v_sb = sb("v_sb", [P, 2, NT, P])
        keep = sb("keep", [P, SLOTS, SEQ])
        take = sb("take", [P, SLOTS, SEQ])
        prod = sb("prod", [P, SLOTS, SEQ])
        wT = sb("wT", [P, 2, CH])
        o_sb = sb("o_sb", [P, P])
        oT_sb = sb("oT_sb", [P, 2, P])
        ident = sb("ident_a", [P, P])
        z_ps = [pb(f"z_ps{i}", [P, CH]) for i in range(ZR)]
        wT_ps = [pb(f"wT_ps{i}", [P, CH]) for i in range(2)]
        o_banks = pb("o_banks", [P, 3, CH])
        o_ps = [o_banks[:, 0, 0:P], o_banks[:, 1, 0:P]]
        oT_ps = o_banks[:, 2, 0:P]

        consts = sem("p3_consts")
        qkv_loaded = [sem(f"p3_qkv_loaded{s}") for s in range(2)]
        z_done = sem("p3_z_done")
        z_read = sem("p3_z_read")
        masked = sem("p3_masked")
        scanned = sem("p3_scanned")
        weighted = sem("p3_weighted")
        turned = sem("p3_turned")
        turned_copied = sem("p3_turned_copied")
        weighed = sem("p3_weighed")
        o_copied = sem("p3_o_copied")
        o_turned = sem("p3_o_turned")
        oT_copied = sem("p3_oT_copied")
        stored = [sem(f"p3_stored{s}") for s in range(2)]
        on_sp, on_act, on_pe, on_dve, on_pool = program.gates_passed

        def tile_of(u):
            return tiles[units[u][0]]

        def cut(u, c):
            start = (n_chunks[u] - 1 - c) * CH
            return start, min(CH, (tile_of(u)[1] + 1) * P - start)

        give_credit(nc, oT_copied, o_copied, o_turned, *stored, turned_copied, weighed, z_read)
        with nc.Block() as block:
            @block.sync
            def _(sp):
                def load(j, pair):
                    rows = bass.ds((j * 2 + pair) * P, P)
                    sp.dma_start(q_sb[:, pair, :], qT_dram[rows, :]).then_inc(qkv_loaded[pair], 16)
                    sp.dma_start(k_sb[:, pair, :], kT_dram[rows, :]).then_inc(qkv_loaded[pair], 16)
                    sp.dma_start(v_sb[:, pair, :, :], v_dram[:, rows].rearrange("(n p) c -> p n c", p=P)).then_inc(qkv_loaded[pair], 16)

                def one_round(j, last):
                    sp.wait_ge(weighed, CREDIT + j * NCH)
                    load(j, 1)
                    for o, (pair, t) in enumerate(tiles):
                        sp.wait_ge(oT_copied, CREDIT + j * NO + o + 1)
                        sp.dma_start(mixT_dram[bass.ds((j * 2 + pair) * P, P), t * P:(t + 1) * P], oT_sb[:, o % 2, :]).then_inc(stored[o % 2], 16)
                        if o == NT - 1 and not last:
                            sp.wait_ge(weighed, CREDIT + j * NCH + first[2 * NT])
                            load(j + 1, 0)

                load(0, 0)
                with sp.Fori(0, ROUNDS - 1) as j:
                    one_round(j, last=False)
                one_round(ROUNDS - 1, last=True)
                for s in range(2):
                    sp.wait_ge(stored[s], CREDIT + 16 * ROUNDS * NO // 2)

            @block.tensor
            def _(pe):
                pe.wait_ge(consts, 1)

                def scores(j, u, c):
                    if u >= NU or c >= n_chunks[u]:
                        return
                    (pair, t), h, n = tile_of(u), units[u][1], first[u] + c
                    hs = slice(h * HD, (h + 1) * HD)
                    start, w = cut(u, c)
                    if c == 0 and u % (NU // 2) == 0:
                        pe.wait_ge(qkv_loaded[pair], j * 48 + 48)
                    pe.wait_ge(z_read, CREDIT + j * NCH + max(n - ZR + 1, 0))
                    pe.matmul(z_ps[n % ZR][:, 0:w], q_sb[hs, pair, t * P:(t + 1) * P], k_sb[hs, pair, start:start + w],
                              start=True, stop=True).then_inc(z_done, 1)

                def turn(j, u, c):
                    (start, w), n = cut(u, c), first[u] + c
                    pe.wait_ge(weighted, j * NCH + n + 1)
                    pe.wait_ge(turned_copied, CREDIT + j * NCH + max(n - 1, 0))
                    for b in range(w // P):
                        s0 = start + b * P
                        last = pe.transpose(wT_ps[n % 2][:, b * P:(b + 1) * P], take[:, u % SLOTS, s0:s0 + P], ident[:, :])
                    last.then_inc(turned, 1)

                def weigh(j, u, c):
                    pair, (o, h), n = tile_of(u)[0], units[u], first[u] + c
                    start, w = cut(u, c)
                    pe.wait_ge(turned_copied, CREDIT + j * NCH + n + 1)
                    if c == 0 and h == 0:
                        pe.wait_ge(o_copied, CREDIT + j * NO + max(o - 1, 0))
                    for b in range(w // P):
                        last = pe.matmul(o_ps[o % 2][:, h * HD:(h + 1) * HD], wT[:, n % 2, b * P:(b + 1) * P],
                                         v_sb[:, pair, start // P + b, h * HD:(h + 1) * HD],
                                         start=(c == b == 0), stop=(c == n_chunks[u] - 1 and b == w // P - 1))
                    last.then_inc(weighed, 1)

                def turn_out(j, o):
                    pe.wait_ge(o_copied, CREDIT + j * NO + o + 1)
                    pe.wait_ge(oT_copied, CREDIT + j * NO + o)
                    pe.transpose(oT_ps, o_sb[:, :], ident[:, :]).then_inc(o_turned, 1)

                with pe.Fori(0, ROUNDS) as j:
                    scores(j, 0, 0)
                    scores(j, 1, 0)
                    for u, (o, h) in enumerate(units):
                        turn(j, u, 0)
                        for c in range(n_chunks[u]):
                            scores(j, u + 2, c)
                            if c + 1 < n_chunks[u]:
                                turn(j, u, c + 1)
                            weigh(j, u, c)
                        for c in range(n_chunks[u], n_chunks[min(u + 2, NU - 1)]):
                            scores(j, u + 2, c)
                        if h == 1 and o >= 1:
                            turn_out(j, o - 1)
                    turn_out(j, NO - 1)

            @block.scalar
            def _(act):
                def copy_out(j, o):
                    act.wait_ge(weighed, CREDIT + j * NCH + first[2 * o + 2])
                    act.wait_ge(o_turned, CREDIT + j * NO + o)
                    act.copy(o_sb[:, :], o_ps[o % 2]).then_inc(o_copied, 1)

                def copy_turned(j, o):
                    act.wait_ge(o_turned, CREDIT + j * NO + o + 1)
                    act.wait_ge(stored[o % 2], CREDIT + j * (8 * NO) + 16 * (o // 2))
                    act.copy(oT_sb[:, o % 2, :], oT_ps).then_inc(oT_copied, 1)

                with act.Fori(0, ROUNDS) as j:
                    for u, (o, h) in enumerate(units):
                        act.wait_ge(weighed, CREDIT + j * NCH + first[max(u - SLOTS + 1, 0)])
                        if h == 0 and o >= 2:
                            copy_out(j, o - 2)
                        if h == 0 and o >= 3:
                            copy_turned(j, o - 3)
                        for c in range(n_chunks[u]):
                            n = first[u] + c
                            start, w = cut(u, c)
                            cols = slice(start, start + w)
                            act.wait_ge(z_done, j * NCH + n + 1)
                            act.activation(keep[:, u % SLOTS, cols], z_ps[n % ZR][:, 0:w], ACT.Sigmoid, scale=-SCALE)
                            act.activation(take[:, u % SLOTS, cols], z_ps[n % ZR][:, 0:w], ACT.Sigmoid, scale=SCALE).then_inc(z_read, 1)
                    copy_out(j, NO - 2)
                    copy_turned(j, NO - 3)
                    copy_turned(j, NO - 2)
                    copy_out(j, NO - 1)
                    copy_turned(j, NO - 1)

            @block.gpsimd
            def _(pool):
                identity(pool, ident[:, :]).then_inc(consts, 1)

                def mask(j, u):
                    t, slot = tile_of(u)[1], u % SLOTS
                    diag = slice(t * P, (t + 1) * P)
                    pool.wait_ge(z_read, CREDIT + j * NCH + first[u] + 1)
                    pool.sem_inc(on_pool, 1)
                    for tile, fill in ((keep, 1.0), (take, 0.0)):
                        last = pool.affine_select(out=tile[:, slot, diag], in_=tile[:, slot, diag], compare_op=ALU.is_gt,
                                                  fill=fill, base=0, pattern=[[-1, P]], channel_multiplier=1)
                    last.then_inc(masked, 1)

                def weight(j, u, c):
                    (start, w), slot, n = cut(u, c), u % SLOTS, first[u] + c
                    end = start + w - (c == 0)
                    pool.wait_ge(scanned, j * NCH + n + 1)
                    pool.sem_inc(on_pool, 1)
                    pool.tensor_tensor(take[:, slot, start:end], take[:, slot, start:end], prod[:, slot, start + 1:end + 1],
                                       ALU.mult).then_inc(weighted, 1)

                with pool.Fori(0, ROUNDS) as j:
                    mask(j, 0)
                    for u in range(NU):
                        if u + 1 < NU:
                            mask(j, u + 1)
                        for c in range(n_chunks[u]):
                            weight(j, u, c)

            @block.vector
            def _(dve):
                def scan(j, u, c):
                    if c >= n_chunks[u]:
                        return
                    (start, w), slot, n = cut(u, c), u % SLOTS, first[u] + c
                    if c == 0:
                        dve.wait_ge(masked, j * NU + u + 1)
                    else:
                        dve.wait_ge(z_read, CREDIT + j * NCH + n + 1)
                        dve.wait_ge(scanned, j * NCH + n)
                    rows = keep[:, slot, start:start + w][:, ::-1]
                    so_far = 1.0 if c == 0 else prod[:, slot, start + w:start + w + 1]
                    dve.tensor_tensor_scan(prod[:, slot, start:start + w][:, ::-1], rows, rows, so_far, ALU.mult, ALU.bypass).then_inc(scanned, 1)

                with dve.Fori(0, ROUNDS) as j:
                    for c in range(n_chunks[0]):
                        scan(j, 0, c)
                    for u in range(NU):
                        for c in range(max(n_chunks[u], n_chunks[min(u + 1, NU - 1)])):
                            if c < n_chunks[u]:
                                n, w = first[u] + c, cut(u, c)[1]
                                dve.wait_ge(turned, j * NCH + n + 1)
                                dve.wait_ge(weighed, CREDIT + j * NCH + max(n - 1, 0))
                                dve.tensor_copy(wT[:, n % 2, 0:w], wT_ps[n % 2][:, 0:w]).then_inc(turned_copied, 1)
                            if u + 1 < NU:
                                scan(j, u + 1, c)


class Stream:

    def __init__(self, p, sb, pb):
        C, NC, GT = HD, 512 // HD, 512
        self.p = p
        self.rkv = sb(f"rkv{p}", [P, 3, GT])
        self.w_up, self.a_up, self.g_up = [sb(f"{n}{p}", [w, P]) for n, w in (("w_up_p", LW), ("a_up_p", LA), ("g_up_p", LG))]
        self.vecs = sb(f"vecs{p}", [P, 5])
        self.lnv = sb(f"lnv{p}", [P, 2])
        self.logw, self.kraw, self.sq, self.root = [sb(f"{n}{p}", [P, GT]) for n in ("logw", "kraw", "sq", "root")]
        self.a_g, self.k2, self.rk, self.kka = [sb(f"{n}{p}", [P, GT]) for n in ("a_g", "k2", "rk", "kka")]
        self.Lsum, self.Dec, self.DecP, self.DecI = [sb(f"{n}{p}", [P, GT]) for n in ("Lsum", "Dec", "DecP", "DecI")]
        self.g, self.bonus, self.dev, self.std = [sb(f"{n}{p}", [P, GT]) for n in ("g", "bonus", "dev", "std")]
        self.r_t = sb(f"r_t{p}", [P, NC, C])
        self.ends = sb(f"ends{p}", [P, NC])
        self.AR = sb(f"AR{p}", [P, NC, 2, C])
        self.b_t, self.k_t, self.b_h, self.k_h = [sb(f"{n}{p}", [P, GT]) for n in ("b_t", "k_t", "b_h", "k_h")]
        self.tok = sb(f"tok{p}", [P, 4, NC, C])
        self.SB1 = sb(f"SB1_{p}", [P, NC, 2, C])
        self.SB2 = sb(f"SB2_{p}", [P, NC, 2, C])
        self.ATl = sb(f"ATl{p}", [P, 5, NC, C])
        self.XX = sb(f"XX{p}", [P, 2, NC, C])
        self.T1 = sb(f"T1_{p}", [P, NC, C])
        self.GW = sb(f"GW{p}", [P, 2, NC, C])
        self.SA = sb(f"SA{p}", [P, C])
        self.S = sb(f"S_state{p}", [P, C])
        self.y = sb(f"y_sb{p}", [P, GT])
        self.outp = sb(f"outp{p}", [P, GT])
        self.QA, self.QB = pb(f"QA{p}", [P, 2, 512]), pb(f"QB{p}", [P, 2, 512])


def time_mixing(nc, program, w0, w_up, a0, a_up, g_up, k_k, k_a, r_k, ln_w, ln_b, pT_dram, mixT_dram):
    with ExitStack() as ctx:
        sb, pb, sem = makers(nc, ctx, program)
        C = HD
        GT = 512
        NG, NC = SEQ // GT, GT // C
        HC = NC // 2
        LEVELS = (2, 4, 8, 16, 32)
        NL = len(LEVELS)
        LORA = 3 * SBW
        N2 = PAIRS // 2

        wd = sb("wd", [LW, GT])
        ad = sb("ad", [LA, GT])
        gd = sb("gd", [LG, GT])
        ident = sb("ident_r", [P, P])
        head_ones = sb("head_ones", [P, P])
        chunk_reset = sb("chunk_reset", [P, GT])
        zero_eps = sb("zero_eps", [P, 2])
        below = sb("below", [P, 2, C])
        lev = sb("lev", [P, NL, C])
        lev1T = sb("lev1T", [P, C])
        lev1 = sb("lev1", [P, C])
        eye = sb("eye", [P, C])
        streams = [Stream(p, sb, pb) for p in range(2)]

        names = """weights lnw_loaded consts loaded0 loaded1 lora_loaded gate_loaded lora_ready gate_ready kk2_ready pre_done pre_read
            L_ready exp_ready root_ready operands_ready bonus_done bonus_read bonus_ready turnedA_done turnedB_done tokA_ready
            tokB_ready scores1_done scores2_done scores1_ready scores2_ready A_done level0_ready levels_ready X_ready T_done
            T_ready dX_done GW_done GW_ready sa_done saA_ready saB_ready dS_done S_ready y_done y_ready g_done g_ready mean_done
            centred_ready var_done std_ready out_ready stored0 stored1""".split()
        (weights, lnw_loaded, consts, loaded0, loaded1, lora_loaded, gate_loaded, lora_ready, gate_ready, kk2_ready, pre_done, pre_read,
         L_ready, exp_ready, root_ready, operands_ready, bonus_done, bonus_read, bonus_ready, turnedA_done, turnedB_done, tokA_ready,
         tokB_ready, scores1_done, scores2_done, scores1_ready, scores2_ready, A_done, level0_ready, levels_ready, X_ready, T_done,
         T_ready, dX_done, GW_done, GW_ready, sa_done, saA_ready, saB_ready, dS_done, S_ready, y_done, y_ready, g_done, g_ready, mean_done,
         centred_ready, var_done, std_ready, out_ready, stored0, stored1) = [sem(f"p4_{n}") for n in names]
        loaded, stored = (loaded0, loaded1), (stored0, stored1)
        on_sp, on_act, on_pe, on_dve, on_pool = program.gates_passed
        N_CONSTS = 2
        N_WEIGHTS = 7 * 2
        N_LNW = 3 * 2

        def chunks(tile):
            return tile[:, :].rearrange("p (c t) -> p c t", t=C)

        def two(bank_pair):
            return bank_pair[:, :, :].rearrange("p b (q x) -> p b q x", q=2)

        def two_sb(tile):
            return tile.rearrange("p q (b h) c -> p b q (h c)", b=2)

        def at(n, st, K=1, x=0):
            return (n * K + x) * 2 + st.p + 1

        PRE = 3
        TURNS = N2 * NG
        def prepare_first(eng, passed, m, st):
            eng.wait_ge(loaded[st.p], m * 48 + 48)
            eng.sem_inc(passed, 1)
            eng.wait_ge(weights, m * (16 * N_WEIGHTS) + 16 * N_WEIGHTS)
            eng.sem_inc(passed, 1)
            eng.tensor_scalar(st.kraw[:, :], st.rkv[:, 1, :], st.vecs[:, 2:3], None, ALU.mult)
            eng.drain()
            eng.tensor_tensor(st.sq[:, :], st.kraw[:, :], st.kraw[:, :], ALU.mult).then_inc(kk2_ready, 1)

        def prepare_k(eng, passed, m, st):
            eng.wait_ge(pre_read, at(m, st, PRE, 1))
            eng.sem_inc(passed, 1)
            eng.tensor_scalar(st.k2[:, :], st.a_g[:, :], -1.0, st.vecs[:, 3:4], ALU.add, ALU.mult)
            eng.tensor_scalar(st.rk[:, :], st.rkv[:, 0, :], st.vecs[:, 4:5], None, ALU.mult)
            eng.drain()
            eng.tensor_scalar(st.k2[:, :], st.k2[:, :], 1.0, None, ALU.add)
            eng.drain()
            eng.tensor_tensor(st.k2[:, :], st.k2[:, :], st.rkv[:, 1, :], ALU.mult)
            eng.drain()
            eng.tensor_tensor(st.rk[:, :], st.rk[:, :], st.k2[:, :], ALU.mult)

        def prepare_operands(eng, passed, m, st):
            eng.wait_ge(root_ready, at(m, st))
            eng.sem_inc(passed, 1)
            eng.wait_ge(exp_ready, at(m, st))
            eng.sem_inc(passed, 1)
            eng.tensor_tensor(st.kraw[:, :], st.kraw[:, :], st.root[:, :], ALU.mult)
            eng.tensor_tensor(st.k_t[:, :], st.k2[:, :], st.DecI[:, :], ALU.mult)
            eng.tensor_tensor(st.AR[:, :, 1, :], st.rkv[:, 0, :].rearrange("p (c t) -> p c t", t=C), chunks(st.Dec), ALU.mult)
            eng.drain()
            end = chunks(st.Dec)[:, :, C - 1:C].to_broadcast([P, NC, C])
            eng.tensor_tensor(st.AR[:, :, 0, :], chunks(st.kraw), chunks(st.DecP), ALU.mult)
            eng.tensor_tensor(st.kka[:, :], st.kraw[:, :], st.a_g[:, :], ALU.mult)
            eng.tensor_tensor(chunks(st.k_h), chunks(st.k_t), end, ALU.mult)
            eng.tensor_scalar(st.DecI[:, :], st.DecI[:, :], -1.0, None, ALU.mult)
            eng.drain()
            eng.tensor_tensor(st.b_t[:, :], st.kka[:, :], st.DecI[:, :], ALU.mult)
            eng.drain()
            eng.tensor_tensor(chunks(st.b_h), chunks(st.b_t), end, ALU.mult).then_inc(operands_ready, 1)

        give_credit(nc, out_ready, std_ready, g_ready, g_done, *stored)
        with nc.Block() as block:
            @block.sync
            def _(sp):
                def load_next(i, g, n):
                    ts = bass.ds(g * GT, GT)
                    sp.dma_start(wd[:, :], pT_dram[LORA:LORA + LW, ts]).then_inc(lora_loaded, 16)
                    sp.dma_start(ad[:, :], pT_dram[LORA + LW:LORA + LW + LA, ts]).then_inc(lora_loaded, 16)
                    for st in streams:
                        cols = bass.ds((i * 2 + st.p) * P, P)
                        sp.dma_start(st.w_up[:, :], w_up[0, :, cols]).then_inc(weights, 16)
                        sp.dma_start(st.a_up[:, :], a_up[0, :, cols]).then_inc(weights, 16)
                        for x, vec in enumerate((w0[0], a0[0], k_k[0], k_a[0], r_k[0].rearrange("h d -> (h d)"))):
                            sp.dma_start(st.vecs[:, x:x + 1], vec[cols].unsqueeze(1)).then_inc(weights, 16)

                def load_rkv(st, i, g):
                    for a in range(3):
                        sp.dma_start(st.rkv[:, a, :], pT_dram[bass.ds((i * 2 + st.p) * P + a * SBW, P), bass.ds(g * GT, GT)]).then_inc(loaded[st.p], 16)

                def turn(i, g, n, next_i, next_g):
                    sp.wait_ge(g_done, CREDIT + n * 2)
                    sp.sem_inc(on_sp, 1)
                    sp.wait_ge(out_ready, CREDIT + n * 2)
                    sp.sem_inc(on_sp, 1)
                    sp.dma_start(gd[:, :], pT_dram[LORA + LW + LA:LORA + LW + LA + LG, bass.ds(g * GT, GT)]).then_inc(gate_loaded, 16)
                    for st in streams:
                        cols = bass.ds((i * 2 + st.p) * P, P)
                        sp.dma_start(st.g_up[:, :], g_up[0, :, cols]).then_inc(lnw_loaded, 16)
                        for x, vec in enumerate((ln_w[0], ln_b[0])):
                            sp.dma_start(st.lnv[:, x:x + 1], vec[cols].unsqueeze(1)).then_inc(lnw_loaded, 16)
                    sp.wait_ge(operands_ready, at(n, streams[1]))
                    sp.sem_inc(on_sp, 1)
                    load_next(next_i, next_g, n + 1)
                    for st in streams:
                        sp.wait_ge(turnedB_done, at(n, st))
                        sp.sem_inc(on_sp, 1)
                        sp.wait_ge(bonus_ready, at(n, st))
                        sp.sem_inc(on_sp, 1)
                        load_rkv(st, next_i, next_g)
                    for st in streams:
                        sp.wait_ge(out_ready, CREDIT + at(n, st))
                        sp.sem_inc(on_sp, 1)
                        sp.dma_start(mixT_dram[bass.ds((i * 2 + st.p) * P + SBW, P), bass.ds(g * GT, GT)], st.outp[:, :]).then_inc(stored[st.p], 16)

                load_next(0, 0, 0)
                for st in streams:
                    load_rkv(st, 0, 0)

                def turns_of(i, after):
                    with sp.Fori(0, NG - 1) as g:
                        turn(i, g, i * NG + g, i, g + 1)
                    turn(i, NG - 1, i * NG + NG - 1, after, 0)

                with sp.Fori(0, N2 - 1) as i:
                    turns_of(i, i + 1)
                turns_of(N2 - 1, 0)
                for st in streams:
                    sp.wait_ge(stored[st.p], CREDIT + 16 * TURNS)

            @block.gpsimd
            def _(pool):
                def block_select(tile, op, base, pattern, mult, fill=0.0):
                    pool.affine_select(out=tile, in_=tile, compare_op=op, fill=fill, base=base,
                                       pattern=pattern, channel_multiplier=mult)
                    pool.drain()

                identity(pool, ident[:, :])
                pool.drain()
                pool.memset(head_ones[:, :], 0.0)
                pool.memset(chunk_reset[:, :], 1.0)
                pool.memset(below[:, :, :], 1.0)
                pool.memset(lev[:, :, :], 0.0)
                pool.memset(lev1[:, :], 0.0)
                pool.memset(lev1T[:, :], 0.0)
                pool.memset(zero_eps[:, 0:1], 0.0)
                pool.memset(zero_eps[:, 1:2], LN_X_EPS)
                pool.drain()
                pool.memset(chunks(chunk_reset)[:, :, 0:1], 0.0)
                for h in range(2):
                    hs = slice(h * C, (h + 1) * C)
                    pool.memset(head_ones[hs, hs], 1.0)
                    pool.tensor_copy(eye[hs, :], ident[hs, hs])
                    block_select(below[hs, 0, :], ALU.is_gt, 0, [[1, C]], -1)
                    block_select(below[hs, 1, :], ALU.is_ge, 0, [[1, C]], -1)
                    block_select(lev1T[hs, :].rearrange("p (n b) -> p n b", b=2)[:, :, 0], ALU.not_equal, -1, [[-2, C // 2]], 1, 1.0)
                    block_select(lev1[hs, :].rearrange("p (n b) -> p n b", b=2)[:, :, 1], ALU.not_equal, 0, [[-2, C // 2]], 1, 1.0)
                    for x, size in enumerate(LEVELS):
                        v = lev[hs, x, :].rearrange("p (n b s) -> p n b s", b=2, s=size)[:, :, 1, :]
                        nb = C // (2 * size)
                        pool.memset(v, 1.0)
                        pool.drain()
                        block_select(v, ALU.is_ge, 0, [[-2 * size, nb], [0, size]], 1)
                        block_select(v, ALU.is_ge, size - 1, [[2 * size, nb], [0, size]], -1)
                pool.drain()
                pool.sem_inc(consts, N_CONSTS)

                for prepare in (prepare_first, prepare_k, prepare_operands):
                    prepare(pool, on_pool, 0, streams[0])
                with pool.Fori(0, TURNS) as n:
                    for st in streams:
                        pool.wait_ge(bonus_read, at(n, st))
                        pool.sem_inc(on_pool, 1)
                        pool.wait_ge(out_ready, CREDIT - 1 + 2 * n + st.p)
                        pool.sem_inc(on_pool, 1)
                        pool.tensor_tensor(st.bonus[:, :], st.kka[:, :], st.rkv[:, 2, :], ALU.mult).then_inc(bonus_ready, 1)
                    for st in streams:
                        pool.wait_ge(scores1_ready, at(n, st))
                        pool.sem_inc(on_pool, 1)
                        for x in range(NL):
                            done = pool.tensor_tensor(st.ATl[:, x, :, :], st.SB1[:, :, 0, :], lev[:, x, :].unsqueeze(1).to_broadcast([P, NC, C]), ALU.mult)
                            if x == 0:
                                done.then_inc(level0_ready, 1)
                                pool.tensor_copy(st.r_t[:, :, :], st.AR[:, :, 1, :])
                                pool.tensor_copy(st.ends[:, :].unsqueeze(2), chunks(st.Dec)[:, :, C - 1:C])
                        done.then_inc(levels_ready, 1)
                    for st in streams:
                        prepare_first(pool, on_pool, n + 1, st)
                    for st in streams:
                        prepare_k(pool, on_pool, n + 1, st)
                    for st in streams:
                        pool.wait_ge(GW_done, at(n, st))
                        pool.sem_inc(on_pool, 1)
                        prepare_operands(pool, on_pool, n + 1, st)

            @block.scalar
            def _(act):
                act.wait_ge(consts, N_CONSTS)

                def wide(st):
                    return st.QB[:, :, 256:512]

                def halves(tile):
                    return tile[:, :].rearrange("p (b x) -> p b x", b=2)

                def bottleneck(m):
                    act.wait_ge(lora_loaded, m * 32 + 32)
                    act.activation(wd[:, :], wd[:, :], ACT.Tanh).then_inc(lora_ready, 1)

                def prepare(m, st, k):
                    act.wait_ge(pre_done, at(m, st, PRE, k))
                    if k == 0:
                        act.activation(halves(st.logw), wide(st), ACT.Sigmoid, bias=st.vecs[:, 0:1]).then_inc(pre_read, 1)
                    if k == 1:
                        act.activation(halves(st.a_g), wide(st), ACT.Sigmoid, bias=st.vecs[:, 1:2]).then_inc(pre_read, 1)
                    if k == 2:
                        act.activation(halves(st.root), wide(st), ACT.Sqrt, bias=zero_eps[:, 0:1]).then_inc(pre_read, 1)

                def exponentials(m, st):
                    act.wait_ge(L_ready, at(m, st))
                    act.activation(st.Dec[:, :], st.Lsum[:, :], ACT.Exp)
                    act.activation(st.DecI[:, :], st.Lsum[:, :], ACT.Exp, scale=-1.0)
                    act.activation(st.DecP[:, :], st.logw[:, :], ACT.Exp).then_inc(exp_ready, 1)

                bottleneck(0)
                act.wait_ge(weights, 16 * N_WEIGHTS)
                for k in range(PRE):
                    for st in streams:
                        prepare(0, st, k)
                for st in streams:
                    exponentials(0, st)
                with act.Fori(0, TURNS) as n:
                    for st in streams:
                        act.wait_ge(bonus_done, at(n, st))
                        act.copy(st.kka[:, :], st.QB[:, 1, :]).then_inc(bonus_read, 1)
                        act.wait_ge(turnedA_done, at(n, st))
                        act.copy(two_sb(st.tok[:, 0:2, :, :]), two(st.QA)).then_inc(tokA_ready, 1)
                    for st in streams:
                        act.wait_ge(turnedB_done, at(n, st))
                        act.copy(two_sb(st.tok[:, 2:4, :, :]), two(st.QB)).then_inc(tokB_ready, 1)
                    act.wait_ge(gate_loaded, n * 16 + 16)
                    act.activation(gd[:, :], gd[:, :], ACT.Sigmoid).then_inc(gate_ready, 1)
                    bottleneck(n + 1)
                    for x in range(NL):
                        for st in streams:
                            act.wait_ge(T_done, at(n, st, NL, x))
                            act.copy(st.T1[:, :, :].rearrange("p (b h) c -> p b (h c)", b=2), st.QB[:, :, 0:256]).then_inc(T_ready, 1)
                        if 1 <= x <= PRE:
                            if x == 1:
                                act.wait_ge(weights, n * (16 * N_WEIGHTS) + 2 * 16 * N_WEIGHTS)
                            for st in streams:
                                prepare(n + 1, st, x - 1)
                        if x == PRE:
                            for st in streams:
                                exponentials(n + 1, st)
                    for st in streams:
                        act.wait_ge(GW_done, at(n, st))
                        act.copy(two_sb(st.GW[:, :, :, :]), two(st.QB)).then_inc(GW_ready, 1)
                    for c in range(NC):
                        for st in streams:
                            act.wait_ge(sa_done, at(n, st, NC, c))
                            act.copy(st.SA[0:C, :], st.QA[0:C, 0, 0:C]).then_inc(saA_ready, 1)
                    for st in streams:
                        act.wait_ge(y_done, at(n, st))
                        for h in range(2):
                            hs = slice(h * C, (h + 1) * C)
                            done = act.copy(st.y[hs, :], st.QB[hs, h, :])
                        done.then_inc(y_ready, 1)
                    for st in streams:
                        act.wait_ge(g_done, CREDIT + at(n, st))
                        act.copy(st.g[:, :], st.QB[:, 0, :]).then_inc(g_ready, 1)
                    for st in streams:
                        act.wait_ge(var_done, at(n, st))
                        act.activation(st.std[:, :], st.QA[:, 1, :], ACT.Sqrt, bias=zero_eps[:, 1:2], scale=1.0 / HD).then_inc(std_ready, 1)

            @block.vector
            def _(dve):
                def decay(m, st):
                    dve.wait_ge(pre_read, at(m, st, PRE, 0))
                    dve.tensor_scalar(st.logw[:, :], st.logw[:, :], -EXP_HALF, None, ALU.mult)
                    dve.drain()
                    dve.tensor_tensor_scan(st.Lsum[:, :], chunk_reset[:, :], st.logw[:, :], 0.0, ALU.mult, ALU.add)
                    dve.drain()
                    dve.tensor_tensor(st.logw[:, :], st.Lsum[:, :], st.logw[:, :], ALU.subtract).then_inc(L_ready, 1)

                def norm(m, st):
                    dve.wait_ge(pre_read, at(m, st, PRE, 2))
                    dve.tensor_scalar(st.root[:, :], st.root[:, :], 1e-12, -1.0, ALU.max, ALU.mult)
                    dve.drain()
                    dve.reciprocal(st.root[:, :], st.root[:, :]).then_inc(root_ready, 1)

                def group(i, g):
                    n = i * NG + g
                    low = below[:, :, :].rearrange("p a t -> p (a t)").unsqueeze(1).to_broadcast([P, NC, 2 * C])
                    for st in streams:
                        for done, ready, banks, to in ((scores1_done, scores1_ready, st.QA, st.SB1), (scores2_done, scores2_ready, st.QB, st.SB2)):
                            dve.wait_ge(done, at(n, st))
                            dve.tensor_tensor(to[:, :, :, :].rearrange("p c a t -> p c (a t)"),
                                              banks[:, :, :].rearrange("p b (h x) -> p (b h) x", x=2 * C), low, ALU.mult).then_inc(ready, 1)
                    dve.drain()
                    for st in streams:
                        dve.tensor_tensor(st.XX[:, 1, :, :], st.SB1[:, :, 0, :], lev1[:, :].unsqueeze(1).to_broadcast([P, NC, C]), ALU.mult)
                        dve.wait_ge(A_done, at(n, st))
                        dve.tensor_tensor(st.XX[:, 0, :, :].rearrange("p (b h) c -> p b h c", b=2),
                                          two(st.QA)[:, :, 0, :].rearrange("p b (h c) -> p b h c", c=C),
                                          lev1T[:, :].unsqueeze(1).unsqueeze(1).to_broadcast([P, 2, HC, C]), ALU.mult)
                        dve.drain()
                        both = st.XX[:, :, :, :].rearrange("p q n c -> p (q n) c")
                        dve.tensor_tensor(both, both, eye[:, :].unsqueeze(1).to_broadcast([P, 2 * NC, C]), ALU.add).then_inc(X_ready, 1)
                    for x in range(NL):
                        for st in streams:
                            dve.wait_ge(dX_done, at(n, st, NL, x))
                            if x < NL - 1:
                                dve.tensor_tensor(two_sb(st.XX[:, :, :, :]), two_sb(st.XX[:, :, :, :]), two(st.QA), ALU.add).then_inc(X_ready, 1)
                            else:
                                XT = st.XX[:, 1, :, :].rearrange("p (b h) c -> p b (h c)", b=2)
                                dve.tensor_tensor(XT, XT, two(st.QA)[:, :, 1, :], ALU.add).then_inc(X_ready, 1)
                        if x == 1:
                            for st in streams:
                                decay(n + 1, st)
                    for st in streams:
                        norm(n + 1, st)
                    for c in range(NC):
                        for st in streams:
                            dve.wait_ge(sa_done, at(n, st, NC, c))
                            dve.tensor_copy(st.SA[C:P, :], st.QA[C:P, 1, 0:C]).then_inc(saB_ready, 1)
                        for st in streams:
                            dve.wait_ge(dS_done, at(n, st, NC, c))
                            for h in range(2):
                                hs = slice(h * C, (h + 1) * C)
                                done = dve.scalar_tensor_tensor(st.S[hs, :], st.S[hs, :], st.ends[hs, c:c + 1],
                                                                st.QA[hs, h, C:2 * C], ALU.mult, ALU.add)
                            done.then_inc(S_ready, 1)
                    for st in streams:
                        dve.wait_ge(mean_done, at(n, st))
                        dve.scalar_tensor_tensor(st.y[:, :], st.QA[:, 0, :], -1.0 / HD, st.y[:, :], ALU.mult, ALU.add)
                        dve.drain()
                        dve.tensor_tensor(st.dev[:, :], st.y[:, :], st.y[:, :], ALU.mult).then_inc(centred_ready, 1)
                    for st in streams:
                        dve.wait_ge(std_ready, CREDIT + at(n, st))
                        dve.reciprocal(st.std[:, :], st.std[:, :])
                        dve.drain()
                        dve.tensor_tensor(st.y[:, :], st.y[:, :], st.std[:, :], ALU.mult)
                        dve.drain()
                        dve.wait_ge(lnw_loaded, n * (16 * N_LNW) + 16 * N_LNW)
                        dve.tensor_scalar(st.y[:, :], st.y[:, :], st.lnv[:, 0:1], st.lnv[:, 1:2], ALU.mult, ALU.add)
                        dve.drain()
                        dve.wait_ge(bonus_ready, at(n, st))
                        dve.tensor_tensor(st.y[:, :], st.y[:, :], st.bonus[:, :], ALU.add)
                        dve.drain()
                        dve.wait_ge(stored[st.p], CREDIT + n * 16)
                        dve.wait_ge(g_ready, CREDIT + at(n, st))
                        dve.tensor_tensor(st.outp[:, :], st.y[:, :], st.g[:, :], ALU.mult).then_inc(out_ready, 1)

                dve.wait_ge(consts, N_CONSTS)
                dve.wait_ge(kk2_ready, 1)
                prepare_first(dve, on_dve, 0, streams[1])
                for st in streams:
                    decay(0, st)
                prepare_k(dve, on_dve, 0, streams[1])
                for st in streams:
                    norm(0, st)
                dve.wait_ge(operands_ready, 1)
                prepare_operands(dve, on_dve, 0, streams[1])
                with dve.Fori(0, N2) as i:
                    for st in streams:
                        dve.memset(st.S[:, :], 0.0).then_inc(S_ready, 1)
                    with dve.Fori(0, NG) as g:
                        group(i, g)

            @block.tensor
            def _(pe):
                HS = [slice(0, C), slice(C, P)]

                def two_heads(one):
                    for c in range(HC):
                        one(0, c)
                        one(1, HC + c)
                    for c in range(HC):
                        one(1, c)
                        done = one(0, HC + c)
                    return done

                def place(bank_pair, q, h, c):
                    x = q * 256 + (c % HC) * C
                    return bank_pair[HS[h], c // HC, x:x + C]

                def part(tile, h, c):
                    return tile[HS[h], c * C:(c + 1) * C]

                def mm(out, lhsT, rhs, start=True, stop=True):
                    return pe.matmul(out, lhsT, rhs, start=start, stop=stop)

                def prepare(m, st, k):
                    if k == 0:
                        pe.wait_ge(lora_ready, m + 1)
                        pe.sem_inc(on_pe, 1)
                        pe.wait_ge(weights, m * (16 * N_WEIGHTS) + 16 * N_WEIGHTS)
                        pe.sem_inc(on_pe, 1)
                    if k == 2:
                        pe.wait_ge(kk2_ready, at(m, st))
                        pe.sem_inc(on_pe, 1)
                    left, right = ((st.w_up, wd), (st.a_up, ad), (head_ones, st.sq))[k]
                    for b in range(2):
                        done = mm(st.QB[:, b, 256:512], left[:, :], right[:, b * 256:(b + 1) * 256])
                    done.then_inc(pre_done, 1)

                def group(i, g):
                    n = i * NG + g
                    eyes = [ident[HS[h], HS[h]] for h in range(2)]
                    for st in streams:
                        pe.wait_ge(operands_ready, at(n, st))
                        pe.sem_inc(on_pe, 1)
                        pe.wait_ge(g_ready, CREDIT - 1 + 2 * n + st.p)
                        pe.sem_inc(on_pe, 1)
                        mm(st.QB[:, 1, :], head_ones[:, :], st.rk[:, :]).then_inc(bonus_done, 1)
                        pe.wait_ge(std_ready, CREDIT - 1 + 2 * n + st.p)
                        pe.sem_inc(on_pe, 1)
                        two_heads(lambda h, c: mm(place(st.QA, 0, h, c), st.AR[HS[h], c, 0, :], eyes[h]))
                        two_heads(lambda h, c: mm(place(st.QA, 1, h, c), part(st.b_h, h, c), eyes[h])).then_inc(turnedA_done, 1)
                    for st in streams:
                        pe.wait_ge(bonus_read, at(n, st))
                        pe.sem_inc(on_pe, 1)
                        two_heads(lambda h, c: mm(place(st.QB, 0, h, c), part(st.k_h, h, c), eyes[h]))
                        two_heads(lambda h, c: mm(place(st.QB, 1, h, c), st.rkv[HS[h], 2, c * C:(c + 1) * C], eyes[h])).then_inc(turnedB_done, 1)

                    def score(st, banks, left):
                        return two_heads(lambda h, c: mm(banks[HS[h], c // HC, (c % HC) * 2 * C:(c % HC + 1) * 2 * C],
                                                         part(left, h, c), st.AR[HS[h], c, :, :]))

                    for st in streams:
                        pe.wait_ge(tokA_ready, at(n, st))
                        pe.sem_inc(on_pe, 1)
                        score(st, st.QA, st.b_t).then_inc(scores1_done, 1)
                        pe.wait_ge(tokB_ready, at(n, st))
                        pe.sem_inc(on_pe, 1)
                        score(st, st.QB, st.k_t).then_inc(scores2_done, 1)
                    for st in streams:
                        pe.wait_ge(scores1_ready, at(n, st))
                        pe.sem_inc(on_pe, 1)
                        two_heads(lambda h, c: mm(place(st.QA, 0, h, c), st.AR[HS[h], c, 0, :], part(st.b_t, h, c))).then_inc(A_done, 1)
                    for x in range(NL):
                        for st in streams:
                            if x == 0:
                                pe.wait_ge(level0_ready, at(n, st))
                                pe.sem_inc(on_pe, 1)
                                pe.wait_ge(scores2_ready, at(n, st))
                                pe.sem_inc(on_pe, 1)
                            if x == 1:
                                pe.wait_ge(levels_ready, at(n, st))
                                pe.sem_inc(on_pe, 1)
                            pe.wait_ge(X_ready, at(n, st, NL + 1, x))
                            pe.sem_inc(on_pe, 1)
                            if 2 <= x <= PRE + 1:
                                pe.wait_ge(pre_read, at(n + 1, st, PRE, x - 2))
                                pe.sem_inc(on_pe, 1)
                            two_heads(lambda h, c: mm(place(st.QB, 0, h, c), st.ATl[HS[h], x, c, :], st.XX[HS[h], 0, c, :])).then_inc(T_done, 1)
                        for st in streams:
                            pe.wait_ge(T_ready, at(n, st, NL, x))
                            pe.sem_inc(on_pe, 1)
                            if 1 <= x <= PRE:
                                prepare(n + 1, st, x - 1)
                            if x < NL - 1:
                                two_heads(lambda h, c: mm(place(st.QA, 0, h, c), st.XX[HS[h], 1, c, :], st.T1[HS[h], c, :]))
                            two_heads(lambda h, c: mm(place(st.QA, 1, h, c), st.T1[HS[h], c, :], st.XX[HS[h], 1, c, :])).then_inc(dX_done, 1)
                    for st in streams:
                        pe.wait_ge(X_ready, at(n, st, NL + 1, NL))
                        pe.sem_inc(on_pe, 1)
                        two_heads(lambda h, c: mm(place(st.QB, 0, h, c), st.tok[HS[h], 0, c, :], st.XX[HS[h], 1, c, :]))
                        two_heads(lambda h, c: mm(place(st.QB, 1, h, c), st.SB2[HS[h], c, 0, :], st.tok[HS[h], 3, c, :])).then_inc(GW_done, 1)
                    for st in streams:
                        pe.wait_ge(GW_ready, at(n, st))
                        pe.sem_inc(on_pe, 1)
                    for c in range(NC):
                        cs = slice(c * C, (c + 1) * C)
                        for st in streams:
                            pe.wait_ge(S_ready, i * (2 + NG * NC * 2) + at(g, st, NC, c))
                            pe.sem_inc(on_pe, 1)
                            for h in range(2):
                                mm(st.QA[HS[h], h, 0:C], st.XX[HS[h], 1, c, :], st.GW[HS[h], 1, c, :], stop=False)
                                done = mm(st.QA[HS[h], h, 0:C], st.GW[HS[h], 0, c, :], st.S[HS[h], :], start=False)
                            done.then_inc(sa_done, 1)
                            for h in range(2):
                                mm(st.QB[HS[h], h, cs], st.tok[HS[h], 3, c, :], st.SB2[HS[h], c, 1, :], stop=False)
                                mm(st.QB[HS[h], h, cs], st.S[HS[h], :], st.r_t[HS[h], c, :], start=False, stop=False)
                        for st in streams:
                            pe.wait_ge(saA_ready, at(n, st, NC, c))
                            pe.sem_inc(on_pe, 1)
                            pe.wait_ge(saB_ready, at(n, st, NC, c))
                            pe.sem_inc(on_pe, 1)
                            for h in range(2):
                                mm(st.QA[HS[h], h, C:2 * C], st.tok[HS[h], 2, c, :], st.tok[HS[h], 3, c, :], stop=False)
                                done = mm(st.QA[HS[h], h, C:2 * C], st.tok[HS[h], 1, c, :], st.SA[HS[h], :], start=False)
                            done.then_inc(dS_done, 1)
                            for h in range(2):
                                done = mm(st.QB[HS[h], h, cs], st.SA[HS[h], :], st.SB1[HS[h], c, 1, :], start=False)
                            if c == NC - 1:
                                done.then_inc(y_done, 1)
                    for st in streams:
                        pe.wait_ge(S_ready, i * (2 + NG * NC * 2) + at(g, st, NC, NC))
                        pe.sem_inc(on_pe, 1)
                        pe.wait_ge(y_ready, at(n, st))
                        pe.sem_inc(on_pe, 1)
                        mm(st.QA[:, 0, :], head_ones[:, :], st.y[:, :]).then_inc(mean_done, 1)
                    for st in streams:
                        pe.wait_ge(gate_ready, n + 1)
                        pe.sem_inc(on_pe, 1)
                        pe.wait_ge(lnw_loaded, n * (16 * N_LNW) + 16 * N_LNW)
                        pe.sem_inc(on_pe, 1)
                        mm(st.QB[:, 0, :], st.g_up[:, :], gd[:, :]).then_inc(g_done, 1)
                    for st in streams:
                        pe.wait_ge(centred_ready, at(n, st))
                        pe.sem_inc(on_pe, 1)
                        mm(st.QA[:, 1, :], head_ones[:, :], st.dev[:, :]).then_inc(var_done, 1)

                pe.wait_ge(consts, N_CONSTS)
                for k in range(PRE):
                    for st in streams:
                        if k > 0:
                            pe.wait_ge(pre_read, at(0, st, PRE, k - 1))
                        prepare(0, st, k)
                for st in streams:
                    pe.wait_ge(pre_read, at(0, st, PRE, PRE - 1))
                with pe.Fori(0, N2) as i:
                    with pe.Fori(0, NG) as g:
                        group(i, g)


class ExpertWeights:

    def __init__(self, nc, ctx, program, w_g, w_u, w_d):
        sb, _, sem = makers(nc, ctx, program)
        self.dram = (w_g, w_u, w_d)
        self.wg = sb("wg", [P, 2, KT, FF])
        self.wu = sb("wu", [P, 2, KT, FF])
        self.wd = sb("wd7", [P, 2, FF // P, D])
        self.gu_loaded = [sem(f"gu_loaded{s}") for s in range(2)]
        self.d_loaded = [sem(f"d_loaded{s}") for s in range(2)]

    def load(self, sp, e, s, part=None):
        w_g, w_u, w_d = self.dram
        for x, (to, src) in enumerate(((self.wg, w_g), (self.wu, w_u))):
            if part in (None, x):
                sp.dma_start(to[:, s, :, :], src[0, bass.ds(e, 1), :, :].rearrange("o (p k) f -> p (o k) f", p=P)).then_inc(self.gu_loaded[s], 16)
        if part in (None, 2):
            sp.dma_start(self.wd[:, s, :, :], w_d[0, bass.ds(e, 1), :, :].rearrange("o (f p) d -> p (o f) d", p=P)).then_inc(self.d_loaded[s], 16)


def mix_out_and_route(nc, program, E_all, ranks, gates, totals, x, w_out, norm2_gain, w_rg, w_re, experts, mixT_dram, x1_dram, h2_dram):
    with ExitStack() as ctx:
        sb, pb, sem = makers(nc, ctx, program)
        NL = N_GROUPS + NE
        w_sb = sb("wo_sb", [P, KT, D])
        w_r = sb("w_r", [P, KT, NL])
        gain = sb("gain2", [P, D])
        mixT = sb("mixT_t", [P, 2, KT, P])
        x_t = sb("x_t5", [P, 2, D])
        h2 = sb("h2_t", [P, 2, D])
        h2T = sb("h2T", [P, KT, P])
        squares = sb("squares5", [P, D])
        ssum, root, rstd = [sb(n, [P, 1]) for n in ("ssum5", "root5", "rstd5")]
        eps = sb("eps5", [P, 1])
        ident = sb("ident5", [P, P])
        earlier = sb("earlier", [P, P])
        ones = sb("ones5", [P, P])
        iota_i = sb("iota_i", [P, NE], I32)
        iota = sb("iota_f", [P, NE])
        lg = sb("lg", [P, NL])
        gl8 = sb("gl8", [P, 8])
        gmax8, emax8 = sb("gmax8", [P, 8]), sb("emax8", [P, 8])
        gidx8, eidx8 = sb("gidx8", [P, 8], U32), sb("eidx8", [P, 8], U32)
        negmax, gidx, gidx_8, gsum, ggate = [sb(n, [P, 1]) for n in ("negmax", "gidx", "gidx_8", "gsum", "ggate")]
        gexp = sb("gexp", [P, N_GROUPS])
        onehot = sb("onehot", [P, N_GROUPS])
        sel = sb("sel", [P, N_GROUPS, PER_GROUP])
        in_group = sb("in_group", [P, PER_GROUP])
        lead, share, eidx, eid = [sb(n, [P, 2]) for n in ("lead", "share", "eidx", "eid")]
        E = sb("E", [P, 2, 2, NE])
        both = sb("both", [P, 2, NE])
        before = sb("before", [P, NE])
        picked = sb("picked", [P, 2, NE])
        o_ps = pb("o_ps5", [P, 2, 2, 512])
        hT_ps = pb("hT_ps5", [P, KT, P])
        lg_ps = pb("lg_ps", [P, 512])
        rank_ps = pb("rank_ps", [P, 512])

        names = """weights consts x1_ready rooted h2_ready turned hT_copied mixed logits_done routed_group
            gates_wanted exped shared picks_ready ranked ranks_ready counted""".split()
        (weights, consts, x1_ready, rooted, h2_ready, turned, hT_copied, mixed, logits_done, routed_group,
         gates_wanted, exped, shared, picks_ready, ranked, ranks_ready, counted) = [sem(f"p5_{n}") for n in names]
        w_out_loaded = [sem(f"p5_w_out_loaded{half}") for half in range(2)]
        loaded = [sem(f"p5_loaded{s}") for s in range(2)]
        stored = [sem(f"p5_stored{s}") for s in range(2)]
        on_sp, on_act, on_pe, on_dve, on_pool = program.gates_passed
        mixT_v = mixT_dram.rearrange("(k p) t -> p k t", p=P)
        give_credit(nc, hT_copied, routed_group, x1_ready, ranks_ready)
        with nc.Block() as block:
            @block.sync
            def _(sp):
                def load(t, s):
                    sp.dma_start(mixT[:, s, :, :], mixT_v[:, :, bass.ds(t * P, P)]).then_inc(loaded[s], 16)
                    sp.dma_start(x_t[:, s, :], x[0, bass.ds(t * P, P), :]).then_inc(loaded[s], 16)

                def store(t, s):
                    sp.wait_ge(h2_ready, t + 1)
                    sp.dma_start(x1_dram[bass.ds(t * P, P), :], x_t[:, s, :]).then_inc(stored[s], 16)
                    sp.dma_start(h2_dram[bass.ds(t * P, P), :], h2[:, s, :]).then_inc(stored[s], 16)

                w_out_v = w_out[0].rearrange("(k p) c -> p k c", p=P)
                load(0, 0)
                for half in range(2):
                    sp.dma_start(w_sb[:, :, half * 512:(half + 1) * 512], w_out_v[:, :, half * 512:(half + 1) * 512]).then_inc(w_out_loaded[half], 16)
                load(1, 1)
                sp.dma_start(w_r[:, :, 0:N_GROUPS], w_rg[0].rearrange("(k p) c -> p k c", p=P)).then_inc(weights, 16)
                sp.dma_start(w_r[:, :, N_GROUPS:NL], w_re[0].rearrange("(k p) c -> p k c", p=P)).then_inc(weights, 16)
                sp.dma_start(gain[:, :], norm2_gain[0, :].partition_broadcast(P)).then_inc(weights, 16)
                for i in range(NT // 2 - 1):
                    if i < 6:
                        experts.load(sp, i // 3, i // 3, part=i % 3)
                    for s in range(2):
                        t = i * 2 + s
                        store(t, s)
                        sp.wait_ge(stored[s], i * 32 + 32)
                        load(t + 2, s)
                for s in range(2):
                    store(NT - 2 + s, s)
                for s in range(2):
                    sp.wait_ge(stored[s], 16 * NT)

            @block.gpsimd
            def _(pool):
                identity(pool, ident[:, :])
                pool.memset(eps[:, :], NORM_EPS)
                pool.memset(ones[:, :], 1.0)
                pool.memset(earlier[:, :], 1.0)
                pool.memset(gl8[:, :], -3.4e38)
                pool.memset(before[:, :], 0.0)
                pool.iota(iota_i[:, :], pattern=[[1, NE]], base=0, channel_multiplier=0)
                pool.drain()
                pool.affine_select(out=earlier[:, :], in_=earlier[:, :], compare_op=ALU.is_gt, fill=0.0, base=0,
                                   pattern=[[1, P]], channel_multiplier=-1)
                pool.tensor_copy(iota[:, :], iota_i[:, :])
                pool.drain()
                pool.sem_inc(consts, 1)

            def tile_pairs(eng, one_tile):
                for s in range(2):
                    one_tile(s, s, 0, first=(s == 0), last=False)
                with eng.Fori(1, NT // 2 - 1) as i:
                    for s in range(2):
                        one_tile(i * 2 + s, s, i, first=False, last=False)
                for s in range(2):
                    one_tile(NT - 2 + s, s, NT // 2 - 1, first=False, last=(s == 1))

            @block.tensor
            def _(pe):
                def mix(t, s, n, half):
                    if half == 0:
                        pe.wait_ge(loaded[s], n * 32 + 32)
                        pe.wait_ge(x1_ready, CREDIT + t - 1)
                    for k in range(KT):
                        done = pe.matmul(o_ps[:, s, half, :], mixT[:, s, k, :], w_sb[:, k, half * 512:(half + 1) * 512],
                                         start=(k == 0), stop=(k == KT - 1))
                    if half == 1:
                        done.then_inc(mixed, 1)

                def rank(t, s):
                    pe.wait_ge(picks_ready, t + 1)
                    pe.wait_ge(ranks_ready, CREDIT + t)
                    pe.matmul(rank_ps[:, 0:NE], earlier[:, :], both[:, s, :], start=True, stop=False)
                    pe.matmul(rank_ps[:, 0:NE], ones[:, :], before[:, :], start=False, stop=True).then_inc(ranked, 1)

                def one_tile(t, s, n, first, last):
                    if not last:
                        mix(t + 1, 1 - s, n + s, 0)
                    pe.wait_ge(h2_ready, t + 1)
                    pe.wait_ge(hT_copied, CREDIT + t)
                    for k in range(KT):
                        done = pe.transpose(hT_ps[:, k, :], h2[:, s, k * P:(k + 1) * P], ident[:, :])
                    done.then_inc(turned, 1)
                    if not last:
                        mix(t + 1, 1 - s, n + s, 1)
                    if not first:
                        rank(t - 1, 1 - s)
                    pe.wait_ge(hT_copied, CREDIT + t + 1)
                    pe.wait_ge(routed_group, CREDIT + t)
                    for k in range(KT):
                        done = pe.matmul(lg_ps[:, 0:NL], h2T[:, k, :], w_r[:, k, :], start=(k == 0), stop=(k == KT - 1))
                    done.then_inc(logits_done, 1)

                pe.wait_ge(consts, 1)
                for half in range(2):
                    pe.wait_ge(w_out_loaded[half], 16)
                    mix(0, 0, 0, half)
                pe.wait_ge(weights, 48)
                tile_pairs(pe, one_tile)
                rank(NT - 1, 1)
                pe.wait_ge(ranks_ready, CREDIT + NT)
                pe.matmul(rank_ps[:, 0:NE], ones[:, :], before[:, :], start=True, stop=True).then_inc(counted, 1)

            @block.scalar
            def _(act):
                def norm(t, s):
                    act.wait_ge(x1_ready, CREDIT + t + 1)
                    act.activation(squares[:, :], x_t[:, s, :], ACT.Square, accum_out=ssum[:, :])
                    act.drain()
                    act.activation(root[:, :], ssum[:, :], ACT.Sqrt, bias=eps[:, :], scale=1.0 / D).then_inc(rooted, 1)

                def one_tile(t, s, n, first, last):
                    act.wait_ge(turned, t + 1)
                    act.copy(h2T[:, :, :], hT_ps[:, :, :]).then_inc(hT_copied, 1)
                    if not last:
                        norm(t + 1, 1 - s)
                    act.wait_ge(routed_group, CREDIT + t + 1)
                    act.activation(gexp[:, :], gl8[:, 0:N_GROUPS], ACT.Exp, bias=negmax[:, :], accum_out=gsum[:, :])
                    act.drain()
                    act.sem_inc(exped, 1)
                    act.wait_ge(gates_wanted, t + 1)
                    act.activation(share[:, :], lead[:, :], ACT.Sigmoid).then_inc(shared, 1)

                act.wait_ge(consts, 1)
                norm(0, 0)
                tile_pairs(act, one_tile)

            @block.vector
            def _(dve):
                def finish(t, s):
                    dve.wait_ge(ranked, t + 1)
                    dve.tensor_tensor(picked[:, :, :], E[:, s, :, :], rank_ps[:, 0:NE].unsqueeze(1).to_broadcast([P, 2, NE]), ALU.mult)
                    dve.drain()
                    dve.reduce_sum(ranks[:, bass.ds(t * 2, 2)], picked[:, :, :], axis=AX_X)
                    dve.tensor_tensor(before[:, :], before[:, :], both[:, s, :], ALU.add).then_inc(ranks_ready, 1)
                    dve.drain()

                def norm(t, s):
                    dve.wait_ge(mixed, t + 1)
                    dve.tensor_tensor(x_t[:, s, :], x_t[:, s, :], o_ps[:, s, :, :].rearrange("p a b -> p (a b)"), ALU.add).then_inc(x1_ready, 1)
                    dve.wait_ge(rooted, t + 1)
                    dve.reciprocal(rstd[:, :], root[:, :])
                    dve.drain()
                    dve.scalar_tensor_tensor(h2[:, s, :], x_t[:, s, :], rstd[:, :], gain[:, :], ALU.mult, ALU.mult).then_inc(h2_ready, 1)

                def one_tile(t, s, n, first, last):
                    if not last:
                        norm(t + 1, 1 - s)
                    if not first:
                        finish(t - 1, 1 - s)
                    dve.wait_ge(logits_done, t + 1)
                    dve.tensor_copy(lg[:, :], lg_ps[:, 0:NL])
                    dve.tensor_copy(gl8[:, 0:N_GROUPS], lg_ps[:, 0:N_GROUPS])
                    dve.drain()
                    dve.max(gmax8[:, :], gl8[:, :])
                    dve.drain()
                    dve.max_index(gidx8[:, :], gmax8[:, :], gl8[:, :])
                    dve.tensor_scalar(negmax[:, :], gmax8[:, 0:1], -1.0, None, ALU.mult).then_inc(routed_group, 1)
                    dve.drain()
                    dve.tensor_copy(gidx[:, :], gidx8[:, 0:1])
                    dve.drain()
                    dve.tensor_scalar(onehot[:, :], iota[:, 0:N_GROUPS], gidx[:, :], None, ALU.is_equal)
                    dve.tensor_scalar(gidx_8[:, :], gidx[:, :], float(PER_GROUP), None, ALU.mult)
                    dve.drain()
                    dve.tensor_tensor(sel[:, :, :], lg[:, N_GROUPS:NL].rearrange("p (g e) -> p g e", g=N_GROUPS),
                                      onehot[:, :].unsqueeze(2).to_broadcast([P, N_GROUPS, PER_GROUP]), ALU.mult)
                    dve.drain()
                    dve.reduce_sum(in_group[:, :], sel[:, :, :].rearrange("p g e -> p e g"), axis=AX_X)
                    dve.drain()
                    dve.max(emax8[:, :], in_group[:, :])
                    dve.drain()
                    dve.max_index(eidx8[:, :], emax8[:, :], in_group[:, :])
                    dve.tensor_tensor(lead[:, 0:1], emax8[:, 0:1], emax8[:, 1:2], ALU.subtract)
                    dve.tensor_tensor(lead[:, 1:2], emax8[:, 1:2], emax8[:, 0:1], ALU.subtract).then_inc(gates_wanted, 1)
                    dve.drain()
                    dve.tensor_copy(eidx[:, :], eidx8[:, 0:2])
                    dve.drain()
                    dve.tensor_scalar(eid[:, :], eidx[:, :], gidx_8[:, :], None, ALU.add)
                    dve.drain()
                    dve.tensor_tensor(E[:, s, :, :], iota[:, :].unsqueeze(1).to_broadcast([P, 2, NE]),
                                      eid[:, :].unsqueeze(2).to_broadcast([P, 2, NE]), ALU.is_equal)
                    dve.drain()
                    dve.tensor_tensor(both[:, s, :], E[:, s, 0, :], E[:, s, 1, :], ALU.add).then_inc(picks_ready, 1)
                    dve.tensor_copy(E_all[:, bass.ds(t * 2, 2), :], E[:, s, :, :])
                    dve.wait_ge(exped, t + 1)
                    dve.reciprocal(ggate[:, :], gsum[:, :])
                    dve.drain()
                    dve.wait_ge(shared, t + 1)
                    dve.tensor_scalar(gates[:, bass.ds(t * 2, 2)], share[:, :], ggate[:, :], None, ALU.mult)

                dve.wait_ge(consts, 1)
                dve.wait_ge(weights, 48)
                norm(0, 0)
                tile_pairs(dve, one_tile)
                finish(NT - 1, 1)
                dve.wait_ge(counted, 1)
                dve.tensor_copy(totals[:, :], rank_ps[:, 0:NE])
                dve.drain()


def place_slots(nc, program, E_all, ranks, totals, n_blocks, first_block, row_slot):
    with ExitStack() as ctx:
        sb, pb, sem = makers(nc, ctx, program)
        up = sb("up", [P, NE])
        blocks_i = sb("blocks_i", [P, NE], I32)
        blocks, ends, starts = [sb(n, [P, NE]) for n in ("blocks", "ends", "starts")]
        rows_of = sb("rows_of", [P, 2 * NT, NE])
        row = sb("row", [P, 2 * NT])
        row_i, block_i, part_i = [sb(n, [P, 2 * NT], I32) for n in ("row_i", "block_i", "part_i")]
        block_f, part_f = [sb(n, [P, 2 * NT]) for n in ("block_f", "part_f")]
        cell = sb("cell", [P, 2 * NT], U32)
        ones = sb("ones6", [P, NE])
        slot = sb("slot", [P, NT, 2], I32)
        spare = sb("spare", [P, TABLE], I32)
        consts, placed, cleared, scattered = [sem(f"p6_{n}") for n in ("consts", "placed", "cleared", "scattered")]
        with nc.Block() as block:
            @block.gpsimd
            def _(pool):
                pool.memset(ones[:, :], 1.0)
                pool.iota(spare[:, :], pattern=[[1, TABLE]], base=2 * SEQ, channel_multiplier=TABLE)
                pool.iota(slot[:, :, :], pattern=[[2 * P, NT], [1, 2]], base=0, channel_multiplier=2)
                pool.drain()
                pool.sem_inc(consts, 1)
                pool.wait_ge(cleared, 16)
                pool.wait_ge(placed, 1)
                for t in range(NT):
                    for k in range(2):
                        col = 2 * t + k
                        pool.indirect_dma_start(out=row_slot[:, :], out_offset=bass.IndirectOffsetOnAxis(ap=cell[:, col:col + 1], axis=0),
                                                in_=slot[:, t, k:k + 1], in_offset=None).then_inc(scattered, 16)
                pool.wait_ge(scattered, 16 * 2 * NT)

            @block.sync
            def _(sp):
                sp.wait_ge(consts, 1)
                sp.dma_start(row_slot.rearrange("(p c) o -> p (c o)", p=P), spare[:, :]).then_inc(cleared, 16)

            @block.vector
            def _(dve):
                dve.wait_ge(consts, 1)
                dve.tensor_scalar(up[:, :], totals[:, :], float(P - 1), None, ALU.add)
                dve.drain()
                dve.tensor_copy(blocks_i[:, :], up[:, :])
                dve.drain()
                dve.tensor_scalar(blocks_i[:, :], blocks_i[:, :], P.bit_length() - 1, None, ALU.arith_shift_right)
                dve.drain()
                dve.tensor_copy(blocks[:, :], blocks_i[:, :])
                dve.drain()
                dve.tensor_scalar(blocks[:, :], blocks[:, :], 1.0, None, ALU.max)
                dve.drain()
                dve.tensor_tensor_scan(ends[:, :], ones[:, :], blocks[:, :], 0.0, ALU.mult, ALU.add)
                dve.drain()
                dve.tensor_tensor(starts[:, :], ends[:, :], blocks[:, :], ALU.subtract)
                dve.tensor_copy(n_blocks[:, :], blocks[:, :])
                dve.drain()
                dve.tensor_copy(first_block[:, :], starts[:, :])
                dve.tensor_scalar(starts[:, :], starts[:, :], float(P), None, ALU.mult)
                dve.drain()
                dve.tensor_tensor(rows_of[:, :, :], E_all[:, :, :], starts[:, :].unsqueeze(1).to_broadcast([P, 2 * NT, NE]), ALU.mult)
                dve.drain()
                dve.reduce_sum(row[:, :], rows_of[:, :, :], axis=AX_X)
                dve.drain()
                dve.tensor_tensor(row[:, :], row[:, :], ranks[:, :], ALU.add)
                dve.drain()
                dve.tensor_copy(row_i[:, :], row[:, :])
                dve.drain()
                dve.tensor_scalar(block_i[:, :], row_i[:, :], P.bit_length() - 1, None, ALU.arith_shift_right)
                dve.tensor_scalar(part_i[:, :], row_i[:, :], P - 1, None, ALU.bitwise_and)
                dve.drain()
                dve.tensor_copy(block_f[:, :], block_i[:, :])
                dve.tensor_copy(part_f[:, :], part_i[:, :])
                dve.drain()
                dve.scalar_tensor_tensor(row[:, :], part_f[:, :], float(TABLE), block_f[:, :], ALU.mult, ALU.add)
                dve.drain()
                dve.tensor_copy(cell[:, :], row[:, :])
                dve.drain()
                dve.sem_inc(placed, 1)


def run_experts(nc, program, n_blocks, first_block, row_slot, experts, h2_dram, y_dram, x1_all, x1_loaded, x1_dram):
    with ExitStack() as ctx:
        sb, pb, sem = makers(nc, ctx, program)
        FT = FF // P
        FH = FF // 2
        wg, wu, wd = experts.wg, experts.wu, experts.wd
        gu_loaded, d_loaded = experts.gu_loaded, experts.d_loaded
        slot_all = sb("slot_all", [P, TABLE], I32)
        tok_all = sb("tok_all", [P, TABLE], I32)
        tok = sb("tok7", [P, 1], I32)
        slot = sb("slot7", [P, 1], I32)
        xg = sb("xg", [P, D])
        xT = sb("xT", [P, KT, P])
        sil = sb("sil", [P, FF])
        h = sb("h7", [P, FF])
        hT = sb("hT7", [P, FT, P])
        y = sb("y7", [P, D])
        ident = sb("ident7", [P, P])
        xT_ps = pb("xT_ps7", [P, KT, P])
        g_ps = pb("g_ps7", [P, FF])
        u_ps = pb("u_ps7", [P, 2, 512])
        hT_ps = pb("hT_ps7", [P, FT, P])
        y_ps = pb("y_ps7", [P, D])
        names = """consts slots_loaded tok_ready gathered turned xT_ready g_done u_done silu_ready h_ready h_turned hT_ready
            y_done y_copied expert_done stored y_free""".split()
        (consts, slots_loaded, tok_ready, gathered, turned, xT_ready, g_done, u_done, silu_ready, h_ready, h_turned, hT_ready,
         y_done, y_copied, expert_done, stored, y_free) = [sem(f"p7_{n}") for n in names]
        on_sp, on_act, on_pe, on_dve, on_pool = program.gates_passed

        def blocks_of(eng, e):
            count = eng.value_load(n_blocks[0:1, bass.ds(e, 1)], min_val=1, max_val=SEQ // P)
            start = eng.value_load(first_block[0:1, bass.ds(e, 1)], min_val=0, max_val=MAX_BLOCKS - 1)
            return count, start

        give_credit(nc, h_ready, h_turned, silu_ready, y_free, y_copied)
        with nc.Block() as block:
            @block.sync
            def _(sp):
                sp.dma_start(slot_all[:, :], row_slot.rearrange("(p b) o -> p (b o)", p=P)).then_inc(slots_loaded, 16)

                def load_x1(t):
                    sp.dma_start(x1_all[:, bass.ds(t, 1), :], x1_dram[bass.ds(t * P, P), :].unsqueeze(1)).then_inc(x1_loaded, 16)

                def pass_stores(e):
                    count, start = blocks_of(sp, e)
                    with sp.Fori(0, count) as i:
                        sp.wait_ge(stored, (start + i) * 16 + 16)
                        sp.sem_inc(y_free, 1)

                load_x1(0)
                with sp.Fori(0, NE // 2 - 1) as i2:
                    load_x1(i2 + 1)
                    for s in range(2):
                        e = i2 * 2 + s
                        pass_stores(e)
                        sp.wait_ge(expert_done, e + 1)
                        experts.load(sp, e + 2, s)
                for e in (NE - 2, NE - 1):
                    pass_stores(e)

            @block.gpsimd
            def _(pool):
                identity(pool, ident[:, :])
                pool.drain()
                pool.sem_inc(consts, 1)
                pool.wait_ge(tok_ready, 1)

                def gather(b):
                    pool.tensor_copy(tok[:, :], tok_all[:, bass.ds(b, 1)])
                    pool.drain()
                    pool.indirect_dma_start(out=xg[:, :], out_offset=None, in_=h2_dram[:, :],
                                            in_offset=bass.IndirectOffsetOnAxis(ap=tok[:, 0:1], axis=0)).then_inc(gathered, 16)

                gather(0)
                pool.wait_ge(turned, 1)
                gather(1)
                with pool.Fori(0, NE) as e:
                    count, start = blocks_of(pool, e)
                    with pool.Fori(0, count) as i:
                        b = start + i
                        pool.wait_ge(turned, b + 2)
                        pool.sem_inc(on_pool, 1)
                        gather(b + 2)
                        pool.wait_ge(y_free, CREDIT + b)
                        pool.sem_inc(on_pool, 1)
                        pool.tensor_copy(slot[:, :], slot_all[:, bass.ds(b, 1)])
                        pool.drain()
                        pool.wait_ge(y_copied, CREDIT + b * 2 + 2)
                        pool.sem_inc(on_pool, 1)
                        pool.indirect_dma_start(out=y_dram[:, :], out_offset=bass.IndirectOffsetOnAxis(ap=slot[:, 0:1], axis=0),
                                                in_=y[:, :], in_offset=None).then_inc(stored, 16)
                pool.drain()

            @block.tensor
            def _(pe):
                def turn(b):
                    pe.wait_ge(gathered, b * 16 + 16)
                    for k in range(KT):
                        last = pe.transpose(xT_ps[:, k, :], xg[:, :].rearrange("t (p k) -> t k p", k=KT)[:, k, :], ident[:, :])
                    last.then_inc(turned, 1)

                def one_block(b, s):
                    pe.wait_ge(xT_ready, b * 2 + 2)
                    pe.wait_ge(silu_ready, CREDIT + b)
                    for k in range(KT):
                        last = pe.matmul(g_ps[:, :], xT[:, k, :], wg[:, s, k, :], start=(k == 0), stop=(k == KT - 1))
                    last.then_inc(g_done, 1)
                    pe.wait_ge(h_ready, CREDIT + b * 2)
                    for half in range(2):
                        for k in range(KT):
                            last = pe.matmul(u_ps[:, half, 0:FH], xT[:, k, :], wu[:, s, k, half * FH:(half + 1) * FH],
                                             start=(k == 0), stop=(k == KT - 1))
                        last.then_inc(u_done, 1)

                    def turn_h(half):
                        pe.wait_ge(h_ready, CREDIT + b * 2 + half + 1)
                        for f in range(2 * half, 2 * half + 2):
                            done = pe.transpose(hT_ps[:, f, :], h[:, f * P:(f + 1) * P], ident[:, :])
                        done.then_inc(h_turned, 1)

                    turn_h(0)
                    turn(b + 1)
                    pe.wait_ge(hT_ready, b * 2 + 1)
                    turn_h(1)
                    pe.wait_ge(y_copied, CREDIT + b * 2)
                    for fh in range(2):
                        if fh == 1:
                            pe.wait_ge(hT_ready, b * 2 + 2)
                        for half in range(2):
                            for f in range(2 * fh, 2 * fh + 2):
                                last = pe.matmul(y_ps[:, half * 512:(half + 1) * 512], hT[:, f, :], wd[:, s, f, half * 512:(half + 1) * 512],
                                                 start=(f == 0), stop=(f == FT - 1))
                            if fh == 1:
                                last.then_inc(y_done, 1)

                pe.wait_ge(consts, 1)
                turn(0)
                with pe.Fori(0, NE // 2) as i2:
                    for s in range(2):
                        e = i2 * 2 + s
                        count, start = blocks_of(pe, e)
                        pe.wait_ge(gu_loaded[s], i2 * 32 + 32)
                        pe.wait_ge(d_loaded[s], i2 * 16 + 16)
                        pe.sem_inc(on_pe, 1)
                        with pe.Fori(0, count) as i:
                            one_block(start + i, s)
                        pe.drain()
                        pe.sem_inc(expert_done, 1)

            @block.scalar
            def _(act):
                def copy_xT(b):
                    act.wait_ge(turned, b + 1)
                    act.copy(xT[:, 0:KT // 2, :], xT_ps[:, 0:KT // 2, :]).then_inc(xT_ready, 1)

                copy_xT(0)
                with act.Fori(0, NE) as e:
                    count, start = blocks_of(act, e)
                    with act.Fori(0, count) as i:
                        b = start + i
                        act.wait_ge(g_done, b + 1)
                        act.wait_ge(h_ready, CREDIT + b * 2)
                        act.activation(sil[:, :], g_ps[:, :], ACT.Silu).then_inc(silu_ready, 1)
                        act.wait_ge(h_turned, CREDIT + b * 2 + 1)
                        act.copy(hT[:, 0:2, :], hT_ps[:, 0:2, :]).then_inc(hT_ready, 1)
                        copy_xT(b + 1)
                        act.wait_ge(h_turned, CREDIT + b * 2 + 2)
                        act.copy(hT[:, 2:4, :], hT_ps[:, 2:4, :]).then_inc(hT_ready, 1)
                        act.wait_ge(y_done, b * 2 + 1)
                        act.wait_ge(y_free, CREDIT + b)
                        act.copy(y[:, 0:512], y_ps[:, 0:512]).then_inc(y_copied, 1)

            @block.vector
            def _(dve):
                def copy_xT(b):
                    dve.wait_ge(turned, b + 1)
                    dve.tensor_copy(xT[:, KT // 2:KT, :], xT_ps[:, KT // 2:KT, :]).then_inc(xT_ready, 1)

                dve.wait_ge(slots_loaded, 16)
                dve.tensor_scalar(tok_all[:, :], slot_all[:, :], 2 * SEQ - 1, None, ALU.min)
                dve.drain()
                dve.tensor_scalar(tok_all[:, :], tok_all[:, :], 1, None, ALU.arith_shift_right).then_inc(tok_ready, 1)
                copy_xT(0)
                with dve.Fori(0, NE) as e:
                    count, start = blocks_of(dve, e)
                    with dve.Fori(0, count) as i:
                        b = start + i
                        dve.wait_ge(silu_ready, CREDIT + b + 1)
                        dve.wait_ge(h_turned, CREDIT + b * 2)
                        for half in range(2):
                            cols = slice(half * FH, (half + 1) * FH)
                            dve.wait_ge(u_done, b * 2 + half + 1)
                            dve.tensor_tensor(h[:, cols], sil[:, cols], u_ps[:, half, 0:FH], ALU.mult).then_inc(h_ready, 1)
                        copy_xT(b + 1)
                        dve.wait_ge(y_done, b * 2 + 2)
                        dve.wait_ge(y_free, CREDIT + b)
                        dve.tensor_copy(y[:, 512:1024], y_ps[:, 512:1024]).then_inc(y_copied, 1)


def combine(nc, program, gates, x1_all, x1_loaded, y_dram, out):
    with ExitStack() as ctx:
        sb, pb, sem = makers(nc, ctx, program)
        rows = sb("rows8", [P, 2, 2, D])
        total = sb("total8", [P, 2, D])
        gate_t = sb("gate_t", [P, 2, 2])
        loaded = [sem(f"p8_loaded{s}") for s in range(2)]
        stored = [sem(f"p8_stored{s}") for s in range(2)]
        summed = sem("p8_summed")
        y_tiles = y_dram[0:2 * SEQ, :].rearrange("(t k) d -> t (k d)", k=2)
        give_credit(nc, *stored)
        with nc.Block() as block:
            @block.sync
            def _(sp):
                def load(t, s):
                    sp.dma_start(rows[:, s, :, :].rearrange("p k d -> p (k d)"), y_tiles[bass.ds(t * P, P), :]).then_inc(loaded[s], 16)

                def store(t, s):
                    sp.dma_start(out[0, bass.ds(t * P, P), :], total[:, s, :]).then_inc(stored[s], 16)

                load(0, 0)
                load(1, 1)
                with sp.Fori(0, NT // 2 - 1) as i:
                    for s in range(2):
                        t = i * 2 + s
                        sp.wait_ge(summed, t + 1)
                        load(t + 2, s)
                        store(t, s)
                for s in range(2):
                    sp.wait_ge(summed, NT - 1 + s)
                    store(NT - 2 + s, s)
                for s in range(2):
                    sp.wait_ge(stored[s], CREDIT + 8 * NT)

            @block.vector
            def _(dve):
                dve.wait_ge(x1_loaded, 16 * NT)
                with dve.Fori(0, NT // 2) as i:
                    for s in range(2):
                        t = i * 2 + s
                        dve.tensor_copy(gate_t[:, s, :], gates[:, bass.ds(t * 2, 2)])
                        dve.drain()
                        dve.wait_ge(loaded[s], i * 16 + 16)
                        x1 = x1_all[:, bass.ds(t, 1), :].rearrange("p o d -> p (o d)")
                        dve.scalar_tensor_tensor(rows[:, s, 0, :], rows[:, s, 0, :], gate_t[:, s, 0:1], x1, ALU.mult, ALU.add)
                        dve.drain()
                        dve.wait_ge(stored[s], CREDIT + i * 16)
                        dve.scalar_tensor_tensor(total[:, s, :], rows[:, s, 1, :], gate_t[:, s, 1:2], rows[:, s, 0, :], ALU.mult, ALU.add).then_inc(summed, 1)


def hybrid_block(nc, x, norm1_gain, w_in, sb_q_gain, sb_k_gain, rw_shift_mu, rw_w0, rw_w_up, rw_a0, rw_a_up, rw_g_up,
                 rw_k_k, rw_k_a, rw_r_k, rw_ln_w, rw_ln_b, w_out, norm2_gain, w_router_group, w_router_expert,
                 w_exp_gate, w_exp_up, w_exp_down, out):
    def dram(name, shape, dt=F32):
        return nc.dram_tensor(name, shape, dt, kind="Internal").ap()

    qT, kT, v = dram("qT", (SBW, SEQ)), dram("kT", (SBW, SEQ)), dram("v", (SEQ, SBW))
    pT = dram("pT", (RW_COLS, SEQ))
    mixT = dram("mixT", (D, SEQ))
    x1, h2 = dram("x1", (SEQ, D)), dram("h2", (SEQ, D))
    row_slot = dram("row_slot", (TABLE * P, 1), I32)
    y = dram("y", (2 * SEQ + TABLE * P, D))
    with ExitStack() as stack:
        program = Program(nc, stack)
        with nc.sbuf_tensor("h_all", [P, KT, SEQ], F32) as h_all:
            project_tokens(nc, program, h_all, x, norm1_gain, w_in, sb_q_gain, sb_k_gain, qT, kT, v)
            project_channels(nc, program, h_all, w_in, rw_shift_mu, pT)
        stick_breaking(nc, program, qT, kT, v, mixT)
        time_mixing(nc, program, rw_w0, rw_w_up, rw_a0, rw_a_up, rw_g_up, rw_k_k, rw_k_a, rw_r_k, rw_ln_w, rw_ln_b, pT, mixT)
        with ExitStack() as ctx:
            sb, _, _ = makers(nc, ctx, program)
            gates = sb("gates", [P, 2 * NT])
            n_blocks, first_block = sb("n_blocks", [P, NE], I32), sb("first_block", [P, NE], I32)
            experts = ExpertWeights(nc, ctx, program, w_exp_gate, w_exp_up, w_exp_down)
            with ExitStack() as routing:
                sb, _, _ = makers(nc, routing, program)
                E_all, ranks, totals = sb("E_all", [P, 2 * NT, NE]), sb("ranks", [P, 2 * NT]), sb("totals", [P, NE])
                mix_out_and_route(nc, program, E_all, ranks, gates, totals, x, w_out, norm2_gain, w_router_group, w_router_expert, experts, mixT, x1, h2)
                place_slots(nc, program, E_all, ranks, totals, n_blocks, first_block, row_slot)
            sb, _, sem = makers(nc, ctx, program)
            x1_all, x1_loaded = sb("x1_all", [P, NT, D]), sem("x1_loaded")
            run_experts(nc, program, n_blocks, first_block, row_slot, experts, h2, y, x1_all, x1_loaded, x1)
            combine(nc, program, gates, x1_all, x1_loaded, y, out)


_INPUTS = ("x norm1_gain w_in sb_q_gain sb_k_gain rw_shift_mu rw_w0 rw_w_up rw_a0 rw_a_up rw_g_up rw_k_k rw_k_a rw_r_k "
           "rw_ln_w rw_ln_b w_out norm2_gain w_router_group w_router_expert w_exp_gate w_exp_up w_exp_down").split()


def kernel(**inputs):
    import concourse.bacc as bacc
    import numpy as np
    from concourse.bass_utils import run_bass_kernel_spmd

    nc = bacc.Bacc("TRN2", target_bir_lowering=False, num_devices=1)
    arrays, aps = {}, []
    for name in _INPUTS:
        a = np.ascontiguousarray(inputs[name])
        arrays[f"in_{name}"] = a
        aps.append(nc.dram_tensor(f"in_{name}", a.shape, mybir.dt.from_np(a.dtype), kind="ExternalInput").ap())
    out = nc.dram_tensor("out", (1, SEQ, D), F32, kind="ExternalOutput").ap()
    hybrid_block(nc, *aps, out)
    r = run_bass_kernel_spmd(nc, [arrays], core_ids=[0])
    return r.results[0]["out"]
```
